# Optimizing a Trainium2 kernel written in Bass

```python
import math
import jax
import jax.numpy as jnp
from jax import lax
import numpy as np

D_MODEL = 1024
BATCH = 1
SEQ = 256
DEPTH = 2

CTX_LEN = 256
GRID_W = 64
D_FF = 2816
CHUNK = 128
LN_EPS = 1e-5
N_MOD = 9

NA_HEADS = 8
NA_HEAD_DIM = 64
NA_WIN_H = 8
NA_WIN_W = 16
NA_WIDTH = NA_HEADS * NA_HEAD_DIM
ML_HEADS = 4
ML_HEAD_DIM = 128
ML_WIDTH = ML_HEADS * ML_HEAD_DIM
ML_CONV = 5
S5_GROUP = 16
S5_GROUPS = 32
S5_WIDTH = S5_GROUP * S5_GROUPS
S5_STATE = 64
RET_HEADS = 4
RET_HEAD_DIM = 128
RET_WIDTH = RET_HEADS * RET_HEAD_DIM
ROPE_BASE = 10000.0

EV_SIZES = (NA_WIDTH, NA_WIDTH, NA_WIDTH, ML_WIDTH, ML_WIDTH, ML_WIDTH, 2 * ML_HEADS, 2 * ML_HEADS)
OD_SIZES = (S5_WIDTH, RET_WIDTH, RET_WIDTH, RET_WIDTH, RET_WIDTH)
EV_IN = sum(EV_SIZES)
OD_IN = sum(OD_SIZES)
MIX_WIDTH = NA_WIDTH + ML_WIDTH

F32 = jnp.float32

kernel_name = 'hybrid_dit_natten_mlstm_s5_retention'

def layer_norm(h, g, b):
    hf = h.astype(F32)
    mu = jnp.mean(hf, -1, keepdims=True)
    var = jnp.mean(jnp.square(hf - mu), -1, keepdims=True)
    return ((hf - mu) * lax.rsqrt(var + LN_EPS) * g.astype(F32) + b.astype(F32)).astype(h.dtype)

def modulate(h, mod, j):
    return h * (1.0 + mod[..., 3 * j + 1, :, :]) + mod[..., 3 * j, :, :]

def gate(mod, j):
    return mod[..., 3 * j + 2, :, :]

def swiglu(h, w_gate, w_up, w_down):
    return (jax.nn.silu(h @ w_gate) * (h @ w_up)) @ w_down

def half_ffn(h, mod, j, w, g, b, alpha):
    y = swiglu(modulate(h, mod, j), *w)
    return layer_norm(alpha * h + 0.5 * gate(mod, j) * y, g, b)

def split_cols(z, sizes):
    parts, off = [], 0
    for s in sizes:
        parts.append(z[..., off:off + s])
        off += s
    return parts

def head_norm(h, w):
    bsz, nh, t, d = h.shape
    mu = jnp.mean(h, -1, keepdims=True)
    var = jnp.mean(jnp.square(h - mu), -1, keepdims=True)
    hn = (h - mu) * lax.rsqrt(var + LN_EPS)
    return hn.transpose(0, 2, 1, 3).reshape(bsz, t, nh * d) * w.astype(F32)

def to_chunks(a, axis):
    t = a.shape[axis]
    a = a.reshape(a.shape[:axis] + (t // CHUNK, CHUNK) + a.shape[axis + 1:])
    return jnp.moveaxis(a, axis, 0)

def from_chunks(a, axis):
    a = jnp.moveaxis(a, 0, axis)
    return a.reshape(a.shape[:axis] + (a.shape[axis] * a.shape[axis + 1],) + a.shape[axis + 2:])

def bidir_scan(scan_fn, ctx_xs, lat_xs, dir_params, init_state, axis):
    ys_c, ys_l = [], []
    for d in range(2):
        flip = (lambda a: jnp.flip(a, axis)) if d == 1 else (lambda a: a)
        y_c, state = scan_fn(*[flip(a) for a in ctx_xs[d]], *dir_params[d], init_state)
        y_l, _ = scan_fn(*[flip(a) for a in lat_xs[d]], *dir_params[d], state)
        ys_c.append(flip(y_c))
        ys_l.append(flip(y_l))
    return ys_c[0] + ys_c[1], ys_l[0] + ys_l[1]

def context_attention(q, k, v):
    s = jnp.einsum('bqhd,bkhd->bhqk', q, k) * (q.shape[-1] ** -0.5)
    p = jax.nn.softmax(s.astype(F32), axis=-1).astype(v.dtype)
    o = jnp.einsum('bhqk,bkhd->bqhd', p, v)
    return o.reshape(o.shape[0], o.shape[1], -1)

def neighbourhood_attention(q, k, v, k_ctx, v_ctx, rpb):
    bsz, seq, nh, dh = q.shape
    rows = seq // GRID_W
    kh, kw = min(NA_WIN_H, rows), NA_WIN_W
    n_loc = kh * kw
    grid = lambda a: a.reshape(bsz, rows, GRID_W, nh, dh).transpose(0, 3, 1, 2, 4)
    kg, vg = grid(k), grid(v)
    q_rows = q.reshape(bsz, rows, GRID_W, nh, dh).transpose(1, 0, 3, 2, 4) * (dh ** -0.5)
    kc, vc = k_ctx.transpose(0, 2, 1, 3), v_ctx.transpose(0, 2, 1, 3)
    cols = jnp.arange(GRID_W)
    col_idx = jnp.clip(cols - kw // 2, 0, GRID_W - kw)[:, None] + jnp.arange(kw)[None, :]
    col_off = col_idx - cols[:, None] + (NA_WIN_W - 1)

    def one_row(args):
        qr, r = args
        rs = jnp.clip(r - kh // 2, 0, rows - kh)
        kwin = jnp.take(lax.dynamic_slice_in_dim(kg, rs, kh, axis=2), col_idx, axis=3)
        vwin = jnp.take(lax.dynamic_slice_in_dim(vg, rs, kh, axis=2), col_idx, axis=3)
        row_off = rs + jnp.arange(kh) - r + (NA_WIN_H - 1)
        bias = rpb[:, row_off[:, None, None], col_off[None, :, :]].transpose(0, 2, 1, 3)
        s_loc = jnp.einsum('bhqd,bhrqwd->bhqrw', qr, kwin) + bias
        s_ctx = jnp.einsum('bhqd,bhcd->bhqc', qr, kc)
        logits = jnp.concatenate([s_loc.reshape(bsz, nh, GRID_W, n_loc), s_ctx], -1).astype(F32)
        p = jax.nn.softmax(logits, axis=-1).astype(v.dtype)
        p_loc = p[..., :n_loc].reshape(bsz, nh, GRID_W, kh, kw)
        return (jnp.einsum('bhqrw,bhrqwd->bhqd', p_loc, vwin)
                + jnp.einsum('bhqc,bhcd->bhqd', p[..., n_loc:], vc))

    out = lax.map(one_row, (q_rows, jnp.arange(rows)))
    return out.transpose(1, 0, 3, 2, 4).reshape(bsz, seq, nh * dh)

def mlstm_scan(q, k, v, i_pre, log_f, state):
    tri = jnp.tril(jnp.ones((CHUNK, CHUNK), dtype=bool))

    def step(carry, xs):
        c_mat, n_vec, m = carry
        qc, kc, vc, ic, fc = xs
        b = jnp.cumsum(fc, axis=-1)
        dlog = jnp.where(tri, b[..., :, None] - b[..., None, :] + ic[..., None, :], -jnp.inf)
        inter = b + m[..., None]
        m_t = jnp.maximum(inter, jnp.max(dlog, axis=-1))
        s = jnp.einsum('bhtd,bhsd->bhts', qc, kc) * jnp.exp(dlog - m_t[..., None])
        w_inter = jnp.exp(inter - m_t)
        num = (jnp.einsum('bhts,bhsd->bhtd', s, vc)
               + w_inter[..., None] * jnp.einsum('bhvk,bhtk->bhtv', c_mat, qc))
        den = jnp.sum(s, -1) + w_inter * jnp.einsum('bhk,bhtk->bht', n_vec, qc)
        h = num / jnp.maximum(jnp.abs(den), jnp.exp(-m_t))[..., None]
        b_last = b[..., -1]
        w_log = b_last[..., None] - b + ic
        m_new = jnp.maximum(b_last + m, jnp.max(w_log, -1))
        carry_decay = jnp.exp(b_last + m - m_new)
        w_in = jnp.exp(w_log - m_new[..., None])
        c_new = carry_decay[..., None, None] * c_mat + jnp.einsum('bhsv,bhsk->bhvk', vc * w_in[..., None], kc)
        n_new = carry_decay[..., None] * n_vec + jnp.einsum('bhs,bhsk->bhk', w_in, kc)
        return (c_new, n_new, m_new), h

    xs = tuple(to_chunks(a, 2) for a in (q, k, v, i_pre, log_f))
    state, hs = lax.scan(step, state, xs)
    return from_chunks(hs, 2), state

def centred_depthwise_conv(x, w, b):
    y = lax.conv_general_dilated(x, w[:, None, :], window_strides=(1,), padding='SAME',
                                 dimension_numbers=('NWC', 'WIO', 'NWC'), feature_group_count=x.shape[-1])
    return y + b

def mlstm_prepare(parts, conv_w, conv_b, wq, wk, i_bias, f_bias):
    xm, zv, zo, zi, zf = parts
    bsz, t, _ = xm.shape
    xc = jax.nn.silu(centred_depthwise_conv(xm, conv_w, conv_b)).astype(F32)
    xc = xc.reshape(bsz, t, ML_HEADS, ML_HEAD_DIM)
    q = jnp.einsum('bthd,hde->bhte', xc, wq.astype(F32))
    k = jnp.einsum('bthd,hde->bhte', xc, wk.astype(F32)) * (ML_HEAD_DIM ** -0.5)
    v = zv.astype(F32).reshape(bsz, t, ML_HEADS, ML_HEAD_DIM).transpose(0, 2, 1, 3)
    i_pre = (zi.astype(F32).reshape(bsz, t, 2, ML_HEADS) + i_bias.astype(F32)).transpose(2, 0, 3, 1)
    log_f = jax.nn.log_sigmoid(zf.astype(F32).reshape(bsz, t, 2, ML_HEADS)
                               + f_bias.astype(F32)).transpose(2, 0, 3, 1)
    xs = [(q, k, v, i_pre[d], log_f[d]) for d in range(2)]
    return xs, jax.nn.sigmoid(zo.astype(F32))

def even_mixer(zc, zl, rpb, conv_w, conv_b, wq, wk, i_bias, f_bias, gn_w):
    pc, pl = split_cols(zc, EV_SIZES), split_cols(zl, EV_SIZES)
    heads = lambda a: a.reshape(a.shape[0], a.shape[1], NA_HEADS, NA_HEAD_DIM)
    na_c = context_attention(heads(pc[0]), heads(pc[1]), heads(pc[2]))
    na_l = neighbourhood_attention(heads(pl[0]), heads(pl[1]), heads(pl[2]),
                                   heads(pc[1]), heads(pc[2]), rpb)
    xs_c, o_c = mlstm_prepare(pc[3:], conv_w, conv_b, wq, wk, i_bias, f_bias)
    xs_l, o_l = mlstm_prepare(pl[3:], conv_w, conv_b, wq, wk, i_bias, f_bias)
    bsz = zl.shape[0]
    init = (jnp.zeros((bsz, ML_HEADS, ML_HEAD_DIM, ML_HEAD_DIM), F32),
            jnp.zeros((bsz, ML_HEADS, ML_HEAD_DIM), F32),
            jnp.zeros((bsz, ML_HEADS), F32))
    h_c, h_l = bidir_scan(mlstm_scan, xs_c, xs_l, ((), ()), init, 2)
    ml_c = (o_c * head_norm(h_c, gn_w)).astype(zc.dtype)
    ml_l = (o_l * head_norm(h_l, gn_w)).astype(zl.dtype)
    return jnp.concatenate([na_c, ml_c], -1), jnp.concatenate([na_l, ml_l], -1)

def s5_scan(u, lam_re, lam_im, log_dt, b_re, b_im, c_re, c_im, state):
    dt = jnp.exp(log_dt)[:, None]
    zr, zi = lam_re * dt, lam_im * dt
    mag = jnp.exp(zr)
    a_re, a_im = mag * jnp.cos(zi), mag * jnp.sin(zi)
    lam_sq = jnp.square(lam_re) + jnp.square(lam_im)
    e_re = ((a_re - 1.0) * lam_re + a_im * lam_im) / lam_sq
    e_im = (a_im * lam_re - (a_re - 1.0) * lam_im) / lam_sq
    bb_re = e_re[..., None] * b_re - e_im[..., None] * b_im
    bb_im = e_re[..., None] * b_im + e_im[..., None] * b_re
    steps = jnp.arange(1, CHUNK + 1, dtype=F32)[:, None, None]
    pmag = jnp.exp(steps * zr)
    p_re, p_im = pmag * jnp.cos(steps * zi), pmag * jnp.sin(steps * zi)

    def combine(e1, e2):
        a1r, a1i, b1r, b1i = e1
        a2r, a2i, b2r, b2i = e2
        return (a2r * a1r - a2i * a1i, a2r * a1i + a2i * a1r,
                a2r * b1r - a2i * b1i + b2r, a2r * b1i + a2i * b1r + b2i)

    def step(carry, uc):
        x0r, x0i = carry
        bu_re = jnp.einsum('blgq,gpq->blgp', uc, bb_re)
        bu_im = jnp.einsum('blgq,gpq->blgp', uc, bb_im)
        _, _, xr, xi = lax.associative_scan(
            combine, (jnp.broadcast_to(a_re, bu_re.shape), jnp.broadcast_to(a_im, bu_im.shape), bu_re, bu_im),
            axis=1)
        xr, xi = (xr + p_re * x0r[:, None] - p_im * x0i[:, None],
                  xi + p_re * x0i[:, None] + p_im * x0r[:, None])
        y = jnp.einsum('blgp,gqp->blgq', xr, c_re) - jnp.einsum('blgp,gqp->blgq', xi, c_im)
        return (xr[:, -1], xi[:, -1]), y

    state, ys = lax.scan(step, state, to_chunks(u, 1))
    return from_chunks(ys, 1), state

def retention_scan(q, k, v, log_g, state):
    j = jnp.arange(CHUNK, dtype=F32)
    rel = j[:, None] - j[None, :]
    dmat = jnp.where(rel >= 0, jnp.exp(jnp.maximum(rel, 0.0) * log_g[:, None, None]), 0.0)
    q_dec = jnp.exp((j + 1.0) * log_g[:, None])[..., None]
    k_dec = jnp.exp((CHUNK - 1.0 - j) * log_g[:, None])[..., None]
    c_dec = jnp.exp(CHUNK * log_g)[:, None, None]

    def step(r, xs):
        qc, kc, vc = xs
        inner = jnp.einsum('bhts,bhsv->bhtv', jnp.einsum('bhtd,bhsd->bhts', qc, kc) * dmat, vc)
        cross = jnp.einsum('bhtd,bhdv->bhtv', qc * q_dec, r)
        r_new = c_dec * r + jnp.einsum('bhsd,bhsv->bhdv', kc * k_dec, vc)
        return r_new, inner + cross

    xs = tuple(to_chunks(a, 2) for a in (q, k, v))
    state, ys = lax.scan(step, state, xs)
    return from_chunks(ys, 2), state

def axial_rope(x, pos_row, pos_col):
    d = x.shape[-1]
    half, nf = d // 2, d // 4
    freqs = ROPE_BASE ** (-jnp.arange(nf, dtype=F32) / nf)

    def rotate(xp, pos):
        ang = pos.astype(F32)[:, None] * freqs
        cos, sin = jnp.cos(ang)[None, :, None, :], jnp.sin(ang)[None, :, None, :]
        x1, x2 = xp[..., :nf], xp[..., nf:]
        return jnp.concatenate([x1 * cos - x2 * sin, x2 * cos + x1 * sin], -1)

    return jnp.concatenate([rotate(x[..., :half], pos_row), rotate(x[..., half:], pos_col)], -1)

def odd_mixer(zc, zl, pos_row, pos_col, lam_re, lam_im, log_dt, b_re, b_im, c_re, c_im,
              d_skip, glu_w, glu_b, decay_logit, gn_w):
    pc, pl = split_cols(zc, OD_SIZES), split_cols(zl, OD_SIZES)
    bsz = zl.shape[0]
    groups = lambda a: a.astype(F32).reshape(a.shape[0], a.shape[1], S5_GROUPS, S5_GROUP)
    uc, ul = groups(pc[0]), groups(pl[0])
    s5_p = [tuple(p[d].astype(F32) for p in (lam_re, lam_im, log_dt, b_re, b_im, c_re, c_im)) for d in range(2)]
    s5_init = (jnp.zeros((bsz, S5_GROUPS, S5_STATE), F32), jnp.zeros((bsz, S5_GROUPS, S5_STATE), F32))
    yc, yl = bidir_scan(s5_scan, [(uc,), (uc,)], [(ul,), (ul,)], s5_p, s5_init, 1)

    def s5_out(y, u):
        y = jax.nn.gelu(y + d_skip.astype(F32) * u)
        y = y.reshape(y.shape[0], y.shape[1], S5_WIDTH)
        return y * jax.nn.sigmoid(y @ glu_w.astype(F32) + glu_b.astype(F32))

    heads = lambda a: a.astype(F32).reshape(a.shape[0], a.shape[1], RET_HEADS, RET_HEAD_DIM)
    bhtd = lambda a: a.transpose(0, 2, 1, 3)
    k_scale = RET_HEAD_DIM ** -0.5
    rc_xs = (bhtd(heads(pc[1])), bhtd(heads(pc[2])) * k_scale, bhtd(heads(pc[3])))
    rl_xs = (bhtd(axial_rope(heads(pl[1]), pos_row, pos_col)),
             bhtd(axial_rope(heads(pl[2]), pos_row, pos_col)) * k_scale,
             bhtd(heads(pl[3])))
    log_g = jax.nn.log_sigmoid(decay_logit.astype(F32))
    ret_init = jnp.zeros((bsz, RET_HEADS, RET_HEAD_DIM, RET_HEAD_DIM), F32)
    rc, rl = bidir_scan(retention_scan, [rc_xs, rc_xs], [rl_xs, rl_xs], [(log_g[0],), (log_g[1],)], ret_init, 2)
    ret_c = jax.nn.silu(pc[4].astype(F32)) * head_norm(rc, gn_w)
    ret_l = jax.nn.silu(pl[4].astype(F32)) * head_norm(rl, gn_w)
    out_c = jnp.concatenate([s5_out(yc, uc), ret_c], -1).astype(zc.dtype)
    out_l = jnp.concatenate([s5_out(yl, ul), ret_l], -1).astype(zl.dtype)
    return out_c, out_l

def setup_inputs(seed: int = 0) -> dict:
    key = jax.random.key(seed)
    ks = jax.random.split(key, 40)
    n_ev, n_od = (DEPTH + 1) // 2, DEPTH // 2
    beta = (8.0 * DEPTH) ** -0.25
    D = D_MODEL
    nrm = lambda i, shape, s: jax.random.normal(ks[i], shape, F32) * s
    ones_n = lambda i, shape: 1.0 + nrm(i, shape, 0.02)
    return {
        'x': nrm(0, (BATCH, SEQ, D), 1.0),
        'c': nrm(1, (BATCH, D), 1.0),
        'ctx': nrm(2, (BATCH, CTX_LEN, D), 1.0),
        'c_ctx': nrm(3, (D,), 1.0),
        'ada_w': nrm(4, (DEPTH, D, N_MOD * D), 0.5 * D ** -0.5),
        'ada_b': nrm(5, (DEPTH, N_MOD * D), 0.02),
        'ffn_w_gate': nrm(6, (DEPTH, 2, D, D_FF), D ** -0.5),
        'ffn_w_up': nrm(7, (DEPTH, 2, D, D_FF), D ** -0.5),
        'ffn_w_down': nrm(8, (DEPTH, 2, D_FF, D), beta * D_FF ** -0.5),
        'ln_g': ones_n(9, (DEPTH, 3, D)),
        'ln_b': nrm(10, (DEPTH, 3, D), 0.02),
        'ev_w_in': nrm(11, (n_ev, D, EV_IN), D ** -0.5),
        'ev_w_out': nrm(12, (n_ev, MIX_WIDTH, D), beta * MIX_WIDTH ** -0.5),
        'na_rpb': nrm(13, (n_ev, NA_HEADS, 2 * NA_WIN_H - 1, 2 * NA_WIN_W - 1), 0.1),
        'ml_conv_w': nrm(14, (n_ev, ML_CONV, ML_WIDTH), ML_CONV ** -0.5),
        'ml_conv_b': nrm(15, (n_ev, ML_WIDTH), 0.02),
        'ml_wq': nrm(16, (n_ev, ML_HEADS, ML_HEAD_DIM, ML_HEAD_DIM), ML_HEAD_DIM ** -0.5),
        'ml_wk': nrm(17, (n_ev, ML_HEADS, ML_HEAD_DIM, ML_HEAD_DIM), ML_HEAD_DIM ** -0.5),
        'ml_i_bias': nrm(18, (n_ev, 2, ML_HEADS), 0.1),
        'ml_f_bias': jnp.linspace(3.0, 6.0, ML_HEADS, dtype=F32) + nrm(19, (n_ev, 2, ML_HEADS), 0.1),
        'ml_gn_w': ones_n(20, (n_ev, ML_WIDTH)),
        'od_w_in': nrm(21, (n_od, D, OD_IN), D ** -0.5),
        'od_w_out': nrm(22, (n_od, MIX_WIDTH, D), beta * MIX_WIDTH ** -0.5),
        's5_lam_re': -0.5 + nrm(23, (n_od, 2, S5_GROUPS, S5_STATE), 0.01),
        's5_lam_im': math.pi * jnp.arange(S5_STATE, dtype=F32) + nrm(24, (n_od, 2, S5_GROUPS, S5_STATE), 0.01),
        's5_log_dt': jax.random.uniform(ks[25], (n_od, 2, S5_GROUPS), F32, math.log(1e-3), math.log(1e-1)),
        's5_b_re': nrm(26, (n_od, 2, S5_GROUPS, S5_STATE, S5_GROUP), (2.0 * S5_GROUP) ** -0.5),
        's5_b_im': nrm(27, (n_od, 2, S5_GROUPS, S5_STATE, S5_GROUP), (2.0 * S5_GROUP) ** -0.5),
        's5_c_re': nrm(28, (n_od, 2, S5_GROUPS, S5_GROUP, S5_STATE), 0.5),
        's5_c_im': nrm(29, (n_od, 2, S5_GROUPS, S5_GROUP, S5_STATE), 0.5),
        's5_d': nrm(30, (n_od, S5_GROUPS, S5_GROUP), 0.5),
        's5_glu_w': nrm(31, (n_od, S5_WIDTH, S5_WIDTH), S5_WIDTH ** -0.5),
        's5_glu_b': nrm(32, (n_od, S5_WIDTH), 0.02),
        'ret_decay_logit': (jnp.log(2.0 ** (5.0 + jnp.arange(RET_HEADS, dtype=F32)) - 1.0)
                            + nrm(33, (n_od, 2, RET_HEADS), 0.01)),
        'ret_gn_w': ones_n(34, (n_od, RET_WIDTH)),
    }

def reference(x, c, ctx, c_ctx, ada_w, ada_b, ffn_w_gate, ffn_w_up, ffn_w_down, ln_g, ln_b,
              ev_w_in, ev_w_out, na_rpb, ml_conv_w, ml_conv_b, ml_wq, ml_wk, ml_i_bias, ml_f_bias, ml_gn_w,
              od_w_in, od_w_out, s5_lam_re, s5_lam_im, s5_log_dt, s5_b_re, s5_b_im, s5_c_re, s5_c_im,
              s5_d, s5_glu_w, s5_glu_b, ret_decay_logit, ret_gn_w):
    bsz, seq, dm = x.shape
    t = jnp.arange(seq)
    pos_row, pos_col = t // GRID_W, t % GRID_W
    alpha = (2.0 * DEPTH) ** 0.25
    silu_c, silu_cc = jax.nn.silu(c), jax.nn.silu(c_ctx)
    cx = ctx
    for l in range(DEPTH):
        e = l // 2
        last = l == DEPTH - 1
        mod_l = (silu_c @ ada_w[l] + ada_b[l]).reshape(bsz, N_MOD, 1, dm)
        mod_c = (silu_cc @ ada_w[l] + ada_b[l]).reshape(N_MOD, 1, dm)
        ffn_a = (ffn_w_gate[l, 0], ffn_w_up[l, 0], ffn_w_down[l, 0])
        ffn_b = (ffn_w_gate[l, 1], ffn_w_up[l, 1], ffn_w_down[l, 1])
        x = half_ffn(x, mod_l, 0, ffn_a, ln_g[l, 0], ln_b[l, 0], alpha)
        cx = half_ffn(cx, mod_c, 0, ffn_a, ln_g[l, 0], ln_b[l, 0], alpha)
        hl, hc = modulate(x, mod_l, 1), modulate(cx, mod_c, 1)
        if l % 2 == 0:
            yc, yl = even_mixer(hc @ ev_w_in[e], hl @ ev_w_in[e], na_rpb[e], ml_conv_w[e], ml_conv_b[e],
                                ml_wq[e], ml_wk[e], ml_i_bias[e], ml_f_bias[e], ml_gn_w[e])
            w_out = ev_w_out[e]
        else:
            yc, yl = odd_mixer(hc @ od_w_in[e], hl @ od_w_in[e], pos_row, pos_col,
                               s5_lam_re[e], s5_lam_im[e], s5_log_dt[e], s5_b_re[e], s5_b_im[e],
                               s5_c_re[e], s5_c_im[e], s5_d[e], s5_glu_w[e], s5_glu_b[e],
                               ret_decay_logit[e], ret_gn_w[e])
            w_out = od_w_out[e]
        x = layer_norm(alpha * x + gate(mod_l, 1) * (yl.astype(x.dtype) @ w_out), ln_g[l, 1], ln_b[l, 1])
        x = half_ffn(x, mod_l, 2, ffn_b, ln_g[l, 2], ln_b[l, 2], alpha)
        if not last:
            cx = layer_norm(alpha * cx + gate(mod_c, 1) * (yc.astype(cx.dtype) @ w_out), ln_g[l, 1], ln_b[l, 1])
            cx = half_ffn(cx, mod_c, 2, ffn_b, ln_g[l, 2], ln_b[l, 2], alpha)
    return x


_drawn_inputs = setup_inputs


def setup_inputs(seed=0):
    import zlib

    import numpy as np

    out = dict(_drawn_inputs(seed))
    spreads = {}
    factors = {'ada_b': 6.015,
     'na_rpb': 64.0,
     'ml_conv_b': 8.0,
     'ml_i_bias': 8.0,
     'ml_gn_w': 58.15,
     's5_lam_re': 64.0,
     's5_lam_im': 20.788,
     's5_log_dt': 22.423,
     's5_b_re': 35.637,
     's5_b_im': 33.875,
     's5_c_re': 37.624,
     's5_c_im': 34.466,
     's5_d': 3.96,
     's5_glu_w': 8.0,
     's5_glu_b': 64.0,
     'ret_decay_logit': 25.728,
     'ret_gn_w': 57.235}
    for name, (base, spread) in spreads.items():
        noise = np.random.default_rng([zlib.crc32(name.encode()), seed]).standard_normal(out[name].shape)
        drawn = base * np.exp(spread * noise) if base else spread * noise
        out[name] = jnp.asarray(drawn.astype(out[name].dtype))
    for name, factor in factors.items():
        out[name] = (out[name] * factor).astype(out[name].dtype)
    return out
```

```python
import contextlib
import math

import numpy as np

import concourse.bass as bass
from concourse import mybir

F32 = mybir.dt.float32
ALU = mybir.AluOpType
ACT = mybir.ActivationFunctionType
AX = mybir.AxisListType

P = 128
D = 1024
KT = D // P
CTX, LAT = 256, 256
T = CTX + LAT
TT = T // P
FF = 2816
FT = FF // P
PAIRS = FT // 2
LAYERS = 2
MODT = 9 * KT
MODG = MODT // 4
ALPHA = (2.0 * LAYERS) ** 0.25
EPS = 1e-5
SLOT = 4 * KT * P
STREAMS = ((0, CTX), (CTX, T))


GRID_W = 64
NA_HEADS, NA_DIM = 8, 64
WIN_W = 16
RPB_H, RPB_W = 15, 31
ROWS = LAT // GRID_W
HEADS, HDIM = 4, P
WIDTH = HEADS * HDIM
CONV = 5
EXP_MAX = 85.0

EVEN_LOADS = [(0, "ev_in", 0, SLOT), (1, "ev_gates", None, KT * 4 * HEADS), (2, "ev_in", 1, SLOT), (3, "ev_in", 2, SLOT),
              (0, "ev_in", 3, SLOT), (1, "ev_v", 0, SLOT), (2, "ev_v", 1, SLOT), (3, "ml_qk", None, 2 * WIDTH),
              (0, "ev_out", 0, SLOT), (1, "ev_out", 1, SLOT)]

S5_STATE, S5_GROUP, S5_GROUPS = 64, 16, 32
S5_TILES = S5_GROUPS * S5_STATE // P
UNITS5 = [(st, way) for st in range(S5_TILES) for way in range(2)]
PAIR = 2 * S5_GROUP
TWO_PI = 2 * math.pi
ROUND = 1.5 * 2.0 ** 23
PI_A = 6.28125
PI_B = float(np.float32(math.floor((TWO_PI - PI_A) * 2 ** 20) / 2 ** 20))
PI_C = float(np.float32(TWO_PI - PI_A - PI_B))
LN2_A = 0.693359375
LN2_B = float(np.float32(math.log(2.0) - LN2_A))
TABLE_RING = 4

ODD_LOADS = [(0, "od_in", 0, SLOT), (1, "od_in", 1, SLOT), (2, "od_v", None, SLOT), (3, "od_in", 2, SLOT),
             (0, "od_in", 3, SLOT), (1, "glu", None, HEADS * WIDTH), (2, "od_out", 0, SLOT), (3, "od_out", 1, SLOT)]


def uses_before(stage):
    n = [2, 2, 2, 0, 0]
    if stage == "start":
        return n
    ffn = lambda ada: [PAIRS - PAIRS // 2, PAIRS // 2, ada, KT // 2, KT // 2]
    n = [a + b for a, b in zip(n, ffn(12))]
    if stage == "odd":
        for load in EVEN_LOADS:
            n[load[0]] += 1
        for ada in (12, 6):
            n = [a + b for a, b in zip(n, ffn(ada))]
    return n


def build(nc, i, out, stop=None):
    stack = contextlib.ExitStack()
    with stack:
        def sb(name, shape):
            return stack.enter_context(nc.sbuf_tensor(name, shape, F32))

        sems = {}

        def sem(name):
            if name not in sems:
                sems[name] = stack.enter_context(nc.semaphore(name))
            return sems[name]

        stages = ["ffn0", "even", "ffn1", "ffn2", "odd", "ffn3"]
        PER_STAGE = {"m_ready": KT, "r_ready": KT, "sq": KT, "sums": 2 * KT, "stat": 2, "stat_read": 2, "var": 1, "std": 1,
                     "c": KT, "z": KT, "h_ready": KT}

        def before(name, stage):
            return PER_STAGE[name] * stages.index(stage)

        h = sb("h", [P, KT, T])
        m = sb("m", [P, KT, T])
        slots = [sb(f"slot{k}", [P, SLOT]) for k in range(5)]
        R = sb("R", [P, 17408])
        L = sb("L", [P, 8 * T])
        mods = sb("mods", [P, LAYERS, MODT, 2])
        modb = sb("modb", [P, LAYERS, MODT, 2])
        ada_sum = sb("ada_sum", [P, 4, 2])
        lng = sb("lng", [P, 2 * 3, KT])
        lnb = sb("lnb", [P, 2 * 3, KT])
        mscale = sb("mscale", [P, 6, KT, 2])
        mshift = sb("mshift", [P, 6, KT, 2])
        mgate = sb("mgate", [P, 6, KT, 2])
        mean_w = sb("mean_w", [P, P])
        banks = [stack.enter_context(nc.psum_tensor(f"bank{k}", [P, T], F32)) for k in range(8)]

        ident = sb("ident", [P, P])
        ones_w = sb("ones_w", [P, P])
        hmean_w = sb("hmean_w", [P, P])
        flip = L[:, 0:P]
        head_sel = sb("head_sel", [HEADS, HEADS, P])
        na_mask = sb("na_mask", [P, GRID_W])
        conv_w = sb("conv_w", [P, HEADS, CONV])
        conv_b = sb("conv_b", [P, HEADS])
        gate_b = sb("gate_b", [HEADS, 4])
        ml_gn = sb("ml_gn", [P, HEADS])
        acol = sb("acol", [P, 2, TT, HEADS])
        col = sb("col", [P, 8])

        s5_par = sb("s5_par", [P, 3, 2 * S5_TILES])
        s5_mag = sb("s5_mag", [P, 2 * S5_TILES])
        s5_e = sb("s5_e", [P, 2, 2 * S5_TILES])
        log_g = sb("log_g", [P, 2, HEADS])
        s5_d, glu_b, ret_gn = sb("s5_d", [P, 4]), sb("glu_b", [P, 4]), sb("ret_gn", [P, 4])

        def view(buf, off, *shape):
            n = 1
            for s in shape:
                n *= s
            v = buf[:, off:off + n]
            if len(shape) == 2:
                return v.rearrange("p (a b) -> p a b", b=shape[1])
            if len(shape) == 3:
                return v.rearrange("p (a b c) -> p a b c", b=shape[1], c=shape[2])
            return v

        g = view(R, 0, FT, T)
        silu_g = view(L, 0, 2, T)
        sq = view(L, 2 * T, 2, T)
        rsum = view(L, 4 * T, T)
        rsq = view(L, 5 * T, T)
        mean = view(L, 6 * T, T)
        rstd = view(L, 7 * T, T)
        csilu = [slots[3 + s_][:, FT * P:FT * P + D] for s_ in range(2)]
        gate_bank, up_bank, out_bank, stat_bank = banks[0:2], banks[2:4], banks[5:7], banks[7]
        stat2_bank = banks[4]

        full = [sem(f"slot{k}_full") for k in range(5)]
        used = [sem(f"slot{k}_used") for k in range(5)]

        def wslot(k):
            return slots[k][:, :].rearrange("p (t k n) -> p t k n", k=KT, n=P)

        NORMS = [(l, n) for l in range(LAYERS) for n in range(3)]
        ADA_IN = {"ffn0": (6, 12), "ffn1": (18, 12), "ffn2": (30, 6), "ffn3": (36, 0)}
        mod_groups = [6 * (n + 1) for n in range(6)]

        xc, sig_o = view(R, 0, HEADS, T), view(R, 2048, HEADS, T)
        ml_v = view(R, 4096, TT, WIDTH)
        na_q, na_k, na_v = view(R, 6144, 4, T), view(R, 8192, 4, T), view(R, 10240, TT, WIDTH)
        xm = view(R, 12288, 2, T)
        na_bias = view(R, 13312, 2, NA_HEADS, LAT)
        bias_flipped = view(R, 0, 2, NA_HEADS, LAT)
        probs = view(L, 0, 2, T)
        probsT = view(L, 2 * T, 2, 4, 2 * P)
        gates_tok = view(L, 6 * T, TT, 16)
        rows = slots[4][0:HEADS, :].rearrange("p (a n) -> p a n", n=T)
        ml_qh, ml_kh = view(R, 6144, 2, T), view(R, 7168, 2, T)
        decay = [view(R, 8192, TT, T), view(R, 10240, TT, T)]
        em_b, quot = view(R, 12288, 2, T), view(R, 13312, 2, T)
        hs = view(R, 14336, HEADS, T)
        hsq, hvar = view(R, 8192, HEADS, T), view(R, 10240, HEADS, T)
        y = m

        TARGETS = [[[(P * n, T)] for n in range(TT)],
                   [[(0, P), (CTX, T)], [(0, T)], [(CTX, CTX + P)], [(CTX, T)]]]
        ORDER = [[0, 1, 2, 3], [1, 0, 3, 2]]
        QK_AT = [(0, 0), (1, 0), (2, 0), (2, 256)]

        def qk_cols(n, a, b):
            bank, off = QK_AT[n]
            lo = 0 if n < 2 else CTX
            return banks[bank][:, off + a - lo:off + b - lo]

        tables_dram = nc.dram_tensor("s5_tables", (len(UNITS5), P, 2 * CTX), F32, kind="Internal").ap()
        small = view(L, 128, 8, 2 * S5_TILES)
        tables_out = view(slots[2], 0, 4, 2, CTX)
        phase = view(slots[2], 2048, 2, 3, CTX)
        steps = view(slots[2], 3584, 2, CTX)
        s5_u = view(R, 0, 4, T)
        ret_k, ret_v = view(R, 2048, HEADS, T), view(R, 4096, TT, WIDTH)
        ret_q, ret_gate = view(R, 6144, HEADS, LAT), view(R, 7168, HEADS, LAT)
        tables = view(R, 8192, TABLE_RING, 2, CTX)
        c_fold = view(R, 10240, 2, 2 * S5_TILES, PAIR)
        c_raw = view(R, 12288, 2, 2 * S5_TILES, PAIR)
        b_raw = R[:, 14336:16384].rearrange("p (r u n) -> p r u n", r=2, n=P)
        rope = view(R, 16384, 2, LAT)
        rope_swap = R[:, 16896:16896 + P]
        prods = view(L, 0, 2, 4, T)
        s5_z = view(slots[4], 0, 2, 2, T)
        s5_x = view(slots[4], 2048, 2, 2, LAT)
        s5_q = view(slots[4], 3072, 4, LAT)
        glu_sig = view(slots[4], 0, 4, LAT)
        rope_tmp = view(slots[4], 1024, 2, LAT)
        s5_init = s5_par[:, 0, 0:4]
        rel = view(R, 8192, 2, T)
        ret_decay = view(L, 0, 8, T)
        ret_s = view(R, 9216, 4, TT, LAT)

        UNITS = [(hp, st, hh, qt) for hp in range(4) for st in range(2) for hh in range(2) for qt in range(2)]

        RET_PARTS = [(0, 0, 0, LAT), (0, 1, 0, LAT), (0, 2, 0, LAT), (0, 3, P, LAT),
                     (1, 0, 0, LAT), (1, 1, 0, LAT), (1, 3, 0, LAT), (1, 2, 0, P)]

        def decay_at(way, n):
            return (LAT - P * n) if way == 0 else (P - P * n if n < 2 else 3 * P - P * (n - 2))

        block = stack.enter_context(nc.Block())

        @block.sync
        def _(sp):
            def load_cvec():
                for s_ in range(2):
                    sp.dma_start(csilu[s_], i["cvec"][:, s_, :]).then_inc(sem("cvec_in"), 16)

            load_cvec()
            loads = [0] * 5

            def load(k, src, width=SLOT, step=None, it=None, per=0):
                n = loads[k]
                if it is None:
                    if n:
                        sp.wait_ge(used[k], n)
                else:
                    sp.wait_ge(used[k], it * per + n)
                sp.dma_start(slots[k][:, 0:width], src).then_inc(full[k], 16)

            for g_ in range(6):
                load(g_ % 3, i["ada"][g_])
                loads[g_ % 3] += 1
                if g_ == 2:
                    for dst, src in ((ident[:, :], "ident"), (flip, "flip"), (head_sel[:, :, :], "head_sel"), (na_mask[:, :], "na_mask"),
                                     (conv_w[:, :, :], "conv_w"), (conv_b[:, :], "conv_b"), (gate_b[:, :], "gate_b"),
                                     (ml_gn[:, :], "ml_gn")):
                        sp.dma_start(dst, i[src]).then_inc(sem("even_params_in"), 16)
                    for qr in range(ROWS):
                        for kr in range(ROWS):
                            at = (kr - qr + RPB_H // 2) * RPB_W + RPB_W // 2 - (GRID_W - 1)
                            src = bass.AP(tensor=i["rpb"].tensor, offset=at, ap=[[1, GRID_W], [RPB_H * RPB_W, NA_HEADS], [1, GRID_W]])
                            p0 = GRID_W * (1 - qr % 2)
                            sp.dma_start(bias_flipped[p0:p0 + GRID_W, qr // 2, :, kr * GRID_W:(kr + 1) * GRID_W], src).then_inc(sem("na_bias_in"), 16)
                if g_ == 0:
                    for dst, src in ((s5_par[:, :, :], "s5_par"), (log_g[:, :, :], "decay_logit")):
                        sp.dma_start(dst, i[src]).then_inc(sem("s5_params_in"), 16)
                if g_ == 3:
                    for dst, src in ((s5_d[:, :], "s5_d"), (glu_b[:, :], "glu_b"), (ret_gn[:, :], "ret_gn")):
                        sp.dma_start(dst, i[src]).then_inc(sem("odd_params_in"), 16)
                if g_ == 1:
                    sp.dma_start(modb[:, :, :, :], i["modb"]).then_inc(sem("params_in"), 16)
                    sp.dma_start(lng[:, :, :], i["lng"]).then_inc(sem("params_in"), 16)
                    sp.dma_start(lnb[:, :, :], i["lnb"]).then_inc(sem("params_in"), 16)
                    sp.dma_start(h[:, :, :], i["x"]).then_inc(sem("x_in"), 16)

            def ffn_loads(s):
                first, n_ada = ADA_IN[f"ffn{s}"]
                src = i["gateup"][s]

                if s == 1:
                    sp.wait_ge(sem("r_ready"), before("r_ready", f"ffn{s}"))
                    load_cvec()
                looped = 5 if n_ada != 6 else 3
                for lo, hi, ada in ((0, looped, n_ada > 0), (looped, 5, False)):
                    if hi <= lo:
                        continue
                    keep = list(loads)
                    with sp.Fori(0, hi - lo) as it:
                        for b in range(2):
                            if ada:
                                ada_src = i["ada"][bass.ds(it * 2 + (first + 2 * lo + b), 1), :, :].rearrange("a p n -> (a p) n")
                                load(2, ada_src, it=it, per=2)
                                loads[2] += 1
                            load(b, src[bass.ds(it * 2 + (2 * lo + b), 1), :, :].rearrange("a p n -> (a p) n"), it=it, per=1)
                            loads[b] += 1
                    for k in range(5):
                        loads[k] = keep[k] + (loads[k] - keep[k]) * (hi - lo)
                if n_ada == 12:
                    load(2, i["ada"][first + 10])
                    loads[2] += 1
                load(0, src[PAIRS - 1])
                loads[0] += 1
                if n_ada == 12:
                    load(2, i["ada"][first + 11])
                    loads[2] += 1
                for d in range(KT):
                    k = 3 + d % 2
                    if d == 0 and s == 2:
                        sp.wait_ge(used[2], loads[2])
                        sp.dma_start(steps, i["steps"]).then_inc(sem("s5_steps_in"), 16)
                        for dst, src in ((c_raw, "s5_c"), (b_raw, "s5_b"), (rope, "rope"), (rope_swap, "rope_swap")):
                            sp.dma_start(dst, i[src]).then_inc(sem("odd_params_in"), 16)
                    if d == 1 and s in (1, 3):
                        sp.wait_ge(sem("r_ready"), before("r_ready", stages[2 * s - 1 if s == 1 else 4]) + 1)
                    load(k, i["down"][s, d], width=FT * P)
                    loads[k] += 1

            for s in range(4):
                ffn_loads(s)
                if s == 0:
                    for k, src, at, width in EVEN_LOADS:
                        load(k, i[src] if at is None else i[src][at], width=width)
                        loads[k] += 1
                if s == 2:
                    n_load = [0]

                    def odd_load():
                        k, src, at, width = ODD_LOADS[n_load[0]]
                        n_load[0] += 1
                        load(k, i[src] if at is None else i[src][at], width=width)
                        loads[k] += 1

                    odd_load()
                    odd_load()
                    for n in range(4):
                        sp.wait_ge(sem(f"table_written{n}"), 16 * (len(UNITS5) // 4))
                    for _ in range(3):
                        odd_load()
                    sp.wait_ge(sem("r_ready"), before("r_ready", "ffn2") + KT)
                    for u, (st, way) in enumerate(UNITS5):
                        if u >= TABLE_RING:
                            sp.wait_ge(sem("s5_x_ready"), u - TABLE_RING + 1)
                        sp.dma_start(tables[:, u % TABLE_RING, :, :].rearrange("p a b -> p (a b)"), tables_dram[u]).then_inc(sem(f"table_in{u % TABLE_RING}"), 16)
                        if u in (14, 22, 30):
                            odd_load()
            sp.wait_ge(sem("out_written"), 16 * KT)

        @block.tensor
        def _(pe):
            uses = uses_before("start")

            def take(k, it=None, per=0):
                uses[k] += 1
                if it is None:
                    pe.wait_ge(full[k], 16 * uses[k])
                else:
                    pe.wait_ge(full[k], it * (16 * per) + 16 * uses[k])

            pe.wait_ge(sem("even_params_in"), 16 * 8)
            pe.wait_ge(sem("na_bias_in"), 16 * ROWS * ROWS)
            for n in range(8):
                nc.tensor.matmul(banks[n][:, :], flip, bias_flipped[:, n // 4, 2 * (n % 4):2 * (n % 4) + 2, :]
                                 .rearrange("p a b -> p (a b)"), start=True, stop=True).then_inc(sem("na_bias_turned"), 1)

            def ffn(s):
                name = f"ffn{s}"
                c0 = CTX if s == 3 else 0
                m_ready, gate_done, up_done = sem("m_ready"), sem("gate_done"), sem("up_done")
                silu_done, g_ready = sem("silu_done"), sem("g_ready")

                def pair(b, n, it):
                    take(b, it, 1)
                    for j in range(2):
                        f = n + j
                        for bank, done, off, freed in ((gate_bank, gate_done, 0, silu_done), (up_bank, up_done, 1, g_ready)):
                            if it is not None:
                                pe.wait_ge(freed, it * 4 + (s * FT + f - 1))
                            elif f >= 2:
                                pe.wait_ge(freed, s * FT + f - 1)
                            for c in range(KT):
                                if f == 0 and off == 0:
                                    pe.wait_ge(m_ready, before("m_ready", name) + c + 1)
                                last = nc.tensor.matmul(bank[j][:, c0:T], wslot(b)[:, 2 * j + off, c, :], m[:, c, c0:T],
                                                        start=(c == 0), stop=(c == KT - 1))
                            if off == 1 and j == 1:
                                last.then_inc(used[b], 1)
                            else:
                                last.then_inc(done, 1)

                if s == 0:
                    pe.wait_ge(sem("na_bias_masked"), 8)
                pair(0, 0, None)
                pair(1, 2, None)
                keep = list(uses)
                with pe.Fori(0, PAIRS // 2 - 1) as it:
                    for b in range(2):
                        pair(b, 4 + 2 * b, it)
                for k in range(5):
                    uses[k] = keep[k] + (uses[k] - keep[k]) * (PAIRS // 2 - 1)
                pair(0, FT - 2, None)
                down_read = sem("r_ready")
                for d in range(KT):
                    take(3 + d % 2)
                    if d >= 2:
                        pe.wait_ge(down_read, before("r_ready", name) + d - 1)
                    for f in range(FT):
                        if d == 0 and f >= FT - 2:
                            pe.wait_ge(g_ready, s * FT + f + 1)
                        if d == 0 and f == 0:
                            pe.wait_ge(g_ready, s * FT + FT - 2)
                        last = nc.tensor.matmul(out_bank[d % 2][:, c0:T], slots[3 + d % 2][:, f * P:(f + 1) * P], g[:, f, c0:T],
                                                start=(f == 0), stop=(f == FT - 1))
                    last.then_inc(used[3 + d % 2], 1)
                norm_stats(name, c0)

            def norm_stats(name, c0):
                pe.wait_ge(sem("mean_w_ready"), 3)
                pe.wait_ge(sem("sums"), before("sums", name) + 2 * KT)
                nc.tensor.matmul(stat_bank[:, c0:T], mean_w[:, :], rsum[:, c0:T], start=True, stop=True).then_inc(sem("stat"), 1)
                nc.tensor.matmul(stat2_bank[:, c0:T], mean_w[:, :], rsq[:, c0:T], start=True, stop=True).then_inc(sem("stat"), 1)
                if name != "ffn3":
                    pe.wait_ge(sem("stat_read"), before("stat_read", name) + 2)

            def out_proj(name, slot_pair, c0):
                for d in range(KT):
                    k = slot_pair[d // 4]
                    if d % 4 == 0:
                        take(k)
                    if d >= 2:
                        pe.wait_ge(sem("r_ready"), before("r_ready", name) + d - 1)
                    for c in range(KT):
                        if d == 0:
                            pe.wait_ge(sem(f"{name}_y{c // 4}"), c % 4 + 1 if c >= 4 or name == "odd" else 2 * (c + 1))
                        last = nc.tensor.matmul(out_bank[d % 2][:, c0:T], wslot(k)[:, d % 4, c, :], y[:, c, c0:T],
                                                start=(c == 0), stop=(c == KT - 1))
                    last.then_inc(used[k] if d % 4 == 3 else sem(f"{name}_out_done"), 1)
                norm_stats(name, c0)

            def project(name, at, k, token_major, c0=0):
                take(k)
                for j in range(4):
                    n = at + j
                    if n >= 4:
                        pe.wait_ge(sem(f"{name}_proj_read"), n - 3)
                    for c in range(KT):
                        if at == 0 and j == 0:
                            pe.wait_ge(sem("m_ready"), before("m_ready", name) + c + 1)
                        if token_major:
                            last = nc.tensor.matmul(banks[n % 4][:, :], m[:, c, j * P:(j + 1) * P],
                                                    slots[k][:, c * WIDTH:(c + 1) * WIDTH], start=(c == 0), stop=(c == KT - 1))
                        else:
                            last = nc.tensor.matmul(banks[n % 4][:, c0:T], wslot(k)[:, j, c, :], m[:, c, c0:T],
                                                    start=(c == 0), stop=(c == KT - 1))
                    last.then_inc(used[k] if j == 3 else sem(f"{name}_proj_done"), 1)

            def even():
                uses[:] = uses_before("even")
                project("even", 0, 0, False)
                take(1)
                gw = slots[1][:, 0:KT * 16].rearrange("p (k n) -> p k n", n=16)
                for t in range(TT):
                    for c in range(KT):
                        last = nc.tensor.matmul(banks[4][:, 16 * t:16 * t + 16], m[:, c, t * P:(t + 1) * P], gw[:, c, :],
                                                start=(c == 0), stop=(c == KT - 1))
                last.then_inc(used[1], 1)
                project("even", 4, 2, False)
                pe.wait_ge(sem("even_params_in"), 16 * 8)
                pe.wait_ge(sem("even_gates_read"), 1)
                for kind in range(4):
                    for t in range(TT):
                        last = nc.tensor.transpose(banks[4 + kind][0:HEADS, t * P:(t + 1) * P],
                                                   gates_tok[:, t, 4 * kind:4 * kind + 4], ident[:, :])
                    last.then_inc(sem("even_rows_done"), 1)
                project("even", 8, 3, False)
                project("even", 12, 0, False)
                project("even", 16, 1, True)
                project("even", 20, 2, True)
                pe.wait_ge(sem("even_a_ready"), 1)
                for way in range(2):
                    for t in range(TT):
                        at = (way * TT + t) * HEADS
                        last = nc.tensor.transpose(banks[6][:, at:at + HEADS], rows[:, way, t * P:(t + 1) * P], ident[0:HEADS, 0:HEADS])
                last.then_inc(sem("even_acol_done"), 1)

                def scores(u):
                    hp, st, hh, qt = UNITS[u]
                    r0 = NA_DIM * hh
                    if u == 0:
                        pe.wait_ge(sem("even_proj_read"), 24)
                    if u >= 2:
                        pe.wait_ge(sem("na_scores_read"), u - 1)
                    q0 = STREAMS[st][0] + qt * P
                    keys = CTX if st == 0 else T
                    nc.tensor.matmul(banks[u % 2][:, 0:keys], na_q[r0:r0 + NA_DIM, hp, q0:q0 + P],
                                     na_k[r0:r0 + NA_DIM, hp, 0:keys], start=True, stop=True).then_inc(sem("na_scores_done"), 1)

                scores(0)
                scores(1)
                for u, (hp, st, hh, qt) in enumerate(UNITS):
                    tiles = 2 if st == 0 else 4
                    pe.wait_ge(sem("na_probs_ready"), u + 1)
                    if u >= 2:
                        pe.wait_ge(sem("na_pT_ready"), u - 1)
                    for kt in range(tiles):
                        last = nc.tensor.transpose(banks[2 + u % 2][:, kt * P:(kt + 1) * P], probs[:, u % 2, kt * P:(kt + 1) * P], ident[:, :])
                    last.then_inc(sem("na_pT_done"), 1)
                    if u + 2 < len(UNITS):
                        scores(u + 2)
                    if qt == 1:
                        pe.wait_ge(sem("na_pT_ready"), u + 1)
                        group = u // 4
                        if group >= 2 and hh == 0:
                            pe.wait_ge(sem("even_y0"), group - 1)
                        for kt in range(tiles):
                            last = nc.tensor.matmul(banks[4 + group % 2][NA_DIM * hh:NA_DIM * (hh + 1), 0:CTX],
                                                    na_v[:, kt, (2 * hp + hh) * NA_DIM:(2 * hp + hh + 1) * NA_DIM],
                                                    probsT[:, (u // 2) % 2, kt, :], start=(kt == 0), stop=(kt == tiles - 1))
                        last.then_inc(sem("na_out_done"), 1)

                take(3)
                qk_w = slots[3][:, 0:2 * WIDTH].rearrange("p (a n) -> p a n", n=P)
                pe.wait_ge(sem("even_y0"), 8)
                for hd in range(HEADS):
                    for a in range(2):
                        if hd:
                            pe.wait_ge(sem("ml_hsum_ready"), hd) if a == 0 else None
                        last = nc.tensor.matmul(banks[6 + a][:, :], qk_w[:, a * HEADS + hd, :], xc[:, hd, :], start=True, stop=True)
                        last.then_inc(used[3] if hd == HEADS - 1 and a == 1 else sem("ml_qk_proj_done"), 1)
                    pe.wait_ge(sem("ml_qk_ready"), 2 * (hd + 1))
                    for n in range(TT):
                        lo = 0 if n < 2 else CTX
                        last = nc.tensor.matmul(qk_cols(n, lo, T), ml_kh[:, hd % 2, n * P:(n + 1) * P], ml_qh[:, hd % 2, lo:T],
                                                start=True, stop=True)
                    last.then_inc(sem("ml_scores_done"), 1)
                    for way in range(2):
                        v = 2 * hd + way
                        if v:
                            pe.wait_ge(sem("ml_arg_ready"), TT * v)
                            pe.wait_ge(sem("ml_em_read"), v)
                        nc.tensor.matmul(banks[3][:, :], head_sel[:, hd, :], rows[:, 4 + way, :], start=True, stop=True).then_inc(sem("ml_negm_done"), 1)
                        nc.tensor.matmul(banks[6][:, :], head_sel[:, hd, :], rows[:, 2 + way, :], start=True, stop=True).then_inc(sem("ml_em_done"), 1)
                        if v:
                            pe.wait_ge(sem("ml_quot_ready"), v)
                        for k, n in enumerate(ORDER[way]):
                            pe.wait_ge(sem("ml_s_ready"), TT * v + k + 1)
                            for a, b in TARGETS[way][n]:
                                s_ = decay[way][:, n, a:b]
                                end = k == TT - 1 and b == TARGETS[way][n][-1][1]
                                nc.tensor.matmul(banks[4][:, a:b], ml_v[:, n, hd * P:(hd + 1) * P], s_, start=(k == 0), stop=end)
                                last = nc.tensor.matmul(banks[5][:, a:b], ones_w[:, :], s_, start=(k == 0), stop=end)
                        last.then_inc(sem("ml_numden_done"), 1)
                head_norm_stats("even", 0)
                out_proj("even", (0, 1), 0)

            def head_norm_stats(name, c0):
                pe.wait_ge(sem(f"{name}_hs_all"), 1)
                for hd in range(HEADS):
                    nc.tensor.matmul(banks[hd][:, c0:T], hmean_w[:, :], hs[:, hd, c0:T], start=True, stop=True).then_inc(sem(f"{name}_hmean_done"), 1)
                for hd in range(HEADS):
                    pe.wait_ge(sem(f"{name}_hsq_ready"), hd + 1)
                    nc.tensor.matmul(banks[hd][:, c0:T], hmean_w[:, :], hsq[:, hd, c0:T], start=True, stop=True).then_inc(sem(f"{name}_hvar_done"), 1)

            def odd():
                uses[:] = uses_before("odd")
                ring, cnt_ = banks[6:8], [0]

                def proj_tile(j, k, token_major, c0=0):
                    if j == 0:
                        take(k)
                    n = cnt_[0]
                    cnt_[0] += 1
                    if n >= 2:
                        pe.wait_ge(sem("odd_proj_read"), n - 1)
                    for c in range(KT):
                        if n == 0:
                            pe.wait_ge(sem("m_ready"), before("m_ready", "odd") + c + 1)
                        if token_major:
                            last = nc.tensor.matmul(ring[n % 2][:, :], m[:, c, j * P:(j + 1) * P],
                                                    slots[k][:, c * WIDTH:(c + 1) * WIDTH], start=(c == 0), stop=(c == KT - 1))
                        else:
                            last = nc.tensor.matmul(ring[n % 2][:, c0:T], wslot(k)[:, j, c, :], m[:, c, c0:T],
                                                    start=(c == 0), stop=(c == KT - 1))
                    last.then_inc(used[k] if j == 3 else sem("odd_proj_done"), 1)

                def inputs(u):
                    st, way = UNITS5[u]
                    k, r0 = st // 4, PAIR * (st % 4)
                    pe.wait_ge(sem("odd_proj_read"), k + 1)
                    if u >= 2:
                        pe.wait_ge(sem("s5_prod_done"), u - 1)
                    for r in range(2):
                        last = nc.tensor.matmul(banks[2 * (u % 2) + r][:, :], b_raw[r0:r0 + PAIR, r, way * 4 + k, :], s5_u[r0:r0 + PAIR, k, :],
                                                start=True, stop=True)
                    last.then_inc(sem("s5_in_done"), 1)

                for j in range(4):
                    proj_tile(j, 0, False)
                pe.wait_ge(sem("odd_params_in"), 16 * 7)
                inputs(0)
                inputs(1)
                tiles = [(j, k, tm, c0) for k, tm, c0 in ((1, False, 0), (2, True, 0), (3, False, CTX), (0, False, CTX)) for j in range(4)]
                pe.wait_ge(sem("s5_c_ready"), 1)
                for u, (st, way) in enumerate(UNITS5):
                    if u % 2 == 0:
                        proj_tile(*tiles[u // 2])
                    if u + 2 < len(UNITS5):
                        inputs(u + 2)
                    pe.wait_ge(sem("s5_x_ready"), u + 1)
                    k, r0 = st // 4, PAIR * (st % 4)
                    for r in range(2):
                        last = nc.tensor.matmul(banks[4 + k // 2][r0:r0 + PAIR, LAT * (k % 2):LAT * (k % 2 + 1)],
                                                c_fold[:, r, way * S5_TILES + st, :], s5_x[:, u % 2, r, :],
                                                start=(way == 0 and r == 0), stop=(way == 1 and r == 1))
                    last.then_inc(sem("s5_y_done"), 1)
                pe.wait_ge(sem("odd_proj_read"), 20)
                for n in range(4):
                    src = ret_q[:, 2 * n:2 * n + 2, :] if n < 2 else ret_k[:, 2 * n - 4:2 * n - 2, CTX:T]
                    nc.tensor.matmul(banks[n][:, :].rearrange("p (a b) -> p a b", b=LAT), rope_swap, src, start=True, stop=True).then_inc(sem("rope_done"), 1)
                take(1)
                pe.wait_ge(sem("s5_act_ready"), 4)
                gw = slots[1][:, 0:4 * WIDTH].rearrange("p (k n) -> p k n", n=WIDTH)
                for d in range(4):
                    if d >= 2:
                        pe.wait_ge(sem("glu_read"), d - 1)
                    for c in range(4):
                        last = nc.tensor.matmul(ring[d % 2][:, 0:LAT], gw[:, c, d * P:(d + 1) * P], s5_u[:, c, CTX:T], start=(c == 0), stop=(c == 3))
                    last.then_inc(used[1] if d == 3 else sem("glu_done"), 1)
                for hd in range(HEADS):
                    pe.wait_ge(sem("rope_ready"), 4 if hd < 2 else 4)
                    if hd >= 2:
                        pe.wait_ge(sem("ret_s_ready"), 8 * (hd - 1))
                    for n in range(TT):
                        last = nc.tensor.matmul(banks[2 * (hd % 2) + n // 2][:, LAT * (n % 2):LAT * (n % 2 + 1)],
                                                ret_k[:, hd, n * P:(n + 1) * P], ret_q[:, hd, :], start=True, stop=True)
                    last.then_inc(sem("ret_scores_done"), 1)
                    if hd:
                        ret_out(hd - 1)
                ret_out(HEADS - 1)
                head_norm_stats("odd", CTX)
                out_proj("odd", (2, 3), CTX)

            def ret_out(hd):
                if hd >= 2:
                    pe.wait_ge(sem("ret_hs_ready"), hd - 1)
                for k, (way, n, a, b) in enumerate(RET_PARTS):
                    pe.wait_ge(sem("ret_s_ready"), 8 * hd + k + 1)
                    last = nc.tensor.matmul(banks[4 + hd % 2][:, a:b], ret_v[:, n, hd * P:(hd + 1) * P],
                                            ret_s[:, (2 * hd + way) % 4, n, a:b], start=(k == 0), stop=(k == 7))
                last.then_inc(sem("ret_out_done"), 1)

            for s in range(4):
                ffn(s)
                if s == 0:
                    even()
                if s == 2:
                    odd()

        @block.scalar
        def _(act):
            def condition(n):
                act.wait_ge(sem("cvec_in"), 32 * (n + 1))
                for s_ in range(2):
                    nc.scalar.activation(csilu[s_], csilu[s_], ACT.Silu).then_inc(sem("csilu_ready"), 1)

            condition(0)

            def modulate(n, c0):
                ready = sem("m_ready")
                act.wait_ge(sem("folded"), 2 * n + 2)
                for d in range(KT):
                    if n:
                        act.wait_ge(sem("z"), before("z", stages[n - 1]) + d + 1)
                    elif d == 0:
                        act.wait_ge(sem("x_in"), 16)
                    for s_, (a, b) in enumerate(STREAMS):
                        if b <= c0:
                            continue
                        last = nc.scalar.activation(m[:, d, a:b], h[:, d, a:b], ACT.Identity,
                                                    scale=mscale[:, n, d, s_:s_ + 1], bias=mshift[:, n, d, s_:s_ + 1])
                    last.then_inc(ready, 1)

            def log_sigmoid_soft(x):
                nc.scalar.activation(x, x, ACT.Exp).then_inc(sem("log_g_soft"), 1)
                act.wait_ge(sem("log_g_soft"), 1)
                nc.scalar.activation(x, x, ACT.Ln, bias=1.0).then_inc(sem("log_g_soft"), 1)

            act.wait_ge(sem("log_g_nabs"), 1)
            log_sigmoid_soft(small[:, 7, 0:2 * HEADS])
            act.wait_ge(sem("s5_small_phase"), 1)
            nc.scalar.activation(small[:, 2, :], small[:, 0, :], ACT.Sin).then_inc(sem("s5_small_sin"), 1)
            nc.scalar.activation(small[:, 3, :], small[:, 0, :], ACT.Sin, scale=0.5).then_inc(sem("s5_small_sin"), 1)

            def sines(u):
                act.wait_ge(sem("phase_ready"), u + 1)
                if u >= 4:
                    act.wait_ge(sem(f"table_written{u % 4}"), 16 * (u // 4))
                nc.scalar.activation(tables_out[:, u % 4, 1, :], phase[:, u % 2, 0, :], ACT.Sin).then_inc(sem("phase_sin"), 1)
                nc.scalar.activation(phase[:, u % 2, 2, :], phase[:, u % 2, 0, :], ACT.Sin, scale=0.5).then_inc(sem("phase_half"), 1)
                if u:
                    table_out(u - 1)

            def table_out(u):
                act.wait_ge(sem("table_cos_ready"), u + 1)
                act.dma_start(tables_dram[u], tables_out[:, u % 4, :, :].rearrange("p a b -> p (a b)")).then_inc(sem(f"table_written{u % 4}"), 16)

            modulate(0, 0)

            def squares(name, c0):
                for d in range(KT):
                    if name == "ffn2":
                        for u in range(4 * d, 4 * d + 4):
                            sines(u)
                        if d == KT - 1:
                            table_out(len(UNITS5) - 1)
                    act.wait_ge(sem("r_ready"), before("r_ready", name) + d + 1)
                    if d >= 2:
                        act.wait_ge(sem("sums"), before("sums", name) + 2 * (d - 1))
                    nc.scalar.activation(sq[:, d % 2, c0:T], h[:, d, c0:T], ACT.Square).then_inc(sem("sq"), 1)

            def norm(n, name, c0):
                act.wait_ge(sem("var"), before("var", name) + 1)
                nc.scalar.activation(rstd[:, c0:T], rstd[:, c0:T], ACT.Sqrt).then_inc(sem("std"), 1)
                if n + 1 < 6:
                    modulate(n + 1, CTX if n + 1 == 5 else 0)

            def ffn(s):
                name = f"ffn{s}"
                c0 = CTX if s == 3 else 0

                def tile(f, j, it=None):
                    if it is None:
                        act.wait_ge(sem("gate_done"), s * FT + f + 1)
                        if f >= 2:
                            act.wait_ge(sem("g_ready"), s * FT + f - 1)
                    else:
                        act.wait_ge(sem("gate_done"), s * FT + it * 2 + f + 1)
                        act.wait_ge(sem("g_ready"), s * FT + it * 2 + (f - 1))
                    nc.scalar.activation(silu_g[:, j, c0:T], gate_bank[j][:, c0:T], ACT.Silu).then_inc(sem("silu_done"), 1)

                if s == 1:
                    condition(1)
                tile(0, 0)
                tile(1, 1)
                with act.Fori(0, PAIRS - 1) as it:
                    tile(2, 0, it)
                    tile(3, 1, it)
                squares(name, c0)

            slot_done = [0] * 5

            def projected(name, n, k):
                if n % 4 == 3:
                    slot_done[k] += 1
                    act.wait_ge(used[k], slot_done[k])
                else:
                    act.wait_ge(sem(f"{name}_proj_done"), 3 * (n // 4) + n % 4 + 1)

            def head_norm(name, c0):
                for hd in range(HEADS):
                    act.wait_ge(sem(f"{name}_hc_ready"), hd + 1)
                    nc.scalar.activation(hsq[:, hd, c0:T], hs[:, hd, c0:T], ACT.Square).then_inc(sem(f"{name}_hsq_ready"), 1)
                act.wait_ge(sem(f"{name}_hvar_ready"), HEADS)
                nc.scalar.activation(hvar[:, :, c0:T], hvar[:, :, c0:T], ACT.Sqrt).then_inc(sem(f"{name}_hstd_ready"), 1)

            def even():
                slot_done[:] = uses_before("even")
                read = sem("even_proj_read")
                act.wait_ge(sem("even_params_in"), 16 * 8)
                for n in range(4):
                    projected("even", n, 0)
                    if n >= 2:
                        act.wait_ge(sem("even_conv_done"), n - 1)
                    nc.scalar.activation(xm[:, n % 2, :], banks[n % 4][:, :], ACT.Copy).then_inc(read, 1)
                slot_done[1] += 1
                act.wait_ge(used[1], slot_done[1])
                nc.scalar.activation(gates_tok.rearrange("p a b -> p (a b)"), banks[4][:, 0:TT * 16], ACT.Copy).then_inc(sem("even_gates_read"), 1)
                for hd in range(HEADS):
                    act.wait_ge(sem("even_conv_done"), hd + 1)
                    nc.scalar.activation(xc[:, hd, :], xc[:, hd, :], ACT.Silu).then_inc(sem("even_xc_ready"), 1)
                for n in range(4, 8):
                    projected("even", n, 2)
                    nc.scalar.activation(sig_o[:, n - 4, :], banks[n % 4][:, :], ACT.Sigmoid).then_inc(read, 1)
                for kind in range(4):
                    act.wait_ge(sem("even_rows_done"), kind + 1)
                    nc.scalar.activation(rows[:, kind, :], banks[4 + kind][0:HEADS, :], ACT.Identity, bias=gate_b[:, kind:kind + 1]).then_inc(sem("even_rows_ready"), 1)
                act.wait_ge(sem("even_nabs_ready"), 1)
                nc.scalar.activation(rows[:, 6:8, :], rows[:, 6:8, :], ACT.Exp).then_inc(sem("even_soft"), 1)
                act.wait_ge(sem("even_soft"), 1)
                nc.scalar.activation(rows[:, 6:8, :], rows[:, 6:8, :], ACT.Ln, bias=1.0).then_inc(sem("even_soft"), 1)
                for n in range(8, 24):
                    if n == 12:
                        act.wait_ge(sem("even_bm_ready"), 1)
                        nc.scalar.activation(rows[:, 2:4, :], rows[:, 2:4, :], ACT.Exp).then_inc(sem("even_em_ready"), 1)
                    projected("even", n, (3, 0, 1, 2)[n // 4 - 2])
                    dst = (na_q, na_k, na_v, ml_v)[n // 4 - 2][:, n % 4, :]
                    nc.scalar.activation(dst, banks[n % 4][:, :], ACT.Copy, scale=NA_DIM ** -0.5 if n < 12 else 1.0).then_inc(read, 1)
                act.wait_ge(sem("even_acol_done"), 1)
                nc.scalar.activation(acol[:, :, :, :].rearrange("p a b c -> p (a b c)"), banks[6][:, 0:2 * TT * HEADS], ACT.Copy).then_inc(sem("even_acol_ready"), 1)

                def exps(u):
                    st = UNITS[u][1]
                    keys = CTX if st == 0 else T
                    act.wait_ge(sem("na_max_ready"), u + 1)
                    src = banks[u % 2][:, 0:keys] if st == 0 else probs[:, u % 2, :]
                    nc.scalar.activation(probs[:, u % 2, 0:keys], src, ACT.Exp, bias=col[:, u % 2:u % 2 + 1],
                                         accum_out=col[:, 2 + u % 2:3 + u % 2]).then_inc(sem("na_exp_done"), 1)

                exps(0)
                for u, (hp, st, hh, qt) in enumerate(UNITS):
                    if u + 1 < len(UNITS):
                        exps(u + 1)
                    tiles = 2 if st == 0 else 4
                    act.wait_ge(sem("na_pT_done"), u + 1)
                    if u >= 4 and qt == 0:
                        act.wait_ge(sem("na_out_done"), u // 2 - 1)
                    nc.scalar.activation(probsT[:, (u // 2) % 2, 0:tiles, qt * P:(qt + 1) * P],
                                         banks[2 + u % 2][:, 0:tiles * P].rearrange("p (a n) -> p a n", n=P), ACT.Copy).then_inc(sem("na_pT_ready"), 1)

                slot_done[3] += 1
                for hd in range(HEADS):
                    for a, (dst, scale) in enumerate(((ml_qh, 1.0), (ml_kh, HDIM ** -0.5))):
                        if hd == HEADS - 1 and a == 1:
                            act.wait_ge(used[3], slot_done[3])
                        else:
                            act.wait_ge(sem("ml_qk_proj_done"), 2 * hd + a + 1)
                        nc.scalar.activation(dst[:, hd % 2, :], banks[6 + a][:, :], ACT.Copy, scale=scale).then_inc(sem("ml_qk_ready"), 1)
                    for way in range(2):
                        v = 2 * hd + way
                        for k, n in enumerate(ORDER[way]):
                            act.wait_ge(sem("ml_arg_ready"), TT * v + k + 1)
                            a, b = TARGETS[way][n][0][0], TARGETS[way][n][-1][1]
                            nc.scalar.activation(decay[way][:, n, a:b], decay[way][:, n, a:b], ACT.Exp).then_inc(sem("ml_exp_done"), 1)
                        act.wait_ge(sem("ml_em_done"), v + 1)
                        nc.scalar.activation(em_b[:, way, :], banks[6][:, :], ACT.Copy).then_inc(sem("ml_em_read"), 1)
                head_norm("even", 0)
                squares("even", 0)
                norm(1, "even", 0)

            def odd():
                slot_done[:] = uses_before("odd")
                read = sem("odd_proj_read")
                for n in range(20):
                    projected("odd", n, (0, 1, 2, 3, 0)[n // 4])
                    bank = banks[6 + n % 2]
                    if n < 4:
                        ins = nc.scalar.activation(s5_u[:, n, :], bank[:, :], ACT.Copy)
                    elif n < 8:
                        ins = nc.scalar.activation(ret_k[:, n - 4, :], bank[:, :], ACT.Copy, scale=HDIM ** -0.5)
                    elif n < 12:
                        ins = nc.scalar.activation(ret_v[:, n - 8, :], bank[:, :], ACT.Copy)
                    elif n < 16:
                        ins = nc.scalar.activation(ret_q[:, n - 12, :], bank[:, CTX:T], ACT.Copy)
                    else:
                        ins = nc.scalar.activation(ret_gate[:, n - 16, :], bank[:, CTX:T], ACT.Silu)
                    ins.then_inc(read, 1)
                for k in range(4):
                    act.wait_ge(sem("s5_skip_ready"), k + 1)
                    nc.scalar.activation(s5_u[:, k, CTX:T], s5_u[:, k, CTX:T], ACT.Gelu_apprx_tanh).then_inc(sem("s5_act_ready"), 1)
                slot_done[1] += 1
                for d in range(4):
                    if d == 3:
                        act.wait_ge(used[1], slot_done[1])
                    else:
                        act.wait_ge(sem("glu_done"), d + 1)
                    nc.scalar.activation(glu_sig[:, d, :], banks[6 + d % 2][:, 0:LAT], ACT.Sigmoid, bias=glu_b[:, d:d + 1]).then_inc(sem("glu_read"), 1)
                act.wait_ge(sem("rel_ready"), 2)
                act.wait_ge(sem("s5_z_ready"), len(UNITS5))
                act.wait_ge(sem("s5_x_ready"), len(UNITS5))
                for hd in range(HEADS):
                    for way in range(2):
                        nc.scalar.activation(ret_decay[:, 2 * hd + way, :], rel[:, way, :], ACT.Exp, scale=log_g[:, way, hd:hd + 1]).then_inc(sem("ret_decay_exp"), 1)
                head_norm("odd", CTX)
                squares("odd", CTX)
                norm(4, "odd", CTX)

            for s in range(4):
                ffn(s)
                norm([0, 2, 3, 5][s], f"ffn{s}", CTX if s == 3 else 0)
                if s == 0:
                    even()
                if s == 2:
                    odd()
            for d in range(KT):
                act.wait_ge(sem("h_ready"), before("h_ready", "ffn3") + d + 1)
                act.dma_start(out[:, d, :], h[:, d, CTX:T]).then_inc(sem("out_written"), 16)

        @block.vector
        def _(dve):
            chain = [0]
            mcount = [0]
            slot_done = [0] * 5

            def link(ins):
                chain[0] += 1
                ins.then_inc(sem("dve_chain"), 1)
                dve.wait_ge(sem("dve_chain"), chain[0])

            nc.vector.memset(mean_w[:, :], 1.0 / D).then_inc(sem("mean_w_ready"), 1)
            def exact_exp(dst, x, k_, p_):
                link(nc.vector.tensor_scalar(x, x, -87.0, 88.0, ALU.max, ALU.min))
                link(nc.vector.tensor_scalar(k_, x, 1.0 / math.log(2.0), ROUND, ALU.mult, ALU.add))
                link(nc.vector.tensor_scalar(k_, k_, ROUND, None, ALU.subtract))
                link(nc.vector.scalar_tensor_tensor(x, k_, -LN2_A, x, ALU.mult, ALU.add))
                link(nc.vector.scalar_tensor_tensor(x, k_, -LN2_B, x, ALU.mult, ALU.add))
                link(nc.vector.tensor_scalar(p_, x, 1.0 / math.factorial(8), None, ALU.mult))
                for n in range(7, 0, -1):
                    link(nc.vector.scalar_tensor_tensor(p_, p_, 1.0 / math.factorial(n), x, ALU.add, ALU.mult))
                link(nc.vector.tensor_scalar(p_, p_, 1.0, None, ALU.add))
                link(nc.vector.tensor_scalar(k_.bitcast(mybir.dt.int32), k_, 2.0 ** 23, 127 * 2.0 ** 23, ALU.mult, ALU.add))
                link(nc.vector.tensor_tensor(dst, p_, k_, ALU.mult))

            def reduce_angle(x, k_):
                link(nc.vector.tensor_scalar(k_, x, 1.0 / TWO_PI, ROUND, ALU.mult, ALU.add))
                link(nc.vector.tensor_scalar(k_, k_, ROUND, None, ALU.subtract))
                for part in (PI_A, PI_B, PI_C):
                    link(nc.vector.scalar_tensor_tensor(x, k_, -part, x, ALU.mult, ALU.add))
                return nc.vector.tensor_scalar(x, x, -math.pi, math.pi, ALU.max, ALU.min)

            dve.wait_ge(sem("s5_params_in"), 32)
            lg = log_g[:, :, :].rearrange("p a b -> p (a b)")
            soft = small[:, 7, 0:2 * HEADS]
            link(nc.vector.tensor_scalar(soft, lg, -1.0, None, ALU.mult))
            nc.vector.tensor_tensor(soft, soft, lg, ALU.min).then_inc(sem("log_g_nabs"), 1)
            re, im, dt = s5_par[:, 0, :], s5_par[:, 1, :], s5_par[:, 2, :]
            exact_exp(small[:, 4, :], dt, small[:, 5, :], small[:, 6, :])
            link(nc.vector.tensor_tensor(small[:, 1, :], re, small[:, 4, :], ALU.mult))
            link(nc.vector.tensor_tensor(dt, im, small[:, 4, :], ALU.mult))
            link(nc.vector.tensor_copy(small[:, 0, :], dt))
            reduce_angle(small[:, 0, :], small[:, 5, :]).then_inc(sem("s5_small_phase"), 1)
            exact_exp(s5_mag[:, :], small[:, 1, :], small[:, 5, :], small[:, 6, :])

            def phases(u):
                st, way = UNITS5[u]
                if u >= 2:
                    dve.wait_ge(sem("table_cos_ready"), u - 1)
                x = phase[:, u % 2, 0, :]
                link(nc.vector.tensor_scalar(x, steps[:, way, :], dt[:, way * S5_TILES + st:way * S5_TILES + st + 1], None, ALU.mult))
                reduce_angle(x, phase[:, u % 2, 1, :]).then_inc(sem("phase_ready"), 1)

            dve.wait_ge(sem("log_g_soft"), 2)
            nc.vector.scalar_tensor_tensor(lg, lg, 0.0, soft, ALU.min, ALU.subtract).then_inc(sem("log_g_ready"), 1)
            dve.wait_ge(sem("s5_small_sin"), 2)
            a_im, a_re, t0, t1 = small[:, 2, :], small[:, 3, :], small[:, 5, :], small[:, 6, :]
            link(nc.vector.tensor_tensor(a_re, a_re, a_re, ALU.mult))
            link(nc.vector.tensor_scalar(a_re, a_re, -2.0, 1.0, ALU.mult, ALU.add))
            link(nc.vector.tensor_tensor(a_re, a_re, s5_mag[:, :], ALU.mult))
            link(nc.vector.tensor_scalar(a_re, a_re, 1.0, None, ALU.subtract))
            link(nc.vector.tensor_tensor(a_im, a_im, s5_mag[:, :], ALU.mult))
            link(nc.vector.tensor_tensor(t0, re, re, ALU.mult))
            link(nc.vector.tensor_tensor(t1, im, im, ALU.mult))
            link(nc.vector.tensor_tensor(t0, t0, t1, ALU.add))
            link(nc.vector.reciprocal(small[:, 4, :], t0))
            for part, (p_, q_, op) in enumerate(((a_re, a_im, ALU.add), (a_im, a_re, ALU.subtract))):
                link(nc.vector.tensor_tensor(t0, p_, re, ALU.mult))
                link(nc.vector.tensor_tensor(t1, q_, im, ALU.mult))
                link(nc.vector.tensor_tensor(t0, t0, t1, op))
                nc.vector.tensor_tensor(s5_e[:, part, :], t0, small[:, 4, :], ALU.mult).then_inc(sem("s5_e_ready"), 1)
                dve.wait_ge(sem("s5_e_ready"), part + 1)
            dve.wait_ge(sem("params_in"), 48)

            def modulation(k, junk, it=None, per=0):
                slot_done[k] += 1
                gi = mcount[0]
                mcount[0] += 1
                turn = lambda step: 0 if it is None else it * step
                if gi:
                    dve.wait_ge(sem("mods_ready"), turn(per) + gi)
                dve.wait_ge(full[k], turn(16 * per) + 16 * slot_done[k])
                for j in range(8):
                    t, s_ = j // 2, j % 2
                    ins = nc.vector.tensor_tensor_reduce(out=junk, in0=slots[k][:, t * D:(t + 1) * D], in1=csilu[s_], scale=1.0, scalar=0.0,
                                                         op0=ALU.mult, op1=ALU.add, accum_out=ada_sum[:, t, s_:s_ + 1])
                    if j < 7:
                        ins.then_inc(sem("ada_part"), 1)
                        dve.wait_ge(sem("ada_part"), turn(7 * per) + 7 * gi + j + 1)
                    else:
                        ins.then_inc(used[k], 1)
                        dve.wait_ge(used[k], turn(per) + slot_done[k])
                flat = lambda buf: buf[:, :, :, :].rearrange("p a b c -> p (a b c)")
                if it is None:
                    dst, b_ = (flat(buf)[:, 8 * gi:8 * gi + 8] for buf in (mods, modb))
                else:
                    dst, b_ = (flat(buf)[:, bass.ds(it * (8 * per) + 8 * gi, 8)] for buf in (mods, modb))
                nc.vector.tensor_tensor(dst, ada_sum[:, :, :].rearrange("p a b -> p (a b)"), b_, ALU.add).then_inc(sem("mods_ready"), 1)

            ada_junk = L[:, 2 * T:4 * T]
            dve.wait_ge(sem("csilu_ready"), 2)
            for g_ in range(6):
                modulation(g_ % 3, R[:, 12288:12288 + D])
                if g_ == 3:
                    for n in range(8):
                        dve.wait_ge(sem("na_bias_turned"), n + 1)
                        cols = lambda v: v.rearrange("p (a c) -> p a c", c=GRID_W)
                        dst = na_bias[:, n // 4, 2 * (n % 4):2 * (n % 4) + 2, :].rearrange("p a b -> p (a b)")
                        nc.vector.tensor_tensor(cols(dst), cols(banks[n][:, :]),
                                                na_mask[:, :].unsqueeze(1).to_broadcast([P, 2 * ROWS, GRID_W]), ALU.add).then_inc(sem("na_bias_masked"), 1)

            def fold(n):
                dve.wait_ge(sem("mods_ready"), mod_groups[n])
                l, j = NORMS[n]
                part = lambda q: mods[:, l, (3 * j + q) * KT:(3 * j + q + 1) * KT, :]
                half = (1.0 if j == 1 else 0.5) / ALPHA
                link(nc.vector.tensor_scalar(mgate[:, n, :, :], part(2), half, None, ALU.mult))
                if n == 0:
                    nc.vector.tensor_scalar(mscale[:, 0, :, :], part(1), 1.0, None, ALU.add).then_inc(sem("folded"), 1)
                    nc.vector.tensor_copy(mshift[:, 0, :, :], part(0)).then_inc(sem("folded"), 1)
                    return
                link(nc.vector.tensor_scalar(mscale[:, n, :, :], part(1), 1.0, None, ALU.add))
                bias = lambda buf: buf[:, n - 1, :].unsqueeze(2).to_broadcast([P, KT, 2])
                link(nc.vector.tensor_tensor(mshift[:, n, :, :], mscale[:, n, :, :], bias(lnb), ALU.mult))
                nc.vector.tensor_tensor(mshift[:, n, :, :], mshift[:, n, :, :], part(0), ALU.add).then_inc(sem("folded"), 1)
                nc.vector.tensor_tensor(mscale[:, n, :, :], mscale[:, n, :, :], bias(lng), ALU.mult).then_inc(sem("folded"), 1)

            fold(0)

            def residual(n, name, d, bank, c0):
                for s_, (a, b) in enumerate(STREAMS):
                    if b <= c0:
                        continue
                    last = nc.vector.scalar_tensor_tensor(h[:, d, a:b], bank[:, a:b], mgate[:, n, d, s_:s_ + 1],
                                                          h[:, d, a:b], ALU.mult, ALU.add)
                last.then_inc(sem("r_ready"), 1)

            def norm(n, name, c0):
                w = slice(c0, T)
                dve.wait_ge(sem("stat"), before("stat", name) + 1)
                nc.vector.tensor_copy(mean[:, w], stat_bank[:, w]).then_inc(sem("stat_read"), 1)
                dve.wait_ge(sem("stat_read"), before("stat_read", name) + 1)
                link(nc.vector.tensor_tensor(rstd[:, w], mean[:, w], mean[:, w], ALU.mult))
                dve.wait_ge(sem("stat"), before("stat", name) + 2)
                nc.vector.tensor_tensor(rstd[:, w], stat2_bank[:, w], rstd[:, w], ALU.subtract).then_inc(sem("stat_read"), 1)
                dve.wait_ge(sem("stat_read"), before("stat_read", name) + 2)
                nc.vector.tensor_scalar(rstd[:, w], rstd[:, w], 0.0, EPS / ALPHA ** 2, ALU.max, ALU.add).then_inc(sem("var"), 1)
                sub = lambda d: nc.vector.tensor_tensor(h[:, d, w], h[:, d, w], mean[:, w], ALU.subtract)
                sub(0).then_inc(sem("c"), 1)
                dve.wait_ge(sem("std"), before("std", name) + 1)
                link(nc.vector.reciprocal(rstd[:, w], rstd[:, w]))
                for d in range(KT):
                    if d + 1 < KT:
                        sub(d + 1).then_inc(sem("c"), 1)
                    dve.wait_ge(sem("c"), before("c", name) + d + 1)
                    nc.vector.tensor_tensor(h[:, d, w], h[:, d, w], rstd[:, w], ALU.mult).then_inc(sem("z"), 1)

            def ffn(s):
                name = f"ffn{s}"
                c0 = CTX if s == 3 else 0

                def pair(b, n, it, ada):
                    if ada:
                        modulation(2, ada_junk, it=it, per=2)
                    slot_done[b] += 1
                    for j in range(2):
                        f = n + j
                        if it is None:
                            dve.wait_ge(sem("silu_done"), s * FT + f + 1)
                            dst = g[:, f, c0:T]
                        else:
                            dve.wait_ge(sem("silu_done"), s * FT + it * 4 + (f + 1))
                            dst = g[:, bass.ds(it * 4 + f, 1), c0:T].rearrange("p a n -> p (a n)")
                        if j == 0:
                            if it is None:
                                dve.wait_ge(sem("up_done"), s * PAIRS + f // 2 + 1)
                            else:
                                dve.wait_ge(sem("up_done"), s * PAIRS + it * 2 + (f // 2 + 1))
                        elif it is None:
                            dve.wait_ge(used[b], slot_done[b])
                        else:
                            dve.wait_ge(used[b], it + slot_done[b])
                        nc.vector.tensor_tensor(dst, silu_g[:, j, c0:T], up_bank[j][:, c0:T], ALU.mult).then_inc(sem("g_ready"), 1)

                n_ada = ADA_IN[name][1]
                looped = 5 if n_ada != 6 else 3
                if s == 1:
                    dve.wait_ge(sem("csilu_ready"), 4)
                pair(0, 0, None, n_ada > 0)
                pair(1, 2, None, n_ada > 0)
                for lo, hi, ada in ((1, looped, n_ada > 0), (looped, 5, False)):
                    if hi <= lo:
                        continue
                    keep, km = list(slot_done), mcount[0]
                    with dve.Fori(0, hi - lo) as it:
                        for b in range(2):
                            pair(b, 4 * lo + 2 * b, it, ada)
                    for k in range(5):
                        slot_done[k] = keep[k] + (slot_done[k] - keep[k]) * (hi - lo)
                    mcount[0] = km + (mcount[0] - km) * (hi - lo)
                pair(0, FT - 2, None, n_ada == 12)
                if n_ada == 12:
                    modulation(2, ada_junk)
                n = [0, 2, 3, 5][s]
                if s == 2:
                    dve.wait_ge(sem("s5_steps_in"), 16)
                for d in range(KT):
                    if s == 2:
                        for u in range(4 * d, 4 * d + 4):
                            phases(u)
                    k = 3 + d % 2
                    slot_done[k] += 1
                    dve.wait_ge(used[k], slot_done[k])
                    if d == 0:
                        dve.wait_ge(sem("h_ready"), before("h_ready", stages[n - 1]) + KT) if n else dve.wait_ge(sem("m_ready"), before("m_ready", name) + KT)
                    residual(n, name, d, out_bank[d % 2], c0)
                if n + 1 < 6:
                    fold(n + 1)
                norm(n, name, c0)

            def head_norm(name, c0, gain, gate):
                w = slice(c0, T)
                for hd in range(HEADS):
                    dve.wait_ge(sem(f"{name}_hmean_done"), hd + 1)
                    nc.vector.tensor_tensor(hs[:, hd, w], hs[:, hd, w], banks[hd][:, w], ALU.subtract).then_inc(sem(f"{name}_hc_ready"), 1)
                for hd in range(HEADS):
                    dve.wait_ge(sem(f"{name}_hvar_done"), hd + 1)
                    nc.vector.tensor_scalar(hvar[:, hd, w], banks[hd][:, w], EPS, None, ALU.add).then_inc(sem(f"{name}_hvar_ready"), 1)
                dve.wait_ge(sem(f"{name}_hstd_ready"), 1)
                for hd in range(HEADS):
                    link(nc.vector.reciprocal(hvar[:, hd, w], hvar[:, hd, w]))
                    link(nc.vector.tensor_tensor(hs[:, hd, w], hs[:, hd, w], hvar[:, hd, w], ALU.mult))
                    nc.vector.scalar_tensor_tensor(y[:, HEADS + hd, w], hs[:, hd, w], gain[:, hd:hd + 1], gate[:, hd, :],
                                                   ALU.mult, ALU.mult).then_inc(sem(f"{name}_y1"), 1)

            def out_residual(n, name, slot_pair, c0):
                for d in range(KT):
                    k = slot_pair[d // 4]
                    if d % 4 == 3:
                        slot_done[k] += 1
                        dve.wait_ge(used[k], slot_done[k])
                    else:
                        dve.wait_ge(sem(f"{name}_out_done"), 3 * (d // 4) + d % 4 + 1)
                    if d == 0:
                        dve.wait_ge(sem("h_ready"), before("h_ready", stages[n - 1]) + KT)
                    residual(n, name, d, out_bank[d % 2], c0)

            def even():
                slot_done[:] = uses_before("even")
                for k, _, _, _ in EVEN_LOADS[:-2]:
                    slot_done[k] += 1
                dve.wait_ge(sem("even_params_in"), 16 * 8)
                two = lambda v: v.rearrange("p (s n) -> p s n", s=2)
                for hd in range(HEADS):
                    dve.wait_ge(sem("even_proj_read"), hd + 1)
                    x_, o_ = two(xm[:, hd % 2, :]), two(xc[:, hd, :])
                    link(nc.vector.tensor_scalar(xc[:, hd, :], xm[:, hd % 2, :], conv_w[:, hd, 2:3], conv_b[:, hd:hd + 1], ALU.mult, ALU.add))
                    for j in (0, 1, 3, 4):
                        sh = j - CONV // 2
                        a, b = max(0, -sh), CTX - max(0, sh)
                        ins = nc.vector.scalar_tensor_tensor(o_[:, :, a:b], x_[:, :, a + sh:b + sh], conv_w[:, hd, j:j + 1],
                                                             o_[:, :, a:b], ALU.mult, ALU.add)
                        if j == CONV - 1:
                            ins.then_inc(sem("even_conv_done"), 1)
                        else:
                            link(ins)
                dve.wait_ge(sem("even_rows_ready"), 4)
                link(nc.vector.tensor_scalar(rows[:, 6:8, :], rows[:, 2:4, :], -1.0, None, ALU.mult))
                nc.vector.tensor_tensor(rows[:, 6:8, :], rows[:, 6:8, :], rows[:, 2:4, :], ALU.min).then_inc(sem("even_nabs_ready"), 1)
                dve.wait_ge(sem("even_soft"), 2)
                link(nc.vector.scalar_tensor_tensor(rows[:, 2:4, :], rows[:, 2:4, :], 0.0, rows[:, 6:8, :], ALU.min, ALU.subtract))
                one = lambda n: ones_w[0:HEADS, 0:1].to_broadcast([HEADS, n])

                def scans(dst, src, op):
                    nc.vector.tensor_tensor_scan(rows[:, dst, :], one(T), rows[:, src, :], 0.0, ALU.mult, op)
                    link(nc.vector.tensor_tensor_scan(rows[:, dst + 1, 0:CTX][:, ::-1], one(CTX), rows[:, src + 1, 0:CTX][:, ::-1], 0.0, ALU.mult, op))
                    link(nc.vector.tensor_tensor_scan(rows[:, dst + 1, CTX:T][:, ::-1], one(LAT), rows[:, src + 1, CTX:T][:, ::-1],
                                                      rows[:, dst + 1, 0:1], ALU.mult, op))

                scans(4, 2, ALU.add)
                nc.vector.tensor_tensor(rows[:, 0:2, :], rows[:, 0:2, :], rows[:, 4:6, :], ALU.subtract).then_inc(sem("even_a_ready"), 1)
                dve.wait_ge(sem("even_a_ready"), 1)
                scans(6, 0, ALU.max)
                link(nc.vector.tensor_tensor(rows[:, 2:4, :], rows[:, 4:6, :], rows[:, 6:8, :], ALU.add))
                nc.vector.tensor_scalar(rows[:, 2:4, :], rows[:, 2:4, :], -1.0, EXP_MAX, ALU.mult, ALU.min).then_inc(sem("even_bm_ready"), 1)
                nc.vector.tensor_scalar(rows[:, 4:6, :], rows[:, 6:8, :], -1.0, None, ALU.mult).then_inc(sem("even_negm_ready"), 1)

                dve.wait_ge(sem("na_bias_masked"), 8)

                def maxima(u):
                    hp, st, hh, qt = UNITS[u]
                    dve.wait_ge(sem("na_scores_done"), u + 1)
                    neg = col[:, u % 2:u % 2 + 1]
                    if u >= 2:
                        dve.wait_ge(sem("na_pT_done"), u - 1)
                    if st == 0:
                        nc.vector.tensor_reduce(neg, banks[u % 2][:, 0:CTX], AX.X, ALU.max, negate=True).then_inc(sem("na_max_ready"), 1)
                    else:
                        nc.vector.tensor_copy(probs[:, u % 2, 0:CTX], banks[u % 2][:, 0:CTX])
                        link(nc.vector.tensor_tensor(probs[:, u % 2, CTX:T], banks[u % 2][:, CTX:T], na_bias[:, qt, 2 * hp + hh, :], ALU.add))
                        nc.vector.tensor_reduce(neg, probs[:, u % 2, :], AX.X, ALU.max, negate=True).then_inc(sem("na_max_ready"), 1)

                maxima(0)
                for u, (hp, st, hh, qt) in enumerate(UNITS):
                    if u + 1 < len(UNITS):
                        maxima(u + 1)
                    keys = CTX if st == 0 else T
                    dve.wait_ge(sem("na_exp_done"), u + 1)
                    rec = col[:, 4 + u % 2:5 + u % 2]
                    nc.vector.reciprocal(rec, col[:, 2 + u % 2:3 + u % 2]).then_inc(sem("na_scores_read"), 1)
                    dve.wait_ge(sem("na_scores_read"), u + 1)
                    nc.vector.tensor_scalar(probs[:, u % 2, 0:keys], probs[:, u % 2, 0:keys], rec, None, ALU.mult).then_inc(sem("na_probs_ready"), 1)
                    if hh == 0 and qt == 0 and u:
                        attention_out(u // 4 - 1)
                attention_out(7)

                dve.wait_ge(sem("even_acol_ready"), 1)
                for hd in range(HEADS):
                    for way in range(2):
                        v = 2 * hd + way
                        dve.wait_ge(sem("ml_negm_done"), v + 1)
                        for n in ORDER[way]:
                            a, b = TARGETS[way][n][0][0], TARGETS[way][n][-1][1]
                            nc.vector.tensor_scalar(decay[way][:, n, a:b], banks[3][:, a:b], acol[:, way, n, hd:hd + 1], 0.0,
                                                    ALU.add, ALU.min).then_inc(sem("ml_arg_ready"), 1)
                        dve.wait_ge(sem("ml_scores_done"), hd + 1)
                        for k, n in enumerate(ORDER[way]):
                            dve.wait_ge(sem("ml_masked"), TT * v + k + 1)
                            for a, b in TARGETS[way][n]:
                                last = nc.vector.tensor_tensor(decay[way][:, n, a:b], decay[way][:, n, a:b], qk_cols(n, a, b), ALU.mult)
                            last.then_inc(sem("ml_s_ready"), 1)
                        dve.wait_ge(sem("ml_numden_done"), v + 1)
                        dve.wait_ge(sem("ml_em_read"), v + 1)
                        link(nc.vector.scalar_tensor_tensor(em_b[:, way, :], banks[5][:, :], -1.0, em_b[:, way, :], ALU.mult, ALU.max))
                        link(nc.vector.tensor_tensor(em_b[:, way, :], banks[5][:, :], em_b[:, way, :], ALU.max))
                        link(nc.vector.reciprocal(quot[:, way, :], em_b[:, way, :]))
                        dst = hs[:, hd, :] if way == 0 else quot[:, 1, :]
                        nc.vector.tensor_tensor(dst, banks[4][:, :], quot[:, way, :], ALU.mult).then_inc(sem("ml_quot_ready"), 1)
                    dve.wait_ge(sem("ml_quot_ready"), 2 * hd + 2)
                    ins = nc.vector.tensor_tensor(hs[:, hd, :], hs[:, hd, :], quot[:, 1, :], ALU.add)
                    ins.then_inc(sem("even_hs_all") if hd == HEADS - 1 else sem("ml_hsum_ready"), 1)
                head_norm("even", 0, ml_gn, sig_o)
                out_residual(1, "even", (0, 1), 0)
                fold(2)
                norm(1, "even", 0)

            def attention_out(group):
                hp, st = group // 2, group % 2
                a, b = STREAMS[st]
                dve.wait_ge(sem("na_out_done"), 2 * group + 2)
                nc.vector.tensor_copy(y[:, hp, a:b], banks[4 + group % 2][:, 0:CTX]).then_inc(sem("even_y0"), 1)

            nc.vector.memset(ones_w[:, :], 1.0).then_inc(sem("mean_w_ready"), 1)
            nc.vector.memset(hmean_w[:, :], 1.0 / HDIM).then_inc(sem("mean_w_ready"), 1)
            def odd():
                slot_done[:] = uses_before("odd")
                for k, _, _, _ in ODD_LOADS[:-2]:
                    slot_done[k] += 1
                both = lambda v: v.rearrange("p (s n) -> p s n", s=2)
                over = lambda v: v.unsqueeze(1).to_broadcast([P, 2, CTX])

                def rotate_in(u):
                    dve.wait_ge(sem(f"table_in{u % TABLE_RING}"), 16 * (u // TABLE_RING + 1))
                    dve.wait_ge(sem("s5_in_done"), u + 1)
                    if u >= 2:
                        dve.wait_ge(sem("s5_w_ready"), 2 * (u - 1))
                        dve.wait_ge(sem("s5_z_ready"), u - 1)
                    cos, sin = (over(tables[:, u % TABLE_RING, c, :]) for c in range(2))
                    re_, im_ = (both(banks[2 * (u % 2) + r][:, :]) for r in range(2))
                    for n, (a, b) in enumerate(((cos, re_), (sin, im_), (cos, im_), (sin, re_))):
                        last = nc.vector.tensor_tensor(both(prods[:, u % 2, n, :]), b, a, ALU.mult)
                    last.then_inc(sem("s5_prod_done"), 1)

                def scan(u):
                    st, way = UNITS5[u]
                    dve.wait_ge(sem("s5_w_ready"), 2 * (u + 1))
                    if u >= 2:
                        dve.wait_ge(sem("s5_x_ready"), u - 1)
                    at = way * S5_TILES + st
                    mag = s5_mag[:, at:at + 1].to_broadcast([P, CTX])
                    end = CTX - 1 if way == 0 else 0
                    order = (lambda v: v) if way == 0 else (lambda v: v[:, ::-1])
                    z = [s5_z[:, u % 2, r, :] for r in range(2)]
                    w = [prods[:, u % 2, 2 * r, :] for r in range(2)]
                    nc.vector.tensor_tensor_scan(order(z[0][:, 0:CTX]), mag, order(w[0][:, 0:CTX]), 0.0, ALU.mult, ALU.add)
                    link(nc.vector.tensor_tensor_scan(order(z[1][:, 0:CTX]), mag, order(w[1][:, 0:CTX]), 0.0, ALU.mult, ALU.add))
                    cos, sin = (tables[:, u % TABLE_RING, c, end:end + 1] for c in range(2))
                    zr, zi = (z[r][:, end:end + 1] for r in range(2))
                    nc.vector.tensor_tensor(s5_init[:, 2:3], zi, sin, ALU.mult)
                    link(nc.vector.tensor_tensor(s5_init[:, 3:4], zr, sin, ALU.mult))
                    nc.vector.scalar_tensor_tensor(s5_init[:, 0:1], zr, cos, s5_init[:, 2:3], ALU.mult, ALU.subtract)
                    link(nc.vector.scalar_tensor_tensor(s5_init[:, 1:2], zi, cos, s5_init[:, 3:4], ALU.mult, ALU.add))
                    for r in range(2):
                        last = nc.vector.tensor_tensor_scan(order(z[r][:, CTX:T]), mag, order(w[r][:, CTX:T]), s5_init[:, r:r + 1], ALU.mult, ALU.add)
                    last.then_inc(sem("s5_z_ready"), 1)

                def skip(k):
                    dve.wait_ge(sem("s5_y_done"), 8 * (k + 1))
                    nc.vector.scalar_tensor_tensor(s5_u[:, k, CTX:T], s5_u[:, k, CTX:T], s5_d[:, k:k + 1],
                                                   banks[4 + k // 2][:, LAT * (k % 2):LAT * (k % 2 + 1)], ALU.mult, ALU.add).then_inc(sem("s5_skip_ready"), 1)

                dve.wait_ge(sem("odd_params_in"), 16 * 7)
                rotate_in(0)
                for u in range(len(UNITS5)):
                    if u + 1 < len(UNITS5):
                        rotate_in(u + 1)
                    scan(u)
                for n in range(4):
                    x = ret_q[:, 2 * n:2 * n + 2, :] if n < 2 else ret_k[:, 2 * n - 4:2 * n - 2, CTX:T]
                    dve.wait_ge(sem("rope_done"), n + 1)
                    if n == 0:
                        dve.wait_ge(sem("s5_x_ready"), len(UNITS5))
                    table = lambda c: rope[:, c, :].unsqueeze(1).to_broadcast([P, 2, LAT])
                    link(nc.vector.tensor_tensor(rope_tmp, banks[n][:, :].rearrange("p (a b) -> p a b", b=LAT), table(1), ALU.mult))
                    link(nc.vector.tensor_tensor(x, x, table(0), ALU.mult))
                    nc.vector.tensor_tensor(x, x, rope_tmp, ALU.add).then_inc(sem("rope_ready"), 1)
                    dve.wait_ge(sem("rope_ready"), n + 1)
                for k in range(4):
                    skip(k)
                for d in range(4):
                    dve.wait_ge(sem("glu_read"), d + 1)
                    nc.vector.tensor_tensor(y[:, d, CTX:T], s5_u[:, d, CTX:T], glu_sig[:, d, :], ALU.mult).then_inc(sem("odd_y0"), 1)
                for hd in range(HEADS):
                    dve.wait_ge(sem("ret_scores_done"), hd + 1)
                    dve.wait_ge(sem("ret_decay_ready"), 2 * (hd + 1))
                    if hd >= 2:
                        dve.wait_ge(sem("ret_out_done"), hd - 1)
                    for way, n, a, b in RET_PARTS:
                        off = decay_at(way, n)
                        nc.vector.tensor_tensor(ret_s[:, (2 * hd + way) % 4, n, a:b],
                                                banks[2 * (hd % 2) + n // 2][:, LAT * (n % 2) + a:LAT * (n % 2) + b],
                                                ret_decay[:, 2 * hd + way, off + a:off + b], ALU.mult).then_inc(sem("ret_s_ready"), 1)
                    if hd:
                        ret_read(hd - 1)
                ret_read(HEADS - 1)
                head_norm("odd", CTX, ret_gn, ret_gate)
                out_residual(4, "odd", (2, 3), CTX)
                fold(5)
                norm(4, "odd", CTX)

            def ret_read(hd):
                dve.wait_ge(sem("ret_out_done"), hd + 1)
                nc.vector.tensor_copy(hs[:, hd, CTX:T], banks[4 + hd % 2][:, 0:LAT]).then_inc(sem("odd_hs_all") if hd == HEADS - 1 else sem("ret_hs_ready"), 1)

            for s in range(4):
                ffn(s)
                if s == 0:
                    even()
                if s == 2:
                    odd()

        @block.gpsimd
        def _(pool):
            def sums(name, c0):
                w = slice(c0, T)
                chain = 0
                for d in range(KT):
                    if name == "ffn2":
                        for u in range(4 * d, 4 * d + 4):
                            cosines(u)
                    pool.wait_ge(sem("r_ready"), before("r_ready", name) + d + 1)
                    if d == 0:
                        nc.gpsimd.tensor_copy(rsum[:, w], h[:, 0, w]).then_inc(sem("sums"), 1)
                    else:
                        nc.gpsimd.tensor_tensor(rsum[:, w], rsum[:, w], h[:, d, w], ALU.add).then_inc(sem("sums"), 1)
                    pool.wait_ge(sem("sq"), before("sq", name) + d + 1)
                    if d == 0:
                        nc.gpsimd.tensor_copy(rsq[:, w], sq[:, 0, w]).then_inc(sem("sums"), 1)
                    else:
                        nc.gpsimd.tensor_tensor(rsq[:, w], rsq[:, w], sq[:, d % 2, w], ALU.add).then_inc(sem("sums"), 1)
                    pool.wait_ge(sem("sums"), before("sums", name) + 2 * d + 2)

            def gains(n, name, c0):
                for d in range(KT):
                    if n + 1 < 6:
                        pool.wait_ge(sem("m_ready"), before("m_ready", stages[n + 1]) + d + 1)
                    else:
                        pool.wait_ge(sem("z"), before("z", name) + d + 1)
                    nc.gpsimd.tensor_scalar(h[:, d, c0:T], h[:, d, c0:T], lng[:, n, d:d + 1], lnb[:, n, d:d + 1],
                                            ALU.mult, ALU.add).then_inc(sem("h_ready"), 1)

            def causal(buf, way):
                sign = 1 if way == 0 else -1
                return nc.gpsimd.affine_select(out=buf, in_=buf, pattern=[[sign, P]], compare_op=ALU.is_ge, fill=0.0,
                                               base=0, channel_multiplier=-sign)

            def even():
                for hd in range(HEADS):
                    for way in range(2):
                        v = 2 * hd + way
                        for k, n in enumerate(ORDER[way]):
                            pool.wait_ge(sem("ml_exp_done"), TT * v + k + 1)
                            causal(decay[way][:, n, n * P:(n + 1) * P], way).then_inc(sem("ml_masked"), 1)
                sums("even", 0)
                gains(1, "even", 0)

            def odd():
                pool.wait_ge(sem("s5_e_ready"), 2)
                pool.wait_ge(sem("odd_params_in"), 16 * 7)
                e = [s5_e[:, r, :].unsqueeze(2).to_broadcast([P, 2 * S5_TILES, PAIR]) for r in range(2)]
                tmp = view(slots[4], 0, 2, 2 * S5_TILES, PAIR)
                nc.gpsimd.tensor_tensor(c_fold[:, 0, :, :], c_raw[:, 0, :, :], e[0], ALU.mult).then_inc(sem("c_steps"), 1)
                nc.gpsimd.tensor_tensor(tmp[:, 0, :, :], c_raw[:, 1, :, :], e[1], ALU.mult).then_inc(sem("c_steps"), 1)
                nc.gpsimd.tensor_tensor(c_fold[:, 1, :, :], c_raw[:, 0, :, :], e[1], ALU.mult).then_inc(sem("c_steps"), 1)
                nc.gpsimd.tensor_tensor(tmp[:, 1, :, :], c_raw[:, 1, :, :], e[0], ALU.mult).then_inc(sem("c_steps"), 1)
                pool.wait_ge(sem("c_steps"), 4)
                nc.gpsimd.tensor_tensor(c_fold[:, 0, :, :], c_fold[:, 0, :, :], tmp[:, 0, :, :], ALU.subtract).then_inc(sem("c_steps"), 1)
                nc.gpsimd.tensor_tensor(c_fold[:, 1, :, :], c_fold[:, 1, :, :], tmp[:, 1, :, :], ALU.add).then_inc(sem("c_steps"), 1)
                pool.wait_ge(sem("c_steps"), 6)
                nc.gpsimd.tensor_scalar(c_fold[:, 1, :, :], c_fold[:, 1, :, :], -1.0, None, ALU.mult).then_inc(sem("s5_c_ready"), 1)

                def weigh(u):
                    pool.wait_ge(sem("s5_prod_done"), u + 1)
                    p_ = prods[:, u % 2, :, :]
                    nc.gpsimd.tensor_tensor(p_[:, 0, :], p_[:, 0, :], p_[:, 1, :], ALU.add).then_inc(sem("s5_w_ready"), 1)
                    nc.gpsimd.tensor_tensor(p_[:, 2, :], p_[:, 2, :], p_[:, 3, :], ALU.subtract).then_inc(sem("s5_w_ready"), 1)

                def states(u):
                    pool.wait_ge(sem("s5_z_ready"), u + 1)
                    if u:
                        pool.wait_ge(sem("s5_x_ready"), u)
                    if u >= 2:
                        pool.wait_ge(sem("s5_y_done"), u - 1)
                    cos, sin = (tables[:, u % TABLE_RING, c, :] for c in range(2))
                    zr, zi = (s5_z[:, u % 2, r, CTX:T] for r in range(2))
                    for n, (a, b) in enumerate(((cos, zr), (sin, zi), (sin, zr), (cos, zi))):
                        nc.gpsimd.tensor_tensor(s5_q[:, n, :], a, b, ALU.mult).then_inc(sem("s5_q_done"), 1)
                    pool.wait_ge(sem("s5_q_done"), 4 * (u + 1))
                    nc.gpsimd.tensor_tensor(s5_x[:, u % 2, 0, :], s5_q[:, 0, :], s5_q[:, 1, :], ALU.subtract)
                    nc.gpsimd.tensor_tensor(s5_x[:, u % 2, 1, :], s5_q[:, 2, :], s5_q[:, 3, :], ALU.add).then_inc(sem("s5_x_ready"), 1)

                weigh(0)
                for u in range(len(UNITS5)):
                    if u + 1 < len(UNITS5):
                        weigh(u + 1)
                    states(u)
                pool.wait_ge(sem("s5_x_ready"), len(UNITS5))
                for way, (base, step) in enumerate(((0, 1), (3 * P, -1))):
                    nc.gpsimd.iota(rel[:, way, :], pattern=[[step, T]], base=base, channel_multiplier=-step,
                                   allow_small_or_imprecise_dtypes=True).then_inc(sem("rel_made"), 1)
                pool.wait_ge(sem("rel_made"), 2)
                for way in range(2):
                    nc.gpsimd.tensor_scalar(rel[:, way, :], rel[:, way, :], 0.0, None, ALU.max).then_inc(sem("rel_ready"), 1)
                for hd in range(HEADS):
                    for way in range(2):
                        n = 2 * hd + way
                        pool.wait_ge(sem("ret_decay_exp"), n + 1)
                        at = 0 if way == 0 else T - P
                        causal(ret_decay[:, n, at:at + P], way).then_inc(sem("ret_decay_ready"), 1)
                sums("odd", CTX)
                gains(4, "odd", CTX)

            def cosines(u):
                half = phase[:, u % 2, 2, :]
                pool.wait_ge(sem("phase_half"), u + 1)
                nc.gpsimd.tensor_tensor(half, half, half, ALU.mult).then_inc(sem("half_squared"), 1)
                pool.wait_ge(sem("half_squared"), u + 1)
                nc.gpsimd.tensor_scalar(tables_out[:, u % 4, 0, :], half, -2.0, 1.0, ALU.mult, ALU.add).then_inc(sem("table_cos_ready"), 1)

            for s in range(4):
                n = [0, 2, 3, 5][s]
                c0 = CTX if s == 3 else 0
                sums(f"ffn{s}", c0)
                gains(n, f"ffn{s}", CTX if n >= 3 else 0)
                if s == 0:
                    even()
                if s == 2:
                    odd()


def _tiles(w):
    k, n = w.shape
    return w.reshape(k // P, P, n // P, P).transpose(2, 1, 0, 3)


def _rows(w):
    k, n = w.shape
    return w.reshape(k // P, P, n).transpose(1, 0, 2)


def _cols(v):
    v = v.reshape(v.shape[:-1] + (v.shape[-1] // P, P))
    return np.moveaxis(v, -1, 0)


def _feature_major(x):
    return x.T.reshape(-1, P, x.shape[0]).transpose(1, 0, 2)


def _layout(v):
    c = np.ascontiguousarray
    x, ctx = v["x"][0], v["ctx"][0]
    a = {}
    a["x"] = c(np.concatenate([_feature_major(ctx), _feature_major(x)], axis=2))
    a["cvec"] = c(np.broadcast_to(np.stack([v["c_ctx"], v["c"][0]]), (P, 2, D)))
    a["ada"] = c(np.stack([w.T.reshape(MODG, 4, P, D).transpose(0, 2, 1, 3) for w in v["ada_w"]]).reshape(LAYERS * MODG, P, SLOT))
    a["modb"] = c(np.repeat(_cols(v["ada_b"])[..., None], 2, axis=-1))
    a["lng"] = c(_cols(v["ln_g"]).reshape(P, 6, KT))
    a["lnb"] = c(_cols(v["ln_b"]).reshape(P, 6, KT))
    gate, up, down = v["ffn_w_gate"], v["ffn_w_up"], v["ffn_w_down"]
    a["gateup"] = c(np.stack([
        np.stack([_tiles(gate[l, s]), _tiles(up[l, s])], axis=1).reshape(PAIRS, 4, P, KT * P).transpose(0, 2, 1, 3)
        for l in range(LAYERS) for s in range(2)]).reshape(4, PAIRS, P, SLOT))
    a["down"] = c(np.stack([_tiles(down[l, s]).reshape(KT, P, FT * P) for l in range(LAYERS) for s in range(2)]))
    w = v["ev_w_in"][0]
    naq, nak, nav, xm, mv, zo, zg = (w[:, a:b] for a, b in ((0, 512), (512, 1024), (1024, 1536), (1536, 2048), (2048, 2560),
                                                           (2560, 3072), (3072, 3088)))
    slot = lambda t: t.transpose(1, 0, 2, 3).reshape(P, SLOT)
    a["ev_in"] = c(np.stack([slot(_tiles(u)) for u in (xm, zo, naq, nak)]))
    a["ev_v"] = c(np.stack([_rows(u).reshape(P, SLOT) for u in (nav, mv)]))
    a["ev_gates"] = c(_rows(zg).reshape(P, KT * 16))
    a["ev_out"] = c(np.stack([slot(u) for u in _tiles(v["ev_w_out"][0]).reshape(2, 4, P, KT, P)]))
    a["ml_qk"] = c(np.concatenate([v["ml_wq"][0], v["ml_wk"][0]]).transpose(1, 0, 2).reshape(P, 2 * WIDTH))
    a["rpb"] = c(v["na_rpb"][0].reshape(-1))
    a["conv_w"] = c(np.moveaxis(_cols(v["ml_conv_w"][0]), 1, 2))
    a["conv_b"] = c(_cols(v["ml_conv_b"][0]))
    a["gate_b"] = c(np.concatenate([v["ml_i_bias"][0], v["ml_f_bias"][0]]).T)
    a["ml_gn"] = c(_cols(v["ml_gn_w"][0]))
    a["ident"] = np.eye(P, dtype=np.float32)
    a["flip"] = np.ascontiguousarray(a["ident"][::-1])
    a["head_sel"] = np.repeat(np.eye(HEADS, dtype=np.float32)[:, :, None], P, axis=2)
    q, k = np.arange(GRID_W)[:, None], np.arange(GRID_W)[None, :]
    first = np.clip(q - WIN_W // 2, 0, GRID_W - WIN_W)
    a["na_mask"] = np.tile(np.where((k >= first) & (k < first + WIN_W), 0.0, -1e30).astype(np.float32), (2, 1))
    w = v["od_w_in"][0]
    su, rq, rk, rv, rg = (w[:, n * 512:(n + 1) * 512] for n in range(5))
    a["od_in"] = c(np.stack([slot(_tiles(u)) for u in (su, rk, rq, rg)]))
    a["od_v"] = c(_rows(rv).reshape(P, SLOT))
    a["od_out"] = c(np.stack([slot(u) for u in _tiles(v["od_w_out"][0]).reshape(2, 4, P, KT, P)]))
    a["glu"] = c(_rows(v["s5_glu_w"][0]).reshape(P, HEADS * WIDTH))
    a["glu_b"] = c(_cols(v["s5_glu_b"][0]))
    a["s5_d"] = c(_cols(v["s5_d"][0].reshape(-1)))
    a["ret_gn"] = c(_cols(v["ret_gn_w"][0]))
    a["decay_logit"] = c(np.broadcast_to(v["ret_decay_logit"][0], (P, 2, HEADS)))
    states = lambda t: t.reshape(2 * S5_TILES, P).T
    log_dt = np.repeat(v["s5_log_dt"][0], S5_STATE, axis=1)
    a["s5_par"] = c(np.stack([states(v["s5_lam_re"][0]), states(v["s5_lam_im"][0]), states(log_dt)], axis=1))
    b_ = np.stack([v["s5_b_re"][0], v["s5_b_im"][0]]).reshape(2, 2, 4, 4, 2, S5_STATE, S5_GROUP)
    blocks = np.zeros((4, 2, S5_GROUP, 2, 2, 4, 2, S5_STATE), np.float32)
    c_ = np.stack([v["s5_c_re"][0], v["s5_c_im"][0]]).reshape(2, 2, S5_TILES, 2, S5_GROUP, S5_STATE)
    cblocks = np.zeros((2, S5_STATE, 2, 2, S5_TILES, 2, S5_GROUP), np.float32)
    for n in range(2):
        blocks[:, n, :, :, :, :, n, :] = b_[:, :, :, :, n].transpose(3, 5, 0, 1, 2, 4)
        cblocks[n, :, :, :, :, n, :] = c_[:, :, :, n].transpose(4, 0, 1, 2, 3)
    a["s5_b"] = c(blocks.reshape(P, 2, 8, P))
    a["s5_c"] = c(cblocks.reshape(P, 2, 2 * S5_TILES, PAIR))
    n = np.arange(1, CTX + 1, dtype=np.float32)
    a["steps"] = c(np.broadcast_to(np.stack([n, n[::-1]]), (P, 2, CTX)))
    f = np.arange(P)
    t = np.arange(LAT)
    pos = np.where(f[:, None] < P // 2, (t // GRID_W)[None, :], (t % GRID_W)[None, :]).astype(np.float32)
    freq = (np.float32(10000.0) ** (-(np.arange(P // 4, dtype=np.float32)) / np.float32(P // 4)))[f % (P // 4)]
    ang = (pos * freq[:, None]).astype(np.float64)
    sign = np.where(f % (P // 2) < P // 4, -1.0, 1.0)[:, None]
    a["rope"] = c(np.stack([np.cos(ang), np.sin(ang) * sign], axis=1).astype(np.float32))
    swap = np.zeros((P, P), np.float32)
    swap[f ^ (P // 4), f] = 1.0
    a["rope_swap"] = swap
    return a


def kernel(**inputs):
    import concourse.bacc as bacc
    from concourse.bass_utils import run_bass_kernel_spmd

    v = {name: np.asarray(a) for name, a in inputs.items()}
    nc = bacc.Bacc("TRN2", target_bir_lowering=False, num_devices=1)
    arrays, args = {}, {}
    for name, a in _layout(v).items():
        arrays[f"in_{name}_dram"] = a
        args[name] = nc.dram_tensor(f"in_{name}_dram", a.shape, mybir.dt.from_np(a.dtype), kind="ExternalInput").ap()
    out = nc.dram_tensor("out_dram", (P, KT, LAT), F32, kind="ExternalOutput").ap()
    build(nc, args, out)
    r = run_bass_kernel_spmd(nc, [arrays], core_ids=[0]).results[0]["out_dram"]
    return np.ascontiguousarray(r.transpose(2, 1, 0).reshape(1, LAT, D))
```

```python
import contextlib
import math

import numpy as np

import concourse.bass as bass
from concourse import mybir

F32 = mybir.dt.float32
F32R = mybir.dt.float32r
ALU = mybir.AluOpType
ACT = mybir.ActivationFunctionType
AX = mybir.AxisListType

P = 128
D = 1024
KT = D // P
CTX, LAT = 256, 256
T = CTX + LAT
TT = T // P
FF = 2816
FT = FF // P
HALF = FT // 2
PAIRS = FT // 2
LAYERS = 2
MODT = 9 * KT
MODG = MODT // 4
ALPHA = (2.0 * LAYERS) ** 0.25
EPS = 1e-5
SLOT = 4 * KT * P
STREAMS = ((0, CTX), (CTX, T))
ADA_IN = {"ffn0": (4, 12), "ffn1": (16, 12), "ffn2": (28, 8), "ffn3": (36, 0)}


GRID_W = 64
NA_HEADS, NA_DIM = 8, 64
WIN_W = 16
RPB_H, RPB_W = 15, 31
ROWS = LAT // GRID_W
HEADS, HDIM = 4, P
WIDTH = HEADS * HDIM
CONV = 5
EXP_MAX = 85.0

EVEN_LOADS = [(0, "ev_in", 0, SLOT), (1, "ev_gates", None, KT * 4 * HEADS), (2, "ev_in", 1, SLOT), (3, "ev_in", 2, SLOT),
              (0, "ev_in", 3, SLOT), (1, "ev_v", 0, SLOT), (2, "ev_v", 1, SLOT), (3, "ml_qk", None, 2 * WIDTH),
              (0, "ev_out", 0, SLOT), (1, "ev_out", 1, SLOT)]

S5_STATE, S5_GROUP, S5_GROUPS = 64, 16, 32
S5_TILES = S5_GROUPS * S5_STATE // P
UNITS5 = [(st, way) for st in range(S5_TILES) for way in range(2)]
PAIR = 2 * S5_GROUP
TWO_PI = 2 * math.pi
ROUND = 1.5 * 2.0 ** 23
PI_A = 6.28125
PI_B = float(np.float32(math.floor((TWO_PI - PI_A) * 2 ** 20) / 2 ** 20))
PI_C = float(np.float32(TWO_PI - PI_A - PI_B))
LN2_A = 0.693359375
LN2_B = float(np.float32(math.log(2.0) - LN2_A))
TABLE_RING = 4

ODD_LOADS = [(0, "od_in", 0, SLOT), (1, "od_in", 1, SLOT), (2, "od_v", None, SLOT), (3, "od_in", 2, SLOT),
             (0, "od_in", 3, SLOT), (1, "glu", None, HEADS * WIDTH), (2, "od_out", 0, SLOT), (3, "od_out", 1, SLOT)]


def uses_before(stage):
    n = [0, 2, 2, 0, 0]
    for name in ("ffn0", "even", "ffn1", "ffn2", "odd", "ffn3"):
        if name == stage:
            return n
        if name in ("even", "odd"):
            for load in EVEN_LOADS if name == "even" else ODD_LOADS:
                n[load[0]] += 1
        else:
            ada = ADA_IN[name][1]
            n = [a + b for a, b in zip(n, [PAIRS - PAIRS // 2, PAIRS // 2, ada, KT // 2, KT // 2])]


def pair_use(s, p):
    return uses_before(f"ffn{s}")[p % 2] + p // 2 + 1


def build(nc, i, out, stop=None):
    stack = contextlib.ExitStack()
    with stack:
        def sb(name, shape):
            return stack.enter_context(nc.sbuf_tensor(name, shape, F32))

        sems = {}

        def sem(name):
            if name not in sems:
                sems[name] = stack.enter_context(nc.semaphore(name))
            return sems[name]

        stages = ["ffn0", "even", "ffn1", "ffn2", "odd", "ffn3"]
        PER_STAGE = {"m_ready": KT, "r_ready": KT, "sq": KT, "sums": 2 * KT, "stat": 2, "stat_read": 2, "var": 1, "std": 1,
                     "c": KT, "z": KT, "h_ready": KT}

        def before(name, stage):
            return PER_STAGE[name] * stages.index(stage)

        def placed(name, shape):
            at = nc.sbuf_base
            t = sb(name, shape)
            assert nc.sbuf_base - at == 4 * int(np.prod(shape[1:]))
            return t, at

        h = sb("h", [P, KT, T])
        m, m_at = placed("m", [P, KT, T])
        slots, slots_at = zip(*(placed(f"slot{k}", [P, SLOT]) for k in range(5)))
        R, R_at = placed("R", [P, 17408])

        def rounded(name, at, off, shape):
            return nc.alloc_sbuf_tensor_at(name, shape, F32R, offset=at + 4 * off)

        m_lo = rounded("m_lo", m_at, 0, [P, KT, T])
        m_hi = rounded("m_hi", R_at, FT * T, [P, KT, T])
        w_hi = rounded("w_hi", R_at, FT * T + KT * T, [P, 2, KT, P])
        w_lo = [rounded(f"w{b}_lo", slots_at[b], 0, [P, 4, KT, P]) for b in range(2)]
        down_hi = rounded("down_hi", slots_at[1], 0, [P, 2, HALF, P])
        down_lo = [rounded(f"down{b}_lo", slots_at[3 + b], 0, [P, 2, HALF, P]) for b in range(2)]
        g_lo = rounded("g_lo", R_at, 0, [P, FT, T])
        g_parts = [(0, rounded("g_hi_first", slots_at[1], FT * P, [P, 2, T])), (2, rounded("g_hi_mid", R_at, FT * T, [P, 12, T])),
                   (14, rounded("g_hi_last", m_at, 0, [P, KT, T]))]

        def g_hi(f):
            first, part = [p_ for p_ in g_parts if p_[0] <= f][-1]
            return part[:, f - first, :]

        L = sb("L", [P, 8 * T])
        mods = sb("mods", [P, LAYERS, MODT, 2])
        modb = sb("modb", [P, LAYERS, MODT, 2])
        ada_sum = sb("ada_sum", [P, 4, 2])
        lng = sb("lng", [P, 2 * 3, KT])
        lnb = sb("lnb", [P, 2 * 3, KT])
        mscale = sb("mscale", [P, 6, KT, 2])
        mshift = sb("mshift", [P, 6, KT, 2])
        mgate = sb("mgate", [P, 6, KT, 2])
        mean_w = sb("mean_w", [P, P])
        banks = [stack.enter_context(nc.psum_tensor(f"bank{k}", [P, T], F32)) for k in range(8)]

        ident = sb("ident", [P, P])
        ones_w = sb("ones_w", [P, P])
        hmean_w = sb("hmean_w", [P, P])
        flip = sb("flip", [P, P])
        head_sel = sb("head_sel", [HEADS, HEADS, P])
        na_mask = sb("na_mask", [P, GRID_W])
        conv_w = sb("conv_w", [P, HEADS, CONV])
        conv_b = sb("conv_b", [P, HEADS])
        gate_b = sb("gate_b", [HEADS, 4])
        ml_gn = sb("ml_gn", [P, HEADS])
        acol = sb("acol", [P, 2, TT, HEADS])
        col = sb("col", [P, 8])

        s5_par = sb("s5_par", [P, 3, 2 * S5_TILES])
        s5_mag = sb("s5_mag", [P, 2 * S5_TILES])
        s5_e = sb("s5_e", [P, 2, 2 * S5_TILES])
        log_g = sb("log_g", [P, 2, HEADS])
        s5_d, glu_b, ret_gn = sb("s5_d", [P, 4]), sb("glu_b", [P, 4]), sb("ret_gn", [P, 4])

        def view(buf, off, *shape):
            n = 1
            for s in shape:
                n *= s
            v = buf[:, off:off + n]
            if len(shape) == 2:
                return v.rearrange("p (a b) -> p a b", b=shape[1])
            if len(shape) == 3:
                return v.rearrange("p (a b c) -> p a b c", b=shape[1], c=shape[2])
            return v

        g = view(R, 0, FT, T)
        silu_g = view(L, 0, 2, T)
        sq = view(L, 2 * T, 2, T)
        rsum = view(L, 4 * T, T)
        rsq = view(L, 5 * T, T)
        mean = view(L, 6 * T, T)
        rstd = view(L, 7 * T, T)
        csilu = [slots[3 + s_][:, FT * P:FT * P + D] for s_ in range(2)]
        gate_bank, up_bank, out_bank, stat_bank = banks[0:2], banks[2:4], banks[5:7], banks[7]
        stat2_bank = banks[4]

        full = [sem(f"slot{k}_full") for k in range(5)]
        used = [sem(f"slot{k}_used") for k in range(5)]

        def wslot(k):
            return slots[k][:, :].rearrange("p (t k n) -> p t k n", k=KT, n=P)

        NORMS = [(l, n) for l in range(LAYERS) for n in range(3)]
        xc, sig_o = view(R, 0, HEADS, T), view(R, 2048, HEADS, T)
        ml_v = view(R, 4096, TT, WIDTH)
        na_q, na_k, na_v = view(R, 6144, 4, T), view(R, 8192, 4, T), view(R, 10240, TT, WIDTH)
        xm = view(R, 12288, 2, T)
        na_bias = view(R, 13312, 2, NA_HEADS, LAT)
        bias_flipped = view(slots[2], 0, 2, NA_HEADS, LAT)
        score_banks = [banks[0], banks[1], banks[7]]
        probs = [L[:, 0:T], L[:, T:2 * T], R[:, 12288:12288 + T]]
        probsT = view(L, 2 * T, 2, 4, 2 * P)
        gates_tok = view(L, 6 * T, TT, 16)
        rows = slots[4][0:HEADS, :].rearrange("p (a n) -> p a n", n=T)
        ml_qh, ml_kh = view(R, 6144, 2, T), view(R, 7168, 2, T)
        decay = [view(R, 8192, TT, T), view(R, 10240, TT, T)]
        em_b, quot = view(R, 12288, 2, T), view(R, 13312, 2, T)
        hs = view(R, 14336, HEADS, T)
        hsq, hvar = view(R, 8192, HEADS, T), view(R, 10240, HEADS, T)
        y = m

        TARGETS = [[[(P * n, T)] for n in range(TT)],
                   [[(0, P), (CTX, T)], [(0, T)], [(CTX, CTX + P)], [(CTX, T)]]]
        ORDER = [[0, 1, 2, 3], [1, 0, 3, 2]]
        QK_AT = [(0, 0), (1, 0), (2, 0), (2, 256)]

        def qk_cols(n, a, b):
            bank, off = QK_AT[n]
            lo = 0 if n < 2 else CTX
            return banks[bank][:, off + a - lo:off + b - lo]

        tables_dram = nc.dram_tensor("s5_tables", (len(UNITS5), P, 2 * CTX), F32, kind="Internal").ap()
        small = view(L, 128, 8, 2 * S5_TILES)
        tables_out = view(slots[2], 0, 4, 2, CTX)
        phase = view(slots[2], 2048, 2, 3, CTX)
        steps = view(slots[2], 3584, 2, CTX)
        s5_u = view(R, 0, 4, T)
        ret_k, ret_v = view(R, 2048, HEADS, T), view(R, 4096, TT, WIDTH)
        ret_q, ret_gate = view(R, 6144, HEADS, LAT), view(R, 7168, HEADS, LAT)
        tables = view(R, 8192, TABLE_RING, 2, CTX)
        c_fold = view(R, 10240, 2, 2 * S5_TILES, PAIR)
        c_raw = view(R, 12288, 2, 2 * S5_TILES, PAIR)
        b_raw = R[:, 14336:16384].rearrange("p (r u n) -> p r u n", r=2, n=P)
        rope = view(R, 16384, 2, LAT)
        rope_swap = R[:, 16896:16896 + P]
        prods = view(L, 0, 2, 4, T)
        s5_z = view(slots[4], 0, 2, 2, T)
        s5_x = view(slots[4], 2048, 2, 2, LAT)
        s5_q = view(slots[4], 3072, 4, LAT)
        glu_sig = view(slots[4], 0, 4, LAT)
        rope_tmp = view(slots[4], 1024, 2, LAT)
        s5_init = s5_par[:, 0, 0:4]
        rel = view(R, 8192, 2, T)
        ret_decay = view(L, 0, 8, T)
        ret_s = view(R, 9216, 4, TT, LAT)

        UNITS = [(hp, st, hh, qt) for hp in range(4) for st in range(2) for hh in range(2) for qt in range(2)]

        RET_PARTS = [(0, 0, 0, LAT), (0, 1, 0, LAT), (0, 2, 0, LAT), (0, 3, P, LAT),
                     (1, 0, 0, LAT), (1, 1, 0, LAT), (1, 3, 0, LAT), (1, 2, 0, P)]

        def decay_at(way, n):
            return (LAT - P * n) if way == 0 else (P - P * n if n < 2 else 3 * P - P * (n - 2))

        block = stack.enter_context(nc.Block())

        @block.sync
        def _(sp):
            def load_cvec():
                for s_ in range(2):
                    sp.dma_start(csilu[s_], i["cvec"][:, s_, :]).then_inc(sem("cvec_in"), 16)

            loads = [0] * 5

            def load(k, src, width=SLOT, step=None, it=None, per=0):
                n = loads[k]
                if it is None:
                    if n:
                        sp.wait_ge(used[k], n)
                else:
                    sp.wait_ge(used[k], it * per + n)
                sp.dma_start(slots[k][:, 0:width], src).then_inc(full[k], 16)

            for g_ in range(4):
                if g_ == 2:
                    load(0, i["gateup"][0, 0])
                    loads[0] += 1
                load(1 + g_ % 2, i["ada"][g_])
                loads[1 + g_ % 2] += 1
                if g_ == 3:
                    for dst, src in ((ident[:, :], "ident"), (flip[:, :], "flip"), (head_sel[:, :, :], "head_sel"), (na_mask[:, :], "na_mask"),
                                     (conv_w[:, :, :], "conv_w"), (conv_b[:, :], "conv_b"), (gate_b[:, :], "gate_b"),
                                     (ml_gn[:, :], "ml_gn")):
                        sp.dma_start(dst, i[src]).then_inc(sem("even_params_in"), 16)
                if g_ == 0:
                    load_cvec()
                if g_ == 3:
                    for dst, src in ((s5_par[:, :, :], "s5_par"), (log_g[:, :, :], "decay_logit")):
                        sp.dma_start(dst, i[src]).then_inc(sem("s5_params_in"), 16)
                    for dst, src in ((s5_d[:, :], "s5_d"), (glu_b[:, :], "glu_b"), (ret_gn[:, :], "ret_gn")):
                        sp.dma_start(dst, i[src]).then_inc(sem("odd_params_in"), 16)
                if g_ == 1:
                    sp.dma_start(modb[:, :, :, :], i["modb"]).then_inc(sem("params_in"), 16)
                    sp.dma_start(lng[:, :, :], i["lng"]).then_inc(sem("params_in"), 16)
                    sp.dma_start(lnb[:, :, :], i["lnb"]).then_inc(sem("params_in"), 16)
                    sp.dma_start(h[:, :, :], i["x"]).then_inc(sem("x_in"), 16)

            def ffn_loads(s):
                first, n_ada = ADA_IN[f"ffn{s}"]
                src = i["gateup"][s]

                if s:
                    load(0, src[0])
                    loads[0] += 1
                if s == 1:
                    sp.wait_ge(sem("r_ready"), before("r_ready", f"ffn{s}"))
                    load_cvec()
                if s == 2:
                    sp.wait_ge(sem("r_ready"), before("r_ready", "ffn1") + KT)
                for lo, hi, ada in ((0, n_ada // 2, True), (n_ada // 2, 5, False)):
                    lo, hi = min(lo, 5), min(hi, 5)
                    if hi == lo:
                        continue
                    keep = list(loads)
                    with sp.Fori(0, hi - lo) as it:
                        for b in (1, 0):
                            load(b, src[bass.ds(it * 2 + (2 * lo + 2 - b), 1), :, :].rearrange("a p n -> (a p) n"), it=it, per=1)
                            loads[b] += 1
                            if ada:
                                ada_src = i["ada"][bass.ds(it * 2 + (first + 2 * lo + 1 - b), 1), :, :].rearrange("a p n -> (a p) n")
                                load(2, ada_src, it=it, per=2)
                                loads[2] += 1
                    for k in range(5):
                        loads[k] = keep[k] + (loads[k] - keep[k]) * (hi - lo)
                if n_ada == 12:
                    load(2, i["ada"][first + 10])
                    loads[2] += 1
                for d in range(KT):
                    k = 3 + d % 2
                    if d == 0 and s == 2:
                        sp.wait_ge(used[2], loads[2])
                        sp.dma_start(steps, i["steps"]).then_inc(sem("s5_steps_in"), 16)
                    if d == 5 and s == 0:
                        sp.wait_ge(used[2], loads[2])
                        for qr in range(ROWS):
                            for kr in range(ROWS):
                                at = (kr - qr + RPB_H // 2) * RPB_W + RPB_W // 2 - (GRID_W - 1)
                                src = bass.AP(tensor=i["rpb"].tensor, offset=at, ap=[[1, GRID_W], [RPB_H * RPB_W, NA_HEADS], [1, GRID_W]])
                                p0 = GRID_W * (1 - qr % 2)
                                sp.dma_start(bias_flipped[p0:p0 + GRID_W, qr // 2, :, kr * GRID_W:(kr + 1) * GRID_W], src).then_inc(sem("na_bias_in"), 16)
                    if d == 1 and s in (1, 3):
                        sp.wait_ge(sem("r_ready"), before("r_ready", stages[2 * s - 1 if s == 1 else 4]) + 1)
                    load(k, i["down"][s, d], width=FT * P)
                    loads[k] += 1
                    if d == 1 and n_ada == 12:
                        load(2, i["ada"][first + 11])
                        loads[2] += 1

            for s in range(4):
                ffn_loads(s)
                if s == 0:
                    for n, (k, src, at, width) in enumerate(EVEN_LOADS):
                        if n == 1:
                            sp.wait_ge(sem("r_ready"), before("r_ready", "ffn0") + KT)
                        if n == 2:
                            sp.wait_ge(sem("na_bias_turned"), 8)
                        load(k, i[src] if at is None else i[src][at], width=width)
                        loads[k] += 1
                if s == 2:
                    n_load = [0]

                    def odd_load():
                        k, src, at, width = ODD_LOADS[n_load[0]]
                        n_load[0] += 1
                        load(k, i[src] if at is None else i[src][at], width=width)
                        loads[k] += 1

                    odd_load()
                    sp.wait_ge(sem("r_ready"), before("r_ready", "ffn2") + KT)
                    odd_load()
                    for dst, src in ((rope, "rope"), (rope_swap, "rope_swap"), (c_raw, "s5_c"), (b_raw, "s5_b")):
                        sp.dma_start(dst, i[src]).then_inc(sem("odd_params_in"), 16)
                    for n in range(4):
                        sp.wait_ge(sem(f"table_written{n}"), 16 * (len(UNITS5) // 4))
                    odd_load()
                    odd_load()
                    for u, (st, way) in enumerate(UNITS5):
                        if u == TABLE_RING:
                            odd_load()
                        if u >= TABLE_RING:
                            sp.wait_ge(sem("s5_x_ready"), u - TABLE_RING + 1)
                        sp.dma_start(tables[:, u % TABLE_RING, :, :].rearrange("p a b -> p (a b)"), tables_dram[u]).then_inc(sem(f"table_in{u % TABLE_RING}"), 16)
                        if u in (14, 22, 30):
                            odd_load()
            sp.wait_ge(sem("out_written"), 16 * KT)

        @block.tensor
        def _(pe):
            uses = uses_before("ffn0")

            def take(k, it=None, per=0):
                uses[k] += 1
                if it is None:
                    pe.wait_ge(full[k], 16 * uses[k])
                else:
                    pe.wait_ge(full[k], it * (16 * per) + 16 * uses[k])

            def ffn(s):
                name = f"ffn{s}"
                c0 = CTX if s == 3 else 0
                m_ready, gate_done, up_done = sem("m_ready"), sem("gate_done"), sem("up_done")
                silu_done, g_ready = sem("silu_done"), sem("g_ready")

                def pair(b, n, it):
                    take(b, it, 1)
                    for j in range(2):
                        f = n + j
                        for bank, done, off, freed in ((gate_bank, gate_done, 0, silu_done), (up_bank, up_done, 1, g_ready)):
                            if it is not None:
                                pe.wait_ge(freed, it * 4 + (s * FT + f - 1))
                            elif f >= 2:
                                pe.wait_ge(freed, s * FT + f - 1)
                            unit = s * 2 * FT + 2 * f + off + 1 if it is None else it * 8 + (s * 2 * FT + 2 * f + off + 1)
                            first = f == 0 and off == 0 and it is None
                            pe.wait_ge(sem("w_hi_ready"), unit)
                            for c in range(KT):
                                if first:
                                    pe.wait_ge(m_ready, before("m_ready", name) + c + 1)
                                nc.tensor.matmul(bank[j][:, c0:T], w_hi[:, off, c, :], m_hi[:, c, c0:T], start=(c == 0), stop=False)
                            for c in range(KT):
                                if first:
                                    pe.wait_ge(sem("m_lo_ready"), s * KT + c + 1)
                                nc.tensor.matmul(bank[j][:, c0:T], w_hi[:, off, c, :], m_lo[:, c, c0:T], start=False, stop=False)
                            pe.wait_ge(sem("w_lo_ready"), unit)
                            for c in range(KT):
                                last = nc.tensor.matmul(bank[j][:, c0:T], w_lo[b][:, 2 * j + off, c, :], m_hi[:, c, c0:T],
                                                        start=False, stop=(c == KT - 1))
                            if off == 1 and j == 1:
                                last.then_inc(used[b], 1)
                            else:
                                last.then_inc(done, 1)

                pair(0, 0, None)
                pair(1, 2, None)
                keep = list(uses)
                with pe.Fori(0, PAIRS // 2 - 1) as it:
                    for b in range(2):
                        pair(b, 4 + 2 * b, it)
                for k in range(5):
                    uses[k] = keep[k] + (uses[k] - keep[k]) * (PAIRS // 2 - 1)
                pair(0, FT - 2, None)
                for d in range(KT):
                    k = 3 + d % 2
                    out_d = out_bank[d % 2][:, c0:T]
                    take(k)
                    if d >= 2:
                        pe.wait_ge(sem("r_ready"), before("r_ready", name) + d - 1)
                    for half in range(2):
                        tiles = range(HALF * half, HALF * half + HALF)
                        pe.wait_ge(sem("down_hi_ready"), 2 * KT * s + 2 * d + half + 1)
                        for f in tiles:
                            if d == 0:
                                pe.wait_ge(sem("g_hi_ready"), s * FT + f + 1)
                            nc.tensor.matmul(out_d, down_hi[:, half, f % HALF, :], g_hi(f)[:, c0:T], start=(f == 0), stop=False)
                        for f in tiles:
                            if d == 0:
                                pe.wait_ge(sem("g_lo_ready"), s * FT + f + 1)
                            nc.tensor.matmul(out_d, down_hi[:, half, f % HALF, :], g_lo[:, f, c0:T], start=False, stop=False)
                        pe.wait_ge(sem("down_lo_ready"), 2 * KT * s + 2 * d + half + 1)
                        for f in tiles:
                            last = nc.tensor.matmul(out_d, down_lo[k - 3][:, half, f % HALF, :], g_hi(f)[:, c0:T],
                                                    start=False, stop=(f == FT - 1))
                        last.then_inc(used[k] if half else sem("down_half_done"), 1)
                norm_stats(name, c0)

            def norm_stats(name, c0):
                pe.wait_ge(sem("mean_w_ready"), 3)
                pe.wait_ge(sem("sums"), before("sums", name) + 2 * KT)
                nc.tensor.matmul(stat_bank[:, c0:T], mean_w[:, :], rsum[:, c0:T], start=True, stop=True).then_inc(sem("stat"), 1)
                nc.tensor.matmul(stat2_bank[:, c0:T], mean_w[:, :], rsq[:, c0:T], start=True, stop=True).then_inc(sem("stat"), 1)
                if name != "ffn3":
                    pe.wait_ge(sem("stat_read"), before("stat_read", name) + 2)

            def out_proj(name, slot_pair, c0):
                for d in range(KT):
                    k = slot_pair[d // 4]
                    if d % 4 == 0:
                        take(k)
                    if d >= 2:
                        pe.wait_ge(sem("r_ready"), before("r_ready", name) + d - 1)
                    for c in range(KT):
                        if d == 0:
                            pe.wait_ge(sem(f"{name}_y{c // 4}"), c % 4 + 1 if c >= 4 or name == "odd" else 2 * (c + 1))
                        last = nc.tensor.matmul(out_bank[d % 2][:, c0:T], wslot(k)[:, d % 4, c, :], y[:, c, c0:T],
                                                start=(c == 0), stop=(c == KT - 1))
                    last.then_inc(used[k] if d % 4 == 3 else sem(f"{name}_out_done"), 1)
                norm_stats(name, c0)

            def project(name, at, k, token_major, c0=0):
                take(k)
                for j in range(4):
                    n = at + j
                    if n >= 4:
                        pe.wait_ge(sem(f"{name}_proj_read"), n - 3)
                    for c in range(KT):
                        if at == 0 and j == 0:
                            pe.wait_ge(sem("m_ready"), before("m_ready", name) + c + 1)
                        if token_major:
                            last = nc.tensor.matmul(banks[n % 4][:, :], m[:, c, j * P:(j + 1) * P],
                                                    slots[k][:, c * WIDTH:(c + 1) * WIDTH], start=(c == 0), stop=(c == KT - 1))
                        else:
                            last = nc.tensor.matmul(banks[n % 4][:, c0:T], wslot(k)[:, j, c, :], m[:, c, c0:T],
                                                    start=(c == 0), stop=(c == KT - 1))
                    last.then_inc(used[k] if j == 3 else sem(f"{name}_proj_done"), 1)

            def even():
                uses[:] = uses_before("even")
                pe.wait_ge(sem("even_params_in"), 16 * 8)
                pe.wait_ge(sem("na_bias_in"), 16 * ROWS * ROWS)
                for n in range(8):
                    nc.tensor.matmul(banks[n][:, :], flip[:, :], bias_flipped[:, n // 4, 2 * (n % 4):2 * (n % 4) + 2, :]
                                     .rearrange("p a b -> p (a b)"), start=True, stop=True).then_inc(sem("na_bias_turned"), 1)
                pe.wait_ge(sem("na_bias_masked"), 8)
                project("even", 0, 0, False)
                take(1)
                gw = slots[1][:, 0:KT * 16].rearrange("p (k n) -> p k n", n=16)
                for t in range(TT):
                    for c in range(KT):
                        last = nc.tensor.matmul(banks[4][:, 16 * t:16 * t + 16], m[:, c, t * P:(t + 1) * P], gw[:, c, :],
                                                start=(c == 0), stop=(c == KT - 1))
                last.then_inc(used[1], 1)
                project("even", 4, 2, False)
                pe.wait_ge(sem("even_params_in"), 16 * 8)
                pe.wait_ge(sem("even_gates_read"), 1)
                for kind in range(4):
                    for t in range(TT):
                        last = nc.tensor.transpose(banks[4 + kind][0:HEADS, t * P:(t + 1) * P],
                                                   gates_tok[:, t, 4 * kind:4 * kind + 4], ident[:, :])
                    last.then_inc(sem("even_rows_done"), 1)
                project("even", 8, 3, False)
                project("even", 12, 0, False)
                project("even", 16, 1, True)
                project("even", 20, 2, True)
                pe.wait_ge(sem("even_a_ready"), 1)
                for way in range(2):
                    for t in range(TT):
                        at = (way * TT + t) * HEADS
                        last = nc.tensor.transpose(banks[6][:, at:at + HEADS], rows[:, way, t * P:(t + 1) * P], ident[0:HEADS, 0:HEADS])
                last.then_inc(sem("even_acol_done"), 1)

                def scores(u):
                    hp, st, hh, qt = UNITS[u]
                    r0 = NA_DIM * hh
                    if u == 0:
                        pe.wait_ge(sem("even_proj_read"), 24)
                    if u >= 3:
                        pe.wait_ge(sem("na_scores_read"), u - 2)
                    q0 = STREAMS[st][0] + qt * P
                    keys = CTX if st == 0 else T
                    nc.tensor.matmul(score_banks[u % 3][:, 0:keys], na_q[r0:r0 + NA_DIM, hp, q0:q0 + P],
                                     na_k[r0:r0 + NA_DIM, hp, 0:keys], start=True, stop=True).then_inc(sem("na_scores_done"), 1)

                for u in range(3):
                    scores(u)
                for u, (hp, st, hh, qt) in enumerate(UNITS):
                    tiles = 2 if st == 0 else 4
                    pe.wait_ge(sem("na_probs_ready"), u + 1)
                    if u >= 2:
                        pe.wait_ge(sem("na_pT_ready"), u - 1)
                    for kt in range(tiles):
                        last = nc.tensor.transpose(banks[2 + u % 2][:, kt * P:(kt + 1) * P], probs[u % 3][:, kt * P:(kt + 1) * P], ident[:, :])
                    last.then_inc(sem("na_pT_done"), 1)
                    if u + 3 < len(UNITS):
                        scores(u + 3)
                    if qt == 1:
                        pe.wait_ge(sem("na_pT_ready"), u + 1)
                        group = u // 4
                        if group >= 2 and hh == 0:
                            pe.wait_ge(sem("even_y0"), group - 1)
                        for kt in range(tiles):
                            last = nc.tensor.matmul(banks[4 + group % 2][NA_DIM * hh:NA_DIM * (hh + 1), 0:CTX],
                                                    na_v[:, kt, (2 * hp + hh) * NA_DIM:(2 * hp + hh + 1) * NA_DIM],
                                                    probsT[:, (u // 2) % 2, kt, :], start=(kt == 0), stop=(kt == tiles - 1))
                        last.then_inc(sem("na_out_done"), 1)

                take(3)
                qk_w = slots[3][:, 0:2 * WIDTH].rearrange("p (a n) -> p a n", n=P)
                pe.wait_ge(sem("even_y0"), 8)

                def running_max(v):
                    if v:
                        pe.wait_ge(sem("ml_arg_ready"), TT * v)
                    nc.tensor.matmul(banks[3][:, :], head_sel[:, v // 2, :], rows[:, 4 + v % 2, :], start=True, stop=True).then_inc(sem("ml_negm_done"), 1)

                running_max(0)
                for hd in range(HEADS):
                    for a in range(2):
                        if hd and a == 0:
                            pe.wait_ge(sem("ml_em_read"), 2 * hd)
                        last = nc.tensor.matmul(banks[6 + a][:, :], qk_w[:, a * HEADS + hd, :], xc[:, hd, :], start=True, stop=True)
                        last.then_inc(used[3] if hd == HEADS - 1 and a == 1 else sem("ml_qk_proj_done"), 1)
                    pe.wait_ge(sem("ml_qk_ready"), 2 * (hd + 1))
                    for n in range(TT):
                        lo = 0 if n < 2 else CTX
                        last = nc.tensor.matmul(qk_cols(n, lo, T), ml_kh[:, hd % 2, n * P:(n + 1) * P], ml_qh[:, hd % 2, lo:T],
                                                start=True, stop=True)
                    last.then_inc(sem("ml_scores_done"), 1)
                    for way in range(2):
                        v = 2 * hd + way
                        if v:
                            pe.wait_ge(sem("ml_em_read"), v)
                        nc.tensor.matmul(banks[6][:, :], head_sel[:, hd, :], rows[:, 2 + way, :], start=True, stop=True).then_inc(sem("ml_em_done"), 1)
                        if v + 1 < 2 * HEADS:
                            running_max(v + 1)
                        if v:
                            pe.wait_ge(sem("ml_quot_ready"), v)
                        for k, n in enumerate(ORDER[way]):
                            pe.wait_ge(sem("ml_s_ready"), TT * v + k + 1)
                            for a, b in TARGETS[way][n]:
                                s_ = decay[way][:, n, a:b]
                                end = k == TT - 1 and b == TARGETS[way][n][-1][1]
                                nc.tensor.matmul(banks[4][:, a:b], ml_v[:, n, hd * P:(hd + 1) * P], s_, start=(k == 0), stop=end)
                                last = nc.tensor.matmul(banks[5][:, a:b], ones_w[:, :], s_, start=(k == 0), stop=end)
                        last.then_inc(sem("ml_numden_done"), 1)
                head_norm_stats("even", 0)
                out_proj("even", (0, 1), 0)

            def head_norm_stats(name, c0):
                pe.wait_ge(sem(f"{name}_hs_all"), 1)
                for hd in range(HEADS):
                    nc.tensor.matmul(banks[hd][:, c0:T], hmean_w[:, :], hs[:, hd, c0:T], start=True, stop=True).then_inc(sem(f"{name}_hmean_done"), 1)
                for hd in range(HEADS):
                    pe.wait_ge(sem(f"{name}_hsq_ready"), hd + 1)
                    nc.tensor.matmul(banks[hd][:, c0:T], hmean_w[:, :], hsq[:, hd, c0:T], start=True, stop=True).then_inc(sem(f"{name}_hvar_done"), 1)

            def odd():
                uses[:] = uses_before("odd")
                ring, cnt_ = banks[6:8], [0]

                def proj_tile(j, k, token_major, c0=0, parts=(0, 1)):
                    n = cnt_[0]
                    if 0 in parts:
                        if j == 0:
                            take(k)
                        if n >= 2:
                            pe.wait_ge(sem("odd_proj_read"), n - 1)
                    if 1 in parts:
                        cnt_[0] += 1
                    for c in range(KT // 2 * parts[0], KT // 2 * (parts[-1] + 1)):
                        if n == 0:
                            pe.wait_ge(sem("m_ready"), before("m_ready", "odd") + c + 1)
                        if token_major:
                            last = nc.tensor.matmul(ring[n % 2][:, :], m[:, c, j * P:(j + 1) * P],
                                                    slots[k][:, c * WIDTH:(c + 1) * WIDTH], start=(c == 0), stop=(c == KT - 1))
                        else:
                            last = nc.tensor.matmul(ring[n % 2][:, c0:T], wslot(k)[:, j, c, :], m[:, c, c0:T],
                                                    start=(c == 0), stop=(c == KT - 1))
                    if 1 in parts:
                        last.then_inc(used[k] if j == 3 else sem("odd_proj_done"), 1)

                def inputs(u):
                    st, way = UNITS5[u]
                    k, r0 = st // 4, PAIR * (st % 4)
                    pe.wait_ge(sem("odd_proj_read"), k + 1)
                    if u >= 2:
                        pe.wait_ge(sem("s5_prod_done"), u - 1)
                    for r in range(2):
                        last = nc.tensor.matmul(banks[2 * (u % 2) + r][:, :], b_raw[r0:r0 + PAIR, r, way * 4 + k, :], s5_u[r0:r0 + PAIR, k, :],
                                                start=True, stop=True)
                    last.then_inc(sem("s5_in_done"), 1)

                for j in range(4):
                    proj_tile(j, 0, False)
                pe.wait_ge(sem("odd_params_in"), 16 * 7)
                inputs(0)
                inputs(1)
                tiles = [(j, k, tm, c0) for k, tm, c0 in ((1, False, 0), (2, True, 0), (3, False, CTX), (0, False, CTX)) for j in range(4)]
                pe.wait_ge(sem("s5_c_ready"), 1)
                for u, (st, way) in enumerate(UNITS5):
                    if u + 2 < len(UNITS5):
                        inputs(u + 2)
                    proj_tile(*tiles[u // 2], parts=(u % 2,))
                    pe.wait_ge(sem("s5_x_ready"), u + 1)
                    k, r0 = st // 4, PAIR * (st % 4)
                    for r in range(2):
                        last = nc.tensor.matmul(banks[4 + k // 2][r0:r0 + PAIR, LAT * (k % 2):LAT * (k % 2 + 1)],
                                                c_fold[:, r, way * S5_TILES + st, :], s5_x[:, u % 2, r, :],
                                                start=(way == 0 and r == 0), stop=(way == 1 and r == 1))
                    last.then_inc(sem("s5_y_done"), 1)
                pe.wait_ge(sem("odd_proj_read"), 20)
                for n in range(4):
                    src = ret_q[:, 2 * n:2 * n + 2, :] if n < 2 else ret_k[:, 2 * n - 4:2 * n - 2, CTX:T]
                    nc.tensor.matmul(banks[n][:, :].rearrange("p (a b) -> p a b", b=LAT), rope_swap, src, start=True, stop=True).then_inc(sem("rope_done"), 1)
                take(1)
                pe.wait_ge(sem("s5_act_ready"), 4)
                gw = slots[1][:, 0:4 * WIDTH].rearrange("p (k n) -> p k n", n=WIDTH)
                for d in range(4):
                    if d >= 2:
                        pe.wait_ge(sem("glu_read"), d - 1)
                    for c in range(4):
                        last = nc.tensor.matmul(ring[d % 2][:, 0:LAT], gw[:, c, d * P:(d + 1) * P], s5_u[:, c, CTX:T], start=(c == 0), stop=(c == 3))
                    last.then_inc(used[1] if d == 3 else sem("glu_done"), 1)
                for hd in range(HEADS):
                    pe.wait_ge(sem("rope_ready"), 4 if hd < 2 else 4)
                    if hd >= 2:
                        pe.wait_ge(sem("ret_s_ready"), 8 * (hd - 1))
                    for n in range(TT):
                        last = nc.tensor.matmul(banks[2 * (hd % 2) + n // 2][:, LAT * (n % 2):LAT * (n % 2 + 1)],
                                                ret_k[:, hd, n * P:(n + 1) * P], ret_q[:, hd, :], start=True, stop=True)
                    last.then_inc(sem("ret_scores_done"), 1)
                    if hd:
                        ret_out(hd - 1)
                ret_out(HEADS - 1)
                head_norm_stats("odd", CTX)
                out_proj("odd", (2, 3), CTX)

            def ret_out(hd):
                if hd >= 2:
                    pe.wait_ge(sem("ret_hs_ready"), hd - 1)
                for k, (way, n, a, b) in enumerate(RET_PARTS):
                    pe.wait_ge(sem("ret_s_ready"), 8 * hd + k + 1)
                    last = nc.tensor.matmul(banks[4 + hd % 2][:, a:b], ret_v[:, n, hd * P:(hd + 1) * P],
                                            ret_s[:, (2 * hd + way) % 4, n, a:b], start=(k == 0), stop=(k == 7))
                last.then_inc(sem("ret_out_done"), 1)

            for s in range(4):
                ffn(s)
                if s == 0:
                    even()
                if s == 2:
                    odd()

        @block.scalar
        def _(act):
            def condition(n):
                act.wait_ge(sem("cvec_in"), 32 * (n + 1))
                for s_ in range(2):
                    nc.scalar.activation(csilu[s_], csilu[s_], ACT.Silu).then_inc(sem("csilu_ready"), 1)

            condition(0)

            def modulate(n, c0):
                ready = sem("m_ready")
                act.wait_ge(sem("folded"), 2 * n + 2)
                for d in range(KT):
                    if n:
                        act.wait_ge(sem("z"), before("z", stages[n - 1]) + d + 1)
                    elif d == 0:
                        act.wait_ge(sem("x_in"), 16)
                    if stages[n] in ADA_IN:
                        if c0 == 0:
                            nc.scalar.activation(m[:, d, 0:CTX], h[:, d, 0:CTX], ACT.Identity,
                                                 scale=mscale[:, n, d, 0:1], bias=mshift[:, n, d, 0:1]).then_inc(sem("m_ctx_ready"), 1)
                        if d:
                            inputs_hi(n, d - 1, c0)
                        if d == KT - 1:
                            inputs_hi(n, d, c0)
                        continue
                    for s_, (a, b) in enumerate(STREAMS):
                        last = nc.scalar.activation(m[:, d, a:b], h[:, d, a:b], ACT.Identity,
                                                    scale=mscale[:, n, d, s_:s_ + 1], bias=mshift[:, n, d, s_:s_ + 1])
                    last.then_inc(ready, 1)

            def inputs_hi(n, d, c0):
                s = (0, 2, 3, 5).index(n)
                if c0 == 0:
                    act.wait_ge(sem("m_ctx_ready"), s * KT + d + 1)
                act.wait_ge(sem("m_lat_ready"), s * KT + d + 1)
                nc.scalar.activation(m_hi[:, d, c0:T], m[:, d, c0:T], ACT.Copy).then_inc(sem("m_ready"), 1)

            def weights_hi(s, f, off, it=None):
                b, turn = f // 2 % 2, (lambda step: 0 if it is None else it * step)
                if off == 0 and f % 2 == 0:
                    act.wait_ge(full[b], turn(16) + 16 * pair_use(s, f // 2))
                if f and off == 0:
                    act.wait_ge(sem("gate_done"), turn(4) + s * FT + f)
                elif f and f % 2 == 1:
                    act.wait_ge(sem("up_done"), turn(2) + s * PAIRS + (f - 1) // 2 + 1)
                elif f:
                    act.wait_ge(used[1 - b], turn(1) + pair_use(s, f // 2 - 1))
                nc.scalar.activation(w_hi[:, off, :, :].rearrange("p a b -> p (a b)"),
                                     slots[b][:, (2 * (f % 2) + off) * D:(2 * (f % 2) + off + 1) * D], ACT.Copy).then_inc(sem("w_hi_ready"), 1)

            def log_sigmoid_soft(x):
                nc.scalar.activation(x, x, ACT.Exp).then_inc(sem("log_g_soft"), 1)
                act.wait_ge(sem("log_g_soft"), 1)
                nc.scalar.activation(x, x, ACT.Ln, bias=1.0).then_inc(sem("log_g_soft"), 1)

            def parameters():
                act.wait_ge(sem("log_g_nabs"), 1)
                log_sigmoid_soft(small[:, 7, 0:2 * HEADS])
                act.wait_ge(sem("s5_small_phase"), 1)
                nc.scalar.activation(small[:, 2, :], small[:, 0, :], ACT.Sin).then_inc(sem("s5_small_sin"), 1)
                nc.scalar.activation(small[:, 3, :], small[:, 0, :], ACT.Sin, scale=0.5).then_inc(sem("s5_small_sin"), 1)

            def sines(u):
                act.wait_ge(sem("phase_ready"), u + 1)
                if u >= 4:
                    act.wait_ge(sem(f"table_written{u % 4}"), 16 * (u // 4))
                nc.scalar.activation(tables_out[:, u % 4, 1, :], phase[:, u % 2, 0, :], ACT.Sin).then_inc(sem("phase_sin"), 1)
                nc.scalar.activation(phase[:, u % 2, 2, :], phase[:, u % 2, 0, :], ACT.Sin, scale=0.5).then_inc(sem("phase_half"), 1)
                if u:
                    table_out(u - 1)

            def table_out(u):
                act.wait_ge(sem("table_cos_ready"), u + 1)
                act.dma_start(tables_dram[u], tables_out[:, u % 4, :, :].rearrange("p a b -> p (a b)")).then_inc(sem(f"table_written{u % 4}"), 16)

            for off in range(2):
                weights_hi(0, 0, off)
            modulate(0, 0)

            def down_weights_hi(s, d, half):
                k = 3 + d % 2
                if half == 0:
                    act.wait_ge(full[k], 16 * (uses_before(f"ffn{s}")[k] + d // 2 + 1))
                if d == 0:
                    act.wait_ge(used[1], pair_use(s, PAIRS - 2))
                elif half == 0:
                    act.wait_ge(sem("down_half_done"), s * KT + d)
                else:
                    act.wait_ge(used[7 - k], uses_before(f"ffn{s}")[7 - k] + (d - 1) // 2 + 1)
                nc.scalar.activation(down_hi[:, half, :, :].rearrange("p a b -> p (a b)"),
                                     slots[k][:, half * HALF * P:(half + 1) * HALF * P], ACT.Copy).then_inc(sem("down_hi_ready"), 1)

            def hidden_hi(s, f, c0):
                if f == 0:
                    act.wait_ge(used[1], pair_use(s, PAIRS - 2))
                if f == 2:
                    act.wait_ge(used[0], pair_use(s, PAIRS - 1))
                act.wait_ge(sem("g_ready"), s * FT + f + 1)
                nc.scalar.activation(g_hi(f)[:, c0:T], g[:, f, c0:T], ACT.Copy).then_inc(sem("g_hi_ready"), 1)

            def squares(name, c0):
                for d in range(KT):
                    if name == "ffn2":
                        for u in range(4 * d, 4 * d + 4):
                            sines(u)
                        if d == KT - 1:
                            table_out(len(UNITS5) - 1)
                    if name[:3] == "ffn" and d + 1 < KT:
                        for half in range(2):
                            down_weights_hi(int(name[3]), d + 1, half)
                    act.wait_ge(sem("r_ready"), before("r_ready", name) + d + 1)
                    if d >= 2:
                        act.wait_ge(sem("sums"), before("sums", name) + 2 * (d - 1))
                    nc.scalar.activation(sq[:, d % 2, c0:T], h[:, d, c0:T], ACT.Square).then_inc(sem("sq"), 1)
                    if name == "ffn0" and d == 3:
                        parameters()

            def norm(n, name, c0):
                if n + 1 in (2, 3, 5):
                    for off in range(2):
                        weights_hi((2, 3, 5).index(n + 1) + 1, 0, off)
                act.wait_ge(sem("var"), before("var", name) + 1)
                nc.scalar.activation(rstd[:, c0:T], rstd[:, c0:T], ACT.Sqrt).then_inc(sem("std"), 1)
                if n + 1 < 6:
                    modulate(n + 1, CTX if n + 1 == 5 else 0)

            def ffn(s):
                name = f"ffn{s}"
                c0 = CTX if s == 3 else 0

                def step(f, it=None):
                    if f + 1 < FT:
                        weights_hi(s, f + 1, 0, it)
                    if it is None:
                        act.wait_ge(sem("gate_done"), s * FT + f + 1)
                        if f >= 2:
                            act.wait_ge(sem("g_ready"), s * FT + f - 1)
                    else:
                        act.wait_ge(sem("gate_done"), it * 4 + (s * FT + f + 1))
                        act.wait_ge(sem("g_ready"), it * 4 + (s * FT + f - 1))
                    nc.scalar.activation(silu_g[:, f % 2, c0:T], gate_bank[f % 2][:, c0:T], ACT.Silu).then_inc(sem("silu_done"), 1)
                    if f + 1 < FT:
                        weights_hi(s, f + 1, 1, it)

                if s == 1:
                    condition(1)
                step(0)
                step(1)
                with act.Fori(0, PAIRS // 2 - 1) as it:
                    for f in range(2, 6):
                        step(f, it)
                for f in range(FT - 4, FT - 1):
                    step(f)
                for half in range(2):
                    down_weights_hi(s, 0, half)
                hidden_hi(s, 0, c0)
                hidden_hi(s, 1, c0)
                step(FT - 1)
                for f in range(2, FT):
                    hidden_hi(s, f, c0)
                squares(name, c0)

            slot_done = [0] * 5

            def projected(name, n, k):
                if n % 4 == 3:
                    slot_done[k] += 1
                    act.wait_ge(used[k], slot_done[k])
                else:
                    act.wait_ge(sem(f"{name}_proj_done"), 3 * (n // 4) + n % 4 + 1)

            def head_norm(name, c0):
                for hd in range(HEADS):
                    act.wait_ge(sem(f"{name}_hc_ready"), hd + 1)
                    nc.scalar.activation(hsq[:, hd, c0:T], hs[:, hd, c0:T], ACT.Square).then_inc(sem(f"{name}_hsq_ready"), 1)
                act.wait_ge(sem(f"{name}_hvar_ready"), HEADS)
                nc.scalar.activation(hvar[:, :, c0:T], hvar[:, :, c0:T], ACT.Sqrt).then_inc(sem(f"{name}_hstd_ready"), 1)

            def even():
                slot_done[:] = uses_before("even")
                read = sem("even_proj_read")
                act.wait_ge(sem("even_params_in"), 16 * 8)
                for n in range(4):
                    projected("even", n, 0)
                    if n >= 2:
                        act.wait_ge(sem("even_conv_done"), n - 1)
                    nc.scalar.activation(xm[:, n % 2, :], banks[n % 4][:, :], ACT.Copy).then_inc(read, 1)
                slot_done[1] += 1
                act.wait_ge(used[1], slot_done[1])
                nc.scalar.activation(gates_tok.rearrange("p a b -> p (a b)"), banks[4][:, 0:TT * 16], ACT.Copy).then_inc(sem("even_gates_read"), 1)
                for hd in range(HEADS):
                    act.wait_ge(sem("even_conv_done"), hd + 1)
                    nc.scalar.activation(xc[:, hd, :], xc[:, hd, :], ACT.Silu).then_inc(sem("even_xc_ready"), 1)
                for n in range(4, 8):
                    projected("even", n, 2)
                    nc.scalar.activation(sig_o[:, n - 4, :], banks[n % 4][:, :], ACT.Sigmoid).then_inc(read, 1)
                for kind in range(4):
                    act.wait_ge(sem("even_rows_done"), kind + 1)
                    nc.scalar.activation(rows[:, kind, :], banks[4 + kind][0:HEADS, :], ACT.Identity, bias=gate_b[:, kind:kind + 1]).then_inc(sem("even_rows_ready"), 1)
                act.wait_ge(sem("even_nabs_ready"), 1)
                nc.scalar.activation(rows[:, 6:8, :], rows[:, 6:8, :], ACT.Exp).then_inc(sem("even_soft"), 1)
                act.wait_ge(sem("even_soft"), 1)
                nc.scalar.activation(rows[:, 6:8, :], rows[:, 6:8, :], ACT.Ln, bias=1.0).then_inc(sem("even_soft"), 1)
                for n in range(8, 24):
                    if n == 12:
                        act.wait_ge(sem("even_bm_ready"), 1)
                        nc.scalar.activation(rows[:, 2:4, :], rows[:, 2:4, :], ACT.Exp).then_inc(sem("even_em_ready"), 1)
                    projected("even", n, (3, 0, 1, 2)[n // 4 - 2])
                    dst = (na_q, na_k, na_v, ml_v)[n // 4 - 2][:, n % 4, :]
                    nc.scalar.activation(dst, banks[n % 4][:, :], ACT.Copy, scale=NA_DIM ** -0.5 if n < 12 else 1.0).then_inc(read, 1)
                act.wait_ge(sem("even_acol_done"), 1)
                nc.scalar.activation(acol[:, :, :, :].rearrange("p a b c -> p (a b c)"), banks[6][:, 0:2 * TT * HEADS], ACT.Copy).then_inc(sem("even_acol_ready"), 1)

                def exps(u):
                    st = UNITS[u][1]
                    keys = CTX if st == 0 else T
                    act.wait_ge(sem("na_max_ready"), u + 1)
                    src = score_banks[u % 3][:, 0:keys] if st == 0 else probs[u % 3][:, :]
                    nc.scalar.activation(probs[u % 3][:, 0:keys], src, ACT.Exp, bias=col[:, u % 2:u % 2 + 1],
                                         accum_out=col[:, 2 + u % 2:3 + u % 2]).then_inc(sem("na_exp_done"), 1)

                exps(0)
                for u, (hp, st, hh, qt) in enumerate(UNITS):
                    if u + 1 < len(UNITS):
                        exps(u + 1)
                    tiles = 2 if st == 0 else 4
                    act.wait_ge(sem("na_pT_done"), u + 1)
                    if u >= 4 and qt == 0:
                        act.wait_ge(sem("na_out_done"), u // 2 - 1)
                    nc.scalar.activation(probsT[:, (u // 2) % 2, 0:tiles, qt * P:(qt + 1) * P],
                                         banks[2 + u % 2][:, 0:tiles * P].rearrange("p (a n) -> p a n", n=P), ACT.Copy).then_inc(sem("na_pT_ready"), 1)

                slot_done[3] += 1
                for hd in range(HEADS):
                    for a, (dst, scale) in enumerate(((ml_qh, 1.0), (ml_kh, HDIM ** -0.5))):
                        if hd == HEADS - 1 and a == 1:
                            act.wait_ge(used[3], slot_done[3])
                        else:
                            act.wait_ge(sem("ml_qk_proj_done"), 2 * hd + a + 1)
                        nc.scalar.activation(dst[:, hd % 2, :], banks[6 + a][:, :], ACT.Copy, scale=scale).then_inc(sem("ml_qk_ready"), 1)
                    for way in range(2):
                        v = 2 * hd + way
                        for k, n in enumerate(ORDER[way]):
                            act.wait_ge(sem("ml_arg_ready"), TT * v + k + 1)
                            a, b = TARGETS[way][n][0][0], TARGETS[way][n][-1][1]
                            nc.scalar.activation(decay[way][:, n, a:b], decay[way][:, n, a:b], ACT.Exp).then_inc(sem("ml_exp_done"), 1)
                        act.wait_ge(sem("ml_em_done"), v + 1)
                        nc.scalar.activation(em_b[:, way, :], banks[6][:, :], ACT.Copy).then_inc(sem("ml_em_read"), 1)
                head_norm("even", 0)
                squares("even", 0)
                norm(1, "even", 0)

            def odd():
                slot_done[:] = uses_before("odd")
                read = sem("odd_proj_read")
                for n in range(20):
                    projected("odd", n, (0, 1, 2, 3, 0)[n // 4])
                    bank = banks[6 + n % 2]
                    if n < 4:
                        ins = nc.scalar.activation(s5_u[:, n, :], bank[:, :], ACT.Copy)
                    elif n < 8:
                        ins = nc.scalar.activation(ret_k[:, n - 4, :], bank[:, :], ACT.Copy, scale=HDIM ** -0.5)
                    elif n < 12:
                        ins = nc.scalar.activation(ret_v[:, n - 8, :], bank[:, :], ACT.Copy)
                    elif n < 16:
                        ins = nc.scalar.activation(ret_q[:, n - 12, :], bank[:, CTX:T], ACT.Copy)
                    else:
                        ins = nc.scalar.activation(ret_gate[:, n - 16, :], bank[:, CTX:T], ACT.Silu)
                    ins.then_inc(read, 1)
                for k in range(4):
                    act.wait_ge(sem("s5_skip_ready"), k + 1)
                    nc.scalar.activation(s5_u[:, k, CTX:T], s5_u[:, k, CTX:T], ACT.Gelu_apprx_tanh).then_inc(sem("s5_act_ready"), 1)
                slot_done[1] += 1
                for d in range(4):
                    if d == 3:
                        act.wait_ge(used[1], slot_done[1])
                    else:
                        act.wait_ge(sem("glu_done"), d + 1)
                    nc.scalar.activation(glu_sig[:, d, :], banks[6 + d % 2][:, 0:LAT], ACT.Sigmoid, bias=glu_b[:, d:d + 1]).then_inc(sem("glu_read"), 1)
                act.wait_ge(sem("rel_ready"), 2)
                act.wait_ge(sem("s5_z_ready"), len(UNITS5))
                act.wait_ge(sem("s5_x_ready"), len(UNITS5))
                for hd in range(HEADS):
                    for way in range(2):
                        nc.scalar.activation(ret_decay[:, 2 * hd + way, :], rel[:, way, :], ACT.Exp, scale=log_g[:, way, hd:hd + 1]).then_inc(sem("ret_decay_exp"), 1)
                head_norm("odd", CTX)
                squares("odd", CTX)
                norm(4, "odd", CTX)

            for s in range(4):
                ffn(s)
                norm([0, 2, 3, 5][s], f"ffn{s}", CTX if s == 3 else 0)
                if s == 0:
                    even()
                if s == 2:
                    odd()
            for d in range(KT):
                act.wait_ge(sem("h_ready"), before("h_ready", "ffn3") + d + 1)
                act.dma_start(out[:, d, :], h[:, d, CTX:T]).then_inc(sem("out_written"), 16)

        @block.vector
        def _(dve):
            chain = [0]
            mcount = [0]
            slot_done = [0] * 5

            def link(ins):
                chain[0] += 1
                ins.then_inc(sem("dve_chain"), 1)
                dve.wait_ge(sem("dve_chain"), chain[0])

            nc.vector.memset(mean_w[:, :], 1.0 / D).then_inc(sem("mean_w_ready"), 1)
            def exact_exp(dst, x, k_, p_):
                link(nc.vector.tensor_scalar(x, x, -87.0, 88.0, ALU.max, ALU.min))
                link(nc.vector.tensor_scalar(k_, x, 1.0 / math.log(2.0), ROUND, ALU.mult, ALU.add))
                link(nc.vector.tensor_scalar(k_, k_, ROUND, None, ALU.subtract))
                link(nc.vector.scalar_tensor_tensor(x, k_, -LN2_A, x, ALU.mult, ALU.add))
                link(nc.vector.scalar_tensor_tensor(x, k_, -LN2_B, x, ALU.mult, ALU.add))
                link(nc.vector.tensor_scalar(p_, x, 1.0 / math.factorial(8), None, ALU.mult))
                for n in range(7, 0, -1):
                    link(nc.vector.scalar_tensor_tensor(p_, p_, 1.0 / math.factorial(n), x, ALU.add, ALU.mult))
                link(nc.vector.tensor_scalar(p_, p_, 1.0, None, ALU.add))
                link(nc.vector.tensor_scalar(k_.bitcast(mybir.dt.int32), k_, 2.0 ** 23, 127 * 2.0 ** 23, ALU.mult, ALU.add))
                link(nc.vector.tensor_tensor(dst, p_, k_, ALU.mult))

            def reduce_angle(x, k_):
                link(nc.vector.tensor_scalar(k_, x, 1.0 / TWO_PI, ROUND, ALU.mult, ALU.add))
                link(nc.vector.tensor_scalar(k_, k_, ROUND, None, ALU.subtract))
                for part in (PI_A, PI_B, PI_C):
                    link(nc.vector.scalar_tensor_tensor(x, k_, -part, x, ALU.mult, ALU.add))
                return nc.vector.tensor_scalar(x, x, -math.pi, math.pi, ALU.max, ALU.min)

            re, im, dt = s5_par[:, 0, :], s5_par[:, 1, :], s5_par[:, 2, :]

            def phases(u):
                st, way = UNITS5[u]
                if u >= 2:
                    dve.wait_ge(sem("table_cos_ready"), u - 1)
                x = phase[:, u % 2, 0, :]
                link(nc.vector.tensor_scalar(x, steps[:, way, :], dt[:, way * S5_TILES + st:way * S5_TILES + st + 1], None, ALU.mult))
                reduce_angle(x, phase[:, u % 2, 1, :]).then_inc(sem("phase_ready"), 1)

            def parameters():
                dve.wait_ge(sem("s5_params_in"), 32)
                lg = log_g[:, :, :].rearrange("p a b -> p (a b)")
                soft = small[:, 7, 0:2 * HEADS]
                link(nc.vector.tensor_scalar(soft, lg, -1.0, None, ALU.mult))
                nc.vector.tensor_tensor(soft, soft, lg, ALU.min).then_inc(sem("log_g_nabs"), 1)
                exact_exp(small[:, 4, :], dt, small[:, 5, :], small[:, 6, :])
                link(nc.vector.tensor_tensor(small[:, 1, :], re, small[:, 4, :], ALU.mult))
                link(nc.vector.tensor_tensor(dt, im, small[:, 4, :], ALU.mult))
                link(nc.vector.tensor_copy(small[:, 0, :], dt))
                reduce_angle(small[:, 0, :], small[:, 5, :]).then_inc(sem("s5_small_phase"), 1)
                exact_exp(s5_mag[:, :], small[:, 1, :], small[:, 5, :], small[:, 6, :])
                dve.wait_ge(sem("log_g_soft"), 2)
                nc.vector.scalar_tensor_tensor(lg, lg, 0.0, soft, ALU.min, ALU.subtract).then_inc(sem("log_g_ready"), 1)
                dve.wait_ge(sem("s5_small_sin"), 2)
                a_im, a_re, t0, t1 = small[:, 2, :], small[:, 3, :], small[:, 5, :], small[:, 6, :]
                link(nc.vector.tensor_tensor(a_re, a_re, a_re, ALU.mult))
                link(nc.vector.tensor_scalar(a_re, a_re, -2.0, 1.0, ALU.mult, ALU.add))
                link(nc.vector.tensor_tensor(a_re, a_re, s5_mag[:, :], ALU.mult))
                link(nc.vector.tensor_scalar(a_re, a_re, 1.0, None, ALU.subtract))
                link(nc.vector.tensor_tensor(a_im, a_im, s5_mag[:, :], ALU.mult))
                link(nc.vector.tensor_tensor(t0, re, re, ALU.mult))
                link(nc.vector.tensor_tensor(t1, im, im, ALU.mult))
                link(nc.vector.tensor_tensor(t0, t0, t1, ALU.add))
                link(nc.vector.reciprocal(small[:, 4, :], t0))
                for part, (p_, q_, op) in enumerate(((a_re, a_im, ALU.add), (a_im, a_re, ALU.subtract))):
                    link(nc.vector.tensor_tensor(t0, p_, re, ALU.mult))
                    link(nc.vector.tensor_tensor(t1, q_, im, ALU.mult))
                    link(nc.vector.tensor_tensor(t0, t0, t1, op))
                    nc.vector.tensor_tensor(s5_e[:, part, :], t0, small[:, 4, :], ALU.mult).then_inc(sem("s5_e_ready"), 1)
                    dve.wait_ge(sem("s5_e_ready"), part + 1)

            def modulation(k, half, it=None, per=0, junk=L[:, 2 * T:4 * T]):
                gi = mcount[0]
                turn = lambda step: 0 if it is None else it * step
                if half == 0:
                    slot_done[k] += 1
                    if gi:
                        dve.wait_ge(sem("mods_ready"), turn(per) + gi)
                    dve.wait_ge(full[k], turn(16 * per) + 16 * slot_done[k])
                for j in range(4 * half, 4 * half + 4):
                    t, s_ = j // 2, j % 2
                    ins = nc.vector.tensor_tensor_reduce(out=junk, in0=slots[k][:, t * D:(t + 1) * D], in1=csilu[s_], scale=1.0, scalar=0.0,
                                                         op0=ALU.mult, op1=ALU.add, accum_out=ada_sum[:, t, s_:s_ + 1])
                    if j < 7:
                        ins.then_inc(sem("ada_part"), 1)
                        dve.wait_ge(sem("ada_part"), turn(7 * per) + 7 * gi + j + 1)
                    else:
                        ins.then_inc(used[k], 1)
                        dve.wait_ge(used[k], turn(per) + slot_done[k])
                if half == 0:
                    return
                mcount[0] += 1
                if gi == 0:
                    dve.wait_ge(sem("params_in"), 48)
                flat = lambda buf: buf[:, :, :, :].rearrange("p a b c -> p (a b c)")
                if it is None:
                    dst, b_ = (flat(buf)[:, 8 * gi:8 * gi + 8] for buf in (mods, modb))
                else:
                    dst, b_ = (flat(buf)[:, bass.ds(it * (8 * per) + 8 * gi, 8)] for buf in (mods, modb))
                nc.vector.tensor_tensor(dst, ada_sum[:, :, :].rearrange("p a b -> p (a b)"), b_, ALU.add).then_inc(sem("mods_ready"), 1)

            dve.wait_ge(sem("csilu_ready"), 2)
            for g_ in range(4):
                for half in range(2):
                    modulation(1 + g_ % 2, half)

            def mask_bias():
                for n in range(8):
                    dve.wait_ge(sem("na_bias_turned"), n + 1)
                    cols = lambda v: v.rearrange("p (a c) -> p a c", c=GRID_W)
                    dst = na_bias[:, n // 4, 2 * (n % 4):2 * (n % 4) + 2, :].rearrange("p a b -> p (a b)")
                    nc.vector.tensor_tensor(cols(dst), cols(banks[n][:, :]),
                                            na_mask[:, :].unsqueeze(1).to_broadcast([P, 2 * ROWS, GRID_W]), ALU.add).then_inc(sem("na_bias_masked"), 1)

            def weights_lo(s, f, off, it=None):
                unit = 2 * f + off + 1 + s * 2 * FT
                dve.wait_ge(sem("w_hi_ready"), unit if it is None else it * 8 + unit)
                b, t = f // 2 % 2, 2 * (f % 2) + off
                nc.vector.tensor_tensor(w_lo[b][:, t, :, :].rearrange("p a b -> p (a b)"), slots[b][:, t * D:(t + 1) * D],
                                        w_hi[:, off, :, :].bitcast(F32).rearrange("p a b -> p (a b)"), ALU.subtract).then_inc(sem("w_lo_ready"), 1)

            def modulation_part(n, q):
                l, j = NORMS[n]
                return mods[:, l, (3 * j + q) * KT:(3 * j + q + 1) * KT, :]

            def gates(n):
                dve.wait_ge(sem("mods_ready"), 6 * n + 6)
                half = (1.0 if NORMS[n][1] == 1 else 0.5) / ALPHA
                link(nc.vector.tensor_scalar(mgate[:, n, :, :], modulation_part(n, 2), half, None, ALU.mult))

            def fold(n):
                dve.wait_ge(sem("mods_ready"), 6 * n + 4)
                part = lambda q: modulation_part(n, q)
                if n == 0:
                    nc.vector.tensor_scalar(mscale[:, 0, :, :], part(1), 1.0, None, ALU.add).then_inc(sem("folded"), 1)
                    nc.vector.tensor_copy(mshift[:, 0, :, :], part(0)).then_inc(sem("folded"), 1)
                    return
                link(nc.vector.tensor_scalar(mscale[:, n, :, :], part(1), 1.0, None, ALU.add))
                bias = lambda buf: buf[:, n - 1, :].unsqueeze(2).to_broadcast([P, KT, 2])
                link(nc.vector.tensor_tensor(mshift[:, n, :, :], mscale[:, n, :, :], bias(lnb), ALU.mult))
                nc.vector.tensor_tensor(mshift[:, n, :, :], mshift[:, n, :, :], part(0), ALU.add).then_inc(sem("folded"), 1)
                nc.vector.tensor_tensor(mscale[:, n, :, :], mscale[:, n, :, :], bias(lng), ALU.mult).then_inc(sem("folded"), 1)

            fold(0)

            def residual(n, name, d, bank, c0):
                for s_, (a, b) in enumerate(STREAMS):
                    if b <= c0:
                        continue
                    last = nc.vector.scalar_tensor_tensor(h[:, d, a:b], bank[:, a:b], mgate[:, n, d, s_:s_ + 1],
                                                          h[:, d, a:b], ALU.mult, ALU.add)
                last.then_inc(sem("r_ready"), 1)

            def norm(n, name, c0):
                w = slice(c0, T)
                if n + 1 in (2, 3, 5):
                    for off in range(2):
                        weights_lo((2, 3, 5).index(n + 1) + 1, 0, off)
                dve.wait_ge(sem("stat"), before("stat", name) + 1)
                nc.vector.tensor_copy(mean[:, w], stat_bank[:, w]).then_inc(sem("stat_read"), 1)
                dve.wait_ge(sem("stat_read"), before("stat_read", name) + 1)
                link(nc.vector.tensor_tensor(rstd[:, w], mean[:, w], mean[:, w], ALU.mult))
                dve.wait_ge(sem("stat"), before("stat", name) + 2)
                nc.vector.tensor_tensor(rstd[:, w], stat2_bank[:, w], rstd[:, w], ALU.subtract).then_inc(sem("stat_read"), 1)
                dve.wait_ge(sem("stat_read"), before("stat_read", name) + 2)
                nc.vector.tensor_scalar(rstd[:, w], rstd[:, w], 0.0, EPS / ALPHA ** 2, ALU.max, ALU.add).then_inc(sem("var"), 1)
                dve.wait_ge(sem("std"), before("std", name) + 1)
                link(nc.vector.reciprocal(rstd[:, w], rstd[:, w]))
                for d in range(KT):
                    dve.wait_ge(sem("c"), before("c", name) + d + 1)
                    nc.vector.tensor_tensor(h[:, d, w], h[:, d, w], rstd[:, w], ALU.mult).then_inc(sem("z"), 1)
                    if n + 1 in (2, 3, 5):
                        inputs(n + 1, d, name)

            def inputs(n, d, name=None):
                s = (0, 2, 3, 5).index(n)
                c0 = CTX if n == 5 else 0

                def latent(d):
                    if name:
                        dve.wait_ge(sem("z"), before("z", name) + d + 1)
                    if d == 0:
                        dve.wait_ge(sem("folded"), 2 * n + 2)
                    nc.vector.tensor_scalar(m[:, d, CTX:T], h[:, d, CTX:T], mscale[:, n, d, 1:2], mshift[:, n, d, 1:2],
                                            ALU.mult, ALU.add).then_inc(sem("m_lat_ready"), 1)

                def rest(d):
                    dve.wait_ge(sem("m_ready"), before("m_ready", f"ffn{s}") + d + 1)
                    nc.vector.tensor_tensor(m_lo[:, d, c0:T], m[:, d, c0:T], m_hi[:, d, c0:T].bitcast(F32), ALU.subtract).then_inc(sem("m_lo_ready"), 1)

                if d:
                    latent(d - 1)
                if d >= 3:
                    rest(d - 3)
                if d == KT - 1:
                    latent(d)
                    for k in range(KT - 3, KT):
                        rest(k)

            def ffn(s):
                name = f"ffn{s}"
                c0 = CTX if s == 3 else 0

                def step(f, it=None, ada=False):
                    if f + 1 < FT:
                        for off in range(2):
                            weights_lo(s, f + 1, off, it)
                    turn = lambda step: 0 if it is None else it * step
                    dve.wait_ge(sem("silu_done"), turn(4) + s * FT + f + 1)
                    if f % 2 == 0:
                        dve.wait_ge(sem("up_done"), turn(2) + s * PAIRS + f // 2 + 1)
                    else:
                        dve.wait_ge(used[f // 2 % 2], turn(1) + pair_use(s, f // 2))
                    dst = g[:, f, c0:T] if it is None else g[:, bass.ds(it * 4 + f, 1), c0:T].rearrange("p a n -> p (a n)")
                    nc.vector.tensor_tensor(dst, silu_g[:, f % 2, c0:T], up_bank[f % 2][:, c0:T], ALU.mult).then_inc(sem("g_ready"), 1)
                    if ada:
                        modulation(2, f % 2, it=it, per=2)

                def down_weights_lo(d, half):
                    dve.wait_ge(sem("down_hi_ready"), 2 * KT * s + 2 * d + half + 1)
                    nc.vector.tensor_tensor(down_lo[d % 2][:, half, :, :].rearrange("p a b -> p (a b)"),
                                            slots[3 + d % 2][:, half * HALF * P:(half + 1) * HALF * P],
                                            down_hi[:, half, :, :].bitcast(F32).rearrange("p a b -> p (a b)"), ALU.subtract).then_inc(sem("down_lo_ready"), 1)

                def hidden_lo(f):
                    dve.wait_ge(sem("g_hi_ready"), s * FT + f + 1)
                    nc.vector.tensor_tensor(g_lo[:, f, c0:T], g[:, f, c0:T], g_hi(f)[:, c0:T].bitcast(F32), ALU.subtract).then_inc(sem("g_lo_ready"), 1)

                slot_done[:] = uses_before(name)
                if s == 1:
                    dve.wait_ge(sem("csilu_ready"), 4)
                if s == 0:
                    dve.wait_ge(sem("x_in"), 16)
                    for d in range(KT):
                        inputs(0, d)
                    for off in range(2):
                        weights_lo(0, 0, off)
                n_ada = ADA_IN[name][1]
                step(0, ada=n_ada > 0)
                step(1, ada=n_ada > 0)
                for lo, hi, ada in {12: ((0, 4, True),), 8: ((0, 3, True), (3, 4, False)), 0: ((0, 4, False),)}[n_ada]:
                    done, groups = slot_done[2], mcount[0]
                    with dve.Fori(0, hi - lo) as it:
                        for f in range(4 * lo + 2, 4 * lo + 6):
                            step(f, it, ada)
                    slot_done[2] = done + (slot_done[2] - done) * (hi - lo)
                    mcount[0] = groups + (mcount[0] - groups) * (hi - lo)
                for f in range(FT - 4, FT - 1):
                    step(f, ada=n_ada == 12 or n_ada == 8 and f < FT - 2)
                for half in range(2):
                    down_weights_lo(0, half)
                hidden_lo(0)
                hidden_lo(1)
                step(FT - 1)
                for f in range(2, FT):
                    hidden_lo(f)
                if n_ada == 12:
                    modulation(2, 1)
                n = [0, 2, 3, 5][s]
                gates(n)
                if s == 2:
                    dve.wait_ge(sem("s5_steps_in"), 16)
                for d in range(KT):
                    if s == 2:
                        for u in range(4 * d, 4 * d + 4):
                            phases(u)
                    if d + 1 < KT:
                        for half in range(2):
                            down_weights_lo(d + 1, half)
                    k = 3 + d % 2
                    slot_done[k] += 1
                    dve.wait_ge(used[k], slot_done[k])
                    if d == 0:
                        dve.wait_ge(sem("h_ready"), before("h_ready", stages[n - 1]) + KT) if n else dve.wait_ge(sem("m_ready"), before("m_ready", name) + KT)
                    residual(n, name, d, out_bank[d % 2], c0)
                    if s == 0 and d == 3:
                        parameters()
                    if n_ada == 12 and d < 2:
                        modulation(2, d, junk=L[:, 0:2 * T])
                if n + 1 < 6:
                    fold(n + 1)
                norm(n, name, c0)

            def head_norm(name, c0, gain, gate):
                w = slice(c0, T)
                for hd in range(HEADS):
                    dve.wait_ge(sem(f"{name}_hmean_done"), hd + 1)
                    nc.vector.tensor_tensor(hs[:, hd, w], hs[:, hd, w], banks[hd][:, w], ALU.subtract).then_inc(sem(f"{name}_hc_ready"), 1)
                for hd in range(HEADS):
                    dve.wait_ge(sem(f"{name}_hvar_done"), hd + 1)
                    nc.vector.tensor_scalar(hvar[:, hd, w], banks[hd][:, w], EPS, None, ALU.add).then_inc(sem(f"{name}_hvar_ready"), 1)
                dve.wait_ge(sem(f"{name}_hstd_ready"), 1)
                for hd in range(HEADS):
                    link(nc.vector.reciprocal(hvar[:, hd, w], hvar[:, hd, w]))
                    link(nc.vector.tensor_tensor(hs[:, hd, w], hs[:, hd, w], hvar[:, hd, w], ALU.mult))
                    nc.vector.scalar_tensor_tensor(y[:, HEADS + hd, w], hs[:, hd, w], gain[:, hd:hd + 1], gate[:, hd, :],
                                                   ALU.mult, ALU.mult).then_inc(sem(f"{name}_y1"), 1)

            def out_residual(n, name, slot_pair, c0):
                gates(n)
                for d in range(KT):
                    k = slot_pair[d // 4]
                    if d % 4 == 3:
                        slot_done[k] += 1
                        dve.wait_ge(used[k], slot_done[k])
                    else:
                        dve.wait_ge(sem(f"{name}_out_done"), 3 * (d // 4) + d % 4 + 1)
                    if d == 0:
                        dve.wait_ge(sem("h_ready"), before("h_ready", stages[n - 1]) + KT)
                    residual(n, name, d, out_bank[d % 2], c0)

            def even():
                mask_bias()
                slot_done[:] = uses_before("even")
                for k, _, _, _ in EVEN_LOADS[:-2]:
                    slot_done[k] += 1
                dve.wait_ge(sem("even_params_in"), 16 * 8)
                two = lambda v: v.rearrange("p (s n) -> p s n", s=2)
                for hd in range(HEADS):
                    dve.wait_ge(sem("even_proj_read"), hd + 1)
                    x_, o_ = two(xm[:, hd % 2, :]), two(xc[:, hd, :])
                    link(nc.vector.tensor_scalar(xc[:, hd, :], xm[:, hd % 2, :], conv_w[:, hd, 2:3], conv_b[:, hd:hd + 1], ALU.mult, ALU.add))
                    for j in (0, 1, 3, 4):
                        sh = j - CONV // 2
                        a, b = max(0, -sh), CTX - max(0, sh)
                        ins = nc.vector.scalar_tensor_tensor(o_[:, :, a:b], x_[:, :, a + sh:b + sh], conv_w[:, hd, j:j + 1],
                                                             o_[:, :, a:b], ALU.mult, ALU.add)
                        if j == CONV - 1:
                            ins.then_inc(sem("even_conv_done"), 1)
                        else:
                            link(ins)
                dve.wait_ge(sem("even_rows_ready"), 4)
                link(nc.vector.tensor_scalar(rows[:, 6:8, :], rows[:, 2:4, :], -1.0, None, ALU.mult))
                nc.vector.tensor_tensor(rows[:, 6:8, :], rows[:, 6:8, :], rows[:, 2:4, :], ALU.min).then_inc(sem("even_nabs_ready"), 1)
                dve.wait_ge(sem("even_soft"), 2)
                link(nc.vector.scalar_tensor_tensor(rows[:, 2:4, :], rows[:, 2:4, :], 0.0, rows[:, 6:8, :], ALU.min, ALU.subtract))
                one = lambda n: ones_w[0:HEADS, 0:1].to_broadcast([HEADS, n])

                def scans(dst, src, op):
                    nc.vector.tensor_tensor_scan(rows[:, dst, :], one(T), rows[:, src, :], 0.0, ALU.mult, op)
                    link(nc.vector.tensor_tensor_scan(rows[:, dst + 1, 0:CTX][:, ::-1], one(CTX), rows[:, src + 1, 0:CTX][:, ::-1], 0.0, ALU.mult, op))
                    link(nc.vector.tensor_tensor_scan(rows[:, dst + 1, CTX:T][:, ::-1], one(LAT), rows[:, src + 1, CTX:T][:, ::-1],
                                                      rows[:, dst + 1, 0:1], ALU.mult, op))

                scans(4, 2, ALU.add)
                nc.vector.tensor_tensor(rows[:, 0:2, :], rows[:, 0:2, :], rows[:, 4:6, :], ALU.subtract).then_inc(sem("even_a_ready"), 1)
                dve.wait_ge(sem("even_a_ready"), 1)
                scans(6, 0, ALU.max)
                link(nc.vector.tensor_tensor(rows[:, 2:4, :], rows[:, 4:6, :], rows[:, 6:8, :], ALU.add))
                nc.vector.tensor_scalar(rows[:, 2:4, :], rows[:, 2:4, :], -1.0, EXP_MAX, ALU.mult, ALU.min).then_inc(sem("even_bm_ready"), 1)
                nc.vector.tensor_scalar(rows[:, 4:6, :], rows[:, 6:8, :], -1.0, None, ALU.mult).then_inc(sem("even_negm_ready"), 1)

                dve.wait_ge(sem("na_bias_masked"), 8)

                def maxima(u):
                    hp, st, hh, qt = UNITS[u]
                    dve.wait_ge(sem("na_scores_done"), u + 1)
                    neg = col[:, u % 2:u % 2 + 1]
                    if u >= 3:
                        dve.wait_ge(sem("na_pT_done"), u - 2)
                    if st == 0:
                        nc.vector.tensor_reduce(neg, score_banks[u % 3][:, 0:CTX], AX.X, ALU.max, negate=True).then_inc(sem("na_max_ready"), 1)
                    else:
                        nc.vector.tensor_copy(probs[u % 3][:, 0:CTX], score_banks[u % 3][:, 0:CTX])
                        link(nc.vector.tensor_tensor(probs[u % 3][:, CTX:T], score_banks[u % 3][:, CTX:T], na_bias[:, qt, 2 * hp + hh, :], ALU.add))
                        nc.vector.tensor_reduce(neg, probs[u % 3][:, :], AX.X, ALU.max, negate=True).then_inc(sem("na_max_ready"), 1)

                maxima(0)
                for u, (hp, st, hh, qt) in enumerate(UNITS):
                    if u + 1 < len(UNITS):
                        maxima(u + 1)
                    keys = CTX if st == 0 else T
                    dve.wait_ge(sem("na_exp_done"), u + 1)
                    rec = col[:, 4 + u % 2:5 + u % 2]
                    nc.vector.reciprocal(rec, col[:, 2 + u % 2:3 + u % 2]).then_inc(sem("na_scores_read"), 1)
                    dve.wait_ge(sem("na_scores_read"), u + 1)
                    nc.vector.tensor_scalar(probs[u % 3][:, 0:keys], probs[u % 3][:, 0:keys], rec, None, ALU.mult).then_inc(sem("na_probs_ready"), 1)
                    if hh == 0 and qt == 0 and u:
                        attention_out(u // 4 - 1)
                attention_out(7)

                dve.wait_ge(sem("even_acol_ready"), 1)
                def exponents(v):
                    hd, way = v // 2, v % 2
                    dve.wait_ge(sem("ml_negm_done"), v + 1)
                    if v >= 2:
                        dve.wait_ge(sem("ml_numden_done"), v - 1)
                    for n in ORDER[way]:
                        a, b = TARGETS[way][n][0][0], TARGETS[way][n][-1][1]
                        nc.vector.tensor_scalar(decay[way][:, n, a:b], banks[3][:, a:b], acol[:, way, n, hd:hd + 1], 0.0,
                                                ALU.add, ALU.min).then_inc(sem("ml_arg_ready"), 1)

                exponents(0)
                for hd in range(HEADS):
                    for way in range(2):
                        v = 2 * hd + way
                        dve.wait_ge(sem("ml_scores_done"), hd + 1)
                        for k, n in enumerate(ORDER[way]):
                            dve.wait_ge(sem("ml_masked"), TT * v + k + 1)
                            for a, b in TARGETS[way][n]:
                                last = nc.vector.tensor_tensor(decay[way][:, n, a:b], decay[way][:, n, a:b], qk_cols(n, a, b), ALU.mult)
                            last.then_inc(sem("ml_s_ready"), 1)
                        if v + 1 < 2 * HEADS:
                            exponents(v + 1)
                        if hd and way == 1:
                            dve.wait_ge(sem("ml_hsum_ready"), hd)
                        dve.wait_ge(sem("ml_numden_done"), v + 1)
                        dve.wait_ge(sem("ml_em_read"), v + 1)
                        link(nc.vector.scalar_tensor_tensor(em_b[:, way, :], banks[5][:, :], -1.0, em_b[:, way, :], ALU.mult, ALU.max))
                        link(nc.vector.tensor_tensor(em_b[:, way, :], banks[5][:, :], em_b[:, way, :], ALU.max))
                        link(nc.vector.reciprocal(quot[:, way, :], em_b[:, way, :]))
                        dst = hs[:, hd, :] if way == 0 else quot[:, 1, :]
                        nc.vector.tensor_tensor(dst, banks[4][:, :], quot[:, way, :], ALU.mult).then_inc(sem("ml_quot_ready"), 1)
                    dve.wait_ge(sem("ml_quot_ready"), 2 * hd + 2)
                    ins = nc.vector.tensor_tensor(hs[:, hd, :], hs[:, hd, :], quot[:, 1, :], ALU.add)
                    ins.then_inc(sem("even_hs_all") if hd == HEADS - 1 else sem("ml_hsum_ready"), 1)
                head_norm("even", 0, ml_gn, sig_o)
                out_residual(1, "even", (0, 1), 0)
                fold(2)
                norm(1, "even", 0)

            def attention_out(group):
                hp, st = group // 2, group % 2
                a, b = STREAMS[st]
                dve.wait_ge(sem("na_out_done"), 2 * group + 2)
                nc.vector.tensor_copy(y[:, hp, a:b], banks[4 + group % 2][:, 0:CTX]).then_inc(sem("even_y0"), 1)

            nc.vector.memset(ones_w[:, :], 1.0).then_inc(sem("mean_w_ready"), 1)
            nc.vector.memset(hmean_w[:, :], 1.0 / HDIM).then_inc(sem("mean_w_ready"), 1)
            def odd():
                slot_done[:] = uses_before("odd")
                for k, _, _, _ in ODD_LOADS[:-2]:
                    slot_done[k] += 1
                both = lambda v: v.rearrange("p (s n) -> p s n", s=2)
                over = lambda v: v.unsqueeze(1).to_broadcast([P, 2, CTX])

                def rotate_in(u):
                    dve.wait_ge(sem(f"table_in{u % TABLE_RING}"), 16 * (u // TABLE_RING + 1))
                    dve.wait_ge(sem("s5_in_done"), u + 1)
                    if u >= 2:
                        dve.wait_ge(sem("s5_w_ready"), u - 1)
                        dve.wait_ge(sem("s5_w_real"), u - 1)
                        dve.wait_ge(sem("s5_z_ready"), u - 1)
                    cos, sin = (over(tables[:, u % TABLE_RING, c, :]) for c in range(2))
                    re_, im_ = (both(banks[2 * (u % 2) + r][:, :]) for r in range(2))
                    for n, (a, b) in enumerate(((cos, re_), (sin, im_), (cos, im_), (sin, re_))):
                        last = nc.vector.tensor_tensor(both(prods[:, u % 2, n, :]), b, a, ALU.mult)
                        if n == 1:
                            last.then_inc(sem("s5_prod_real"), 1)
                    last.then_inc(sem("s5_prod_done"), 1)
                    dve.wait_ge(sem("s5_prod_real"), u + 1)
                    p_ = prods[:, u % 2, :, :]
                    nc.vector.tensor_tensor(p_[:, 0, :], p_[:, 0, :], p_[:, 1, :], ALU.add).then_inc(sem("s5_w_real"), 1)

                def scan(u):
                    st, way = UNITS5[u]
                    dve.wait_ge(sem("s5_w_real"), u + 1)
                    dve.wait_ge(sem("s5_w_ready"), u + 1)
                    if u >= 2:
                        dve.wait_ge(sem("s5_x_ready"), u - 1)
                    at = way * S5_TILES + st
                    mag = s5_mag[:, at:at + 1].to_broadcast([P, CTX])
                    end = CTX - 1 if way == 0 else 0
                    order = (lambda v: v) if way == 0 else (lambda v: v[:, ::-1])
                    z = [s5_z[:, u % 2, r, :] for r in range(2)]
                    w = [prods[:, u % 2, 2 * r, :] for r in range(2)]
                    nc.vector.tensor_tensor_scan(order(z[0][:, 0:CTX]), mag, order(w[0][:, 0:CTX]), 0.0, ALU.mult, ALU.add)
                    link(nc.vector.tensor_tensor_scan(order(z[1][:, 0:CTX]), mag, order(w[1][:, 0:CTX]), 0.0, ALU.mult, ALU.add))
                    cos, sin = (tables[:, u % TABLE_RING, c, end:end + 1] for c in range(2))
                    zr, zi = (z[r][:, end:end + 1] for r in range(2))
                    nc.vector.tensor_tensor(s5_init[:, 2:3], zi, sin, ALU.mult)
                    link(nc.vector.tensor_tensor(s5_init[:, 3:4], zr, sin, ALU.mult))
                    nc.vector.scalar_tensor_tensor(s5_init[:, 0:1], zr, cos, s5_init[:, 2:3], ALU.mult, ALU.subtract)
                    link(nc.vector.scalar_tensor_tensor(s5_init[:, 1:2], zi, cos, s5_init[:, 3:4], ALU.mult, ALU.add))
                    for r in range(2):
                        last = nc.vector.tensor_tensor_scan(order(z[r][:, CTX:T]), mag, order(w[r][:, CTX:T]), s5_init[:, r:r + 1], ALU.mult, ALU.add)
                    last.then_inc(sem("s5_z_ready"), 1)

                def skip(k):
                    dve.wait_ge(sem("s5_y_done"), 8 * (k + 1))
                    nc.vector.scalar_tensor_tensor(s5_u[:, k, CTX:T], s5_u[:, k, CTX:T], s5_d[:, k:k + 1],
                                                   banks[4 + k // 2][:, LAT * (k % 2):LAT * (k % 2 + 1)], ALU.mult, ALU.add).then_inc(sem("s5_skip_ready"), 1)

                dve.wait_ge(sem("odd_params_in"), 16 * 7)
                rotate_in(0)
                for u in range(len(UNITS5)):
                    if u + 1 < len(UNITS5):
                        rotate_in(u + 1)
                    scan(u)
                for n in range(4):
                    x = ret_q[:, 2 * n:2 * n + 2, :] if n < 2 else ret_k[:, 2 * n - 4:2 * n - 2, CTX:T]
                    dve.wait_ge(sem("rope_done"), n + 1)
                    if n == 0:
                        dve.wait_ge(sem("s5_x_ready"), len(UNITS5))
                    table = lambda c: rope[:, c, :].unsqueeze(1).to_broadcast([P, 2, LAT])
                    link(nc.vector.tensor_tensor(rope_tmp, banks[n][:, :].rearrange("p (a b) -> p a b", b=LAT), table(1), ALU.mult))
                    link(nc.vector.tensor_tensor(x, x, table(0), ALU.mult))
                    nc.vector.tensor_tensor(x, x, rope_tmp, ALU.add).then_inc(sem("rope_ready"), 1)
                    dve.wait_ge(sem("rope_ready"), n + 1)
                for k in range(4):
                    skip(k)
                for d in range(4):
                    dve.wait_ge(sem("glu_read"), d + 1)
                    nc.vector.tensor_tensor(y[:, d, CTX:T], s5_u[:, d, CTX:T], glu_sig[:, d, :], ALU.mult).then_inc(sem("odd_y0"), 1)
                for hd in range(HEADS):
                    dve.wait_ge(sem("ret_scores_done"), hd + 1)
                    dve.wait_ge(sem("ret_decay_ready"), 2 * (hd + 1))
                    if hd >= 2:
                        dve.wait_ge(sem("ret_out_done"), hd - 1)
                    for way, n, a, b in RET_PARTS:
                        off = decay_at(way, n)
                        nc.vector.tensor_tensor(ret_s[:, (2 * hd + way) % 4, n, a:b],
                                                banks[2 * (hd % 2) + n // 2][:, LAT * (n % 2) + a:LAT * (n % 2) + b],
                                                ret_decay[:, 2 * hd + way, off + a:off + b], ALU.mult).then_inc(sem("ret_s_ready"), 1)
                    if hd:
                        ret_read(hd - 1)
                ret_read(HEADS - 1)
                head_norm("odd", CTX, ret_gn, ret_gate)
                out_residual(4, "odd", (2, 3), CTX)
                fold(5)
                norm(4, "odd", CTX)

            def ret_read(hd):
                dve.wait_ge(sem("ret_out_done"), hd + 1)
                nc.vector.tensor_copy(hs[:, hd, CTX:T], banks[4 + hd % 2][:, 0:LAT]).then_inc(sem("odd_hs_all") if hd == HEADS - 1 else sem("ret_hs_ready"), 1)

            for s in range(4):
                ffn(s)
                if s == 0:
                    even()
                if s == 2:
                    odd()

        @block.gpsimd
        def _(pool):
            def sums(name, c0):
                w = slice(c0, T)
                chain = 0
                for d in range(KT):
                    if name == "ffn2":
                        for u in range(4 * d, 4 * d + 4):
                            cosines(u)
                    pool.wait_ge(sem("r_ready"), before("r_ready", name) + d + 1)
                    if d == 0:
                        nc.gpsimd.tensor_copy(rsum[:, w], h[:, 0, w]).then_inc(sem("sums"), 1)
                    else:
                        nc.gpsimd.tensor_tensor(rsum[:, w], rsum[:, w], h[:, d, w], ALU.add).then_inc(sem("sums"), 1)
                    pool.wait_ge(sem("sq"), before("sq", name) + d + 1)
                    if d == 0:
                        nc.gpsimd.tensor_copy(rsq[:, w], sq[:, 0, w]).then_inc(sem("sums"), 1)
                    else:
                        nc.gpsimd.tensor_tensor(rsq[:, w], rsq[:, w], sq[:, d % 2, w], ALU.add).then_inc(sem("sums"), 1)
                    pool.wait_ge(sem("sums"), before("sums", name) + 2 * d + 2)

            def centre(name, c0):
                w = slice(c0, T)
                pool.wait_ge(sem("stat_read"), before("stat_read", name) + 1)
                for d in range(KT):
                    nc.gpsimd.tensor_tensor(h[:, d, w], h[:, d, w], mean[:, w], ALU.subtract).then_inc(sem("c"), 1)

            def gains(n, name, c0):
                for d in range(KT):
                    if n + 1 < 6:
                        pool.wait_ge(sem("m_ready"), before("m_ready", stages[n + 1]) + d + 1)
                    else:
                        pool.wait_ge(sem("z"), before("z", name) + d + 1)
                    nc.gpsimd.tensor_scalar(h[:, d, c0:T], h[:, d, c0:T], lng[:, n, d:d + 1], lnb[:, n, d:d + 1],
                                            ALU.mult, ALU.add).then_inc(sem("h_ready"), 1)

            def causal(buf, way):
                sign = 1 if way == 0 else -1
                return nc.gpsimd.affine_select(out=buf, in_=buf, pattern=[[sign, P]], compare_op=ALU.is_ge, fill=0.0,
                                               base=0, channel_multiplier=-sign)

            def even():
                for hd in range(HEADS):
                    for way in range(2):
                        v = 2 * hd + way
                        for k, n in enumerate(ORDER[way]):
                            pool.wait_ge(sem("ml_exp_done"), TT * v + k + 1)
                            causal(decay[way][:, n, n * P:(n + 1) * P], way).then_inc(sem("ml_masked"), 1)
                sums("even", 0)
                centre("even", 0)
                gains(1, "even", 0)

            def odd():
                pool.wait_ge(sem("s5_e_ready"), 2)
                pool.wait_ge(sem("odd_params_in"), 16 * 7)
                e = [s5_e[:, r, :].unsqueeze(2).to_broadcast([P, 2 * S5_TILES, PAIR]) for r in range(2)]
                tmp = view(slots[4], 0, 2, 2 * S5_TILES, PAIR)
                nc.gpsimd.tensor_tensor(c_fold[:, 0, :, :], c_raw[:, 0, :, :], e[0], ALU.mult).then_inc(sem("c_steps"), 1)
                nc.gpsimd.tensor_tensor(tmp[:, 0, :, :], c_raw[:, 1, :, :], e[1], ALU.mult).then_inc(sem("c_steps"), 1)
                nc.gpsimd.tensor_tensor(c_fold[:, 1, :, :], c_raw[:, 0, :, :], e[1], ALU.mult).then_inc(sem("c_steps"), 1)
                nc.gpsimd.tensor_tensor(tmp[:, 1, :, :], c_raw[:, 1, :, :], e[0], ALU.mult).then_inc(sem("c_steps"), 1)
                pool.wait_ge(sem("c_steps"), 4)
                nc.gpsimd.tensor_tensor(c_fold[:, 0, :, :], c_fold[:, 0, :, :], tmp[:, 0, :, :], ALU.subtract).then_inc(sem("c_steps"), 1)
                nc.gpsimd.tensor_tensor(c_fold[:, 1, :, :], c_fold[:, 1, :, :], tmp[:, 1, :, :], ALU.add).then_inc(sem("c_steps"), 1)
                pool.wait_ge(sem("c_steps"), 6)
                nc.gpsimd.tensor_scalar(c_fold[:, 1, :, :], c_fold[:, 1, :, :], -1.0, None, ALU.mult).then_inc(sem("s5_c_ready"), 1)

                def weigh(u):
                    pool.wait_ge(sem("s5_prod_done"), u + 1)
                    p_ = prods[:, u % 2, :, :]
                    nc.gpsimd.tensor_tensor(p_[:, 2, :], p_[:, 2, :], p_[:, 3, :], ALU.subtract).then_inc(sem("s5_w_ready"), 1)

                def states(u):
                    pool.wait_ge(sem("s5_z_ready"), u + 1)
                    if u:
                        pool.wait_ge(sem("s5_x_ready"), u)
                    if u >= 2:
                        pool.wait_ge(sem("s5_y_done"), u - 1)
                    cos, sin = (tables[:, u % TABLE_RING, c, :] for c in range(2))
                    zr, zi = (s5_z[:, u % 2, r, CTX:T] for r in range(2))
                    for n, (a, b) in enumerate(((cos, zr), (sin, zi), (sin, zr), (cos, zi))):
                        nc.gpsimd.tensor_tensor(s5_q[:, n, :], a, b, ALU.mult).then_inc(sem("s5_q_done"), 1)
                    pool.wait_ge(sem("s5_q_done"), 4 * (u + 1))
                    nc.gpsimd.tensor_tensor(s5_x[:, u % 2, 0, :], s5_q[:, 0, :], s5_q[:, 1, :], ALU.subtract)
                    nc.gpsimd.tensor_tensor(s5_x[:, u % 2, 1, :], s5_q[:, 2, :], s5_q[:, 3, :], ALU.add).then_inc(sem("s5_x_ready"), 1)

                weigh(0)
                for u in range(len(UNITS5)):
                    if u + 1 < len(UNITS5):
                        weigh(u + 1)
                    states(u)
                pool.wait_ge(sem("s5_x_ready"), len(UNITS5))
                for way, (base, step) in enumerate(((0, 1), (3 * P, -1))):
                    nc.gpsimd.iota(rel[:, way, :], pattern=[[step, T]], base=base, channel_multiplier=-step,
                                   allow_small_or_imprecise_dtypes=True).then_inc(sem("rel_made"), 1)
                pool.wait_ge(sem("rel_made"), 2)
                for way in range(2):
                    nc.gpsimd.tensor_scalar(rel[:, way, :], rel[:, way, :], 0.0, None, ALU.max).then_inc(sem("rel_ready"), 1)
                for hd in range(HEADS):
                    for way in range(2):
                        n = 2 * hd + way
                        pool.wait_ge(sem("ret_decay_exp"), n + 1)
                        at = 0 if way == 0 else T - P
                        causal(ret_decay[:, n, at:at + P], way).then_inc(sem("ret_decay_ready"), 1)
                sums("odd", CTX)
                centre("odd", CTX)
                gains(4, "odd", CTX)

            def cosines(u):
                half = phase[:, u % 2, 2, :]
                pool.wait_ge(sem("phase_half"), u + 1)
                nc.gpsimd.tensor_tensor(half, half, half, ALU.mult).then_inc(sem("half_squared"), 1)
                pool.wait_ge(sem("half_squared"), u + 1)
                nc.gpsimd.tensor_scalar(tables_out[:, u % 4, 0, :], half, -2.0, 1.0, ALU.mult, ALU.add).then_inc(sem("table_cos_ready"), 1)

            for s in range(4):
                n = [0, 2, 3, 5][s]
                c0 = CTX if s == 3 else 0
                sums(f"ffn{s}", c0)
                centre(f"ffn{s}", c0)
                gains(n, f"ffn{s}", CTX if n >= 3 else 0)
                if s == 0:
                    even()
                if s == 2:
                    odd()


def _tiles(w):
    k, n = w.shape
    return w.reshape(k // P, P, n // P, P).transpose(2, 1, 0, 3)


def _rows(w):
    k, n = w.shape
    return w.reshape(k // P, P, n).transpose(1, 0, 2)


def _cols(v):
    v = v.reshape(v.shape[:-1] + (v.shape[-1] // P, P))
    return np.moveaxis(v, -1, 0)


def _feature_major(x):
    return x.T.reshape(-1, P, x.shape[0]).transpose(1, 0, 2)


def _layout(v):
    c = np.ascontiguousarray
    x, ctx = v["x"][0], v["ctx"][0]
    a = {}
    a["x"] = c(np.concatenate([_feature_major(ctx), _feature_major(x)], axis=2))
    a["cvec"] = c(np.broadcast_to(np.stack([v["c_ctx"], v["c"][0]]), (P, 2, D)))
    a["ada"] = c(np.stack([w.T.reshape(MODG, 4, P, D).transpose(0, 2, 1, 3) for w in v["ada_w"]]).reshape(LAYERS * MODG, P, SLOT))
    a["modb"] = c(np.repeat(_cols(v["ada_b"])[..., None], 2, axis=-1))
    a["lng"] = c(_cols(v["ln_g"]).reshape(P, 6, KT))
    a["lnb"] = c(_cols(v["ln_b"]).reshape(P, 6, KT))
    gate, up, down = v["ffn_w_gate"], v["ffn_w_up"], v["ffn_w_down"]
    a["gateup"] = c(np.stack([
        np.stack([_tiles(gate[l, s]), _tiles(up[l, s])], axis=1).reshape(PAIRS, 4, P, KT * P).transpose(0, 2, 1, 3)
        for l in range(LAYERS) for s in range(2)]).reshape(4, PAIRS, P, SLOT))
    a["down"] = c(np.stack([_tiles(down[l, s]).reshape(KT, P, FT * P) for l in range(LAYERS) for s in range(2)]))
    w = v["ev_w_in"][0]
    naq, nak, nav, xm, mv, zo, zg = (w[:, a:b] for a, b in ((0, 512), (512, 1024), (1024, 1536), (1536, 2048), (2048, 2560),
                                                           (2560, 3072), (3072, 3088)))
    slot = lambda t: t.transpose(1, 0, 2, 3).reshape(P, SLOT)
    a["ev_in"] = c(np.stack([slot(_tiles(u)) for u in (xm, zo, naq, nak)]))
    a["ev_v"] = c(np.stack([_rows(u).reshape(P, SLOT) for u in (nav, mv)]))
    a["ev_gates"] = c(_rows(zg).reshape(P, KT * 16))
    a["ev_out"] = c(np.stack([slot(u) for u in _tiles(v["ev_w_out"][0]).reshape(2, 4, P, KT, P)]))
    a["ml_qk"] = c(np.concatenate([v["ml_wq"][0], v["ml_wk"][0]]).transpose(1, 0, 2).reshape(P, 2 * WIDTH))
    a["rpb"] = c(v["na_rpb"][0].reshape(-1))
    a["conv_w"] = c(np.moveaxis(_cols(v["ml_conv_w"][0]), 1, 2))
    a["conv_b"] = c(_cols(v["ml_conv_b"][0]))
    a["gate_b"] = c(np.concatenate([v["ml_i_bias"][0], v["ml_f_bias"][0]]).T)
    a["ml_gn"] = c(_cols(v["ml_gn_w"][0]))
    a["ident"] = np.eye(P, dtype=np.float32)
    a["flip"] = np.ascontiguousarray(a["ident"][::-1])
    a["head_sel"] = np.repeat(np.eye(HEADS, dtype=np.float32)[:, :, None], P, axis=2)
    q, k = np.arange(GRID_W)[:, None], np.arange(GRID_W)[None, :]
    first = np.clip(q - WIN_W // 2, 0, GRID_W - WIN_W)
    a["na_mask"] = np.tile(np.where((k >= first) & (k < first + WIN_W), 0.0, -1e30).astype(np.float32), (2, 1))
    w = v["od_w_in"][0]
    su, rq, rk, rv, rg = (w[:, n * 512:(n + 1) * 512] for n in range(5))
    a["od_in"] = c(np.stack([slot(_tiles(u)) for u in (su, rk, rq, rg)]))
    a["od_v"] = c(_rows(rv).reshape(P, SLOT))
    a["od_out"] = c(np.stack([slot(u) for u in _tiles(v["od_w_out"][0]).reshape(2, 4, P, KT, P)]))
    a["glu"] = c(_rows(v["s5_glu_w"][0]).reshape(P, HEADS * WIDTH))
    a["glu_b"] = c(_cols(v["s5_glu_b"][0]))
    a["s5_d"] = c(_cols(v["s5_d"][0].reshape(-1)))
    a["ret_gn"] = c(_cols(v["ret_gn_w"][0]))
    a["decay_logit"] = c(np.broadcast_to(v["ret_decay_logit"][0], (P, 2, HEADS)))
    states = lambda t: t.reshape(2 * S5_TILES, P).T
    log_dt = np.repeat(v["s5_log_dt"][0], S5_STATE, axis=1)
    a["s5_par"] = c(np.stack([states(v["s5_lam_re"][0]), states(v["s5_lam_im"][0]), states(log_dt)], axis=1))
    b_ = np.stack([v["s5_b_re"][0], v["s5_b_im"][0]]).reshape(2, 2, 4, 4, 2, S5_STATE, S5_GROUP)
    blocks = np.zeros((4, 2, S5_GROUP, 2, 2, 4, 2, S5_STATE), np.float32)
    c_ = np.stack([v["s5_c_re"][0], v["s5_c_im"][0]]).reshape(2, 2, S5_TILES, 2, S5_GROUP, S5_STATE)
    cblocks = np.zeros((2, S5_STATE, 2, 2, S5_TILES, 2, S5_GROUP), np.float32)
    for n in range(2):
        blocks[:, n, :, :, :, :, n, :] = b_[:, :, :, :, n].transpose(3, 5, 0, 1, 2, 4)
        cblocks[n, :, :, :, :, n, :] = c_[:, :, :, n].transpose(4, 0, 1, 2, 3)
    a["s5_b"] = c(blocks.reshape(P, 2, 8, P))
    a["s5_c"] = c(cblocks.reshape(P, 2, 2 * S5_TILES, PAIR))
    n = np.arange(1, CTX + 1, dtype=np.float32)
    a["steps"] = c(np.broadcast_to(np.stack([n, n[::-1]]), (P, 2, CTX)))
    f = np.arange(P)
    t = np.arange(LAT)
    pos = np.where(f[:, None] < P // 2, (t // GRID_W)[None, :], (t % GRID_W)[None, :]).astype(np.float32)
    freq = (np.float32(10000.0) ** (-(np.arange(P // 4, dtype=np.float32)) / np.float32(P // 4)))[f % (P // 4)]
    ang = (pos * freq[:, None]).astype(np.float64)
    sign = np.where(f % (P // 2) < P // 4, -1.0, 1.0)[:, None]
    a["rope"] = c(np.stack([np.cos(ang), np.sin(ang) * sign], axis=1).astype(np.float32))
    swap = np.zeros((P, P), np.float32)
    swap[f ^ (P // 4), f] = 1.0
    a["rope_swap"] = swap
    return a


def kernel(**inputs):
    import concourse.bacc as bacc
    from concourse.bass_utils import run_bass_kernel_spmd

    v = {name: np.asarray(a) for name, a in inputs.items()}
    nc = bacc.Bacc("TRN2", target_bir_lowering=False, num_devices=1)
    arrays, args = {}, {}
    for name, a in _layout(v).items():
        arrays[f"in_{name}_dram"] = a
        args[name] = nc.dram_tensor(f"in_{name}_dram", a.shape, mybir.dt.from_np(a.dtype), kind="ExternalInput").ap()
    out = nc.dram_tensor("out_dram", (P, KT, LAT), F32, kind="ExternalOutput").ap()
    build(nc, args, out)
    r = run_bass_kernel_spmd(nc, [arrays], core_ids=[0]).results[0]["out_dram"]
    return np.ascontiguousarray(r.transpose(2, 1, 0).reshape(1, LAT, D))
```
